# Optimizing a Trainium2 kernel written in Bass

```python
import math
import jax, jax.numpy as jnp
from jax import lax
import numpy as np

D_MODEL = 1024
BATCH = 1
SEQ = 1024
DEPTH = 1

N_META = 16
H_A = 8
DH_A = 64
W_A = H_A * DH_A
H_IDX = 8
D_IDX = 64
TOPK_MAX = 256
Q_BLOCK = 64
N_BUCKETS = 32
MAX_DISTANCE = 128
H_B = 8
DK_B = 128
DV_B = 128
W_B = H_B * DV_B
CONV_K = 4
CHUNK = 64
EPS = 1e-6

COLUMN_SIZES = (W_A, W_A, W_A, W_A, H_IDX * D_IDX, D_IDX, H_IDX,
                H_B * DK_B, H_B * DK_B, W_B, W_B, H_B, H_B, D_MODEL, D_MODEL)
N_IN = 4 * W_A + H_IDX * D_IDX + D_IDX + H_IDX + 2 * H_B * DK_B + 2 * W_B + 2 * H_B + 2 * D_MODEL

kernel_name = 'hybrid_dsa_gdn_gated_merge'

def rms_norm(x, w):
    xf = x.astype(jnp.float32)
    y = xf * lax.rsqrt(jnp.mean(xf * xf, axis=-1, keepdims=True) + EPS)
    return (y * w.astype(jnp.float32)).astype(x.dtype)

def l2_norm(x):
    xf = x.astype(jnp.float32)
    return xf * lax.rsqrt(jnp.sum(xf * xf, axis=-1, keepdims=True) + EPS)

def split_columns(p):
    offsets = []
    acc = 0
    for s in COLUMN_SIZES[:-1]:
        acc += s
        offsets.append(acc)
    return jnp.split(p, offsets, axis=-1)

def t5_bucket(dist):
    max_exact = N_BUCKETS // 2
    d = jnp.maximum(dist, 0)
    ratio = jnp.maximum(d, max_exact).astype(jnp.float32) / max_exact
    large = max_exact + (jnp.log(ratio) / math.log(MAX_DISTANCE / max_exact)
                         * (N_BUCKETS - max_exact)).astype(jnp.int32)
    large = jnp.minimum(large, N_BUCKETS - 1)
    return jnp.where(d < max_exact, d, large)

def sparse_attention(q, k, v, q_idx, k_idx, w_idx, rel_bias, q_norm_w, k_norm_w):
    B, T = q.shape[0], q.shape[1]
    topk = min(TOPK_MAX, SEQ // 4)
    q = rms_norm(q, q_norm_w)
    k = rms_norm(k, k_norm_w)
    n_blk = -(-T // Q_BLOCK)
    pad = n_blk * Q_BLOCK - T

    def to_blocks(a):
        a = jnp.pad(a, [(0, 0), (0, pad)] + [(0, 0)] * (a.ndim - 2))
        return a.reshape((B, n_blk, Q_BLOCK) + a.shape[2:]).swapaxes(0, 1)

    key_pos = jnp.arange(T, dtype=jnp.int32)
    idx_scale = (H_IDX ** -0.5) * (D_IDX ** -0.5)
    attn_scale = DH_A ** -0.5

    def block(args):
        blk, q_b, qi_b, wi_b = args
        q_pos = blk * Q_BLOCK + jnp.arange(Q_BLOCK, dtype=jnp.int32)
        causal = key_pos[None, :] <= q_pos[:, None]
        rel = jax.nn.relu(jnp.einsum('bqhd,bsd->bqhs', qi_b, k_idx).astype(jnp.float32))
        score = jnp.einsum('bqhs,bqh->bqs', rel, wi_b.astype(jnp.float32)) * idx_scale
        score = jnp.where(causal[None], score, -jnp.inf)
        _, sel = lax.top_k(score, topk)
        valid = sel <= q_pos[None, :, None]
        k_sel = jax.vmap(lambda kb, ib: kb[ib])(k, sel)
        v_sel = jax.vmap(lambda vb, ib: vb[ib])(v, sel)
        logits = jnp.einsum('bqhd,bqkhd->bhqk', q_b, k_sel).astype(jnp.float32) * attn_scale
        bias = rel_bias[t5_bucket(q_pos[None, :, None] - sel)]
        logits = logits + jnp.transpose(bias, (0, 3, 1, 2)).astype(jnp.float32)
        logits = jnp.where(valid[:, None], logits, -jnp.inf)
        p = jax.nn.softmax(logits, axis=-1)
        return jnp.einsum('bhqk,bqkhd->bqhd', p.astype(v.dtype), v_sel)

    out = lax.map(block, (jnp.arange(n_blk, dtype=jnp.int32), to_blocks(q), to_blocks(q_idx), to_blocks(w_idx)))
    out = jnp.transpose(out, (1, 0, 2, 3, 4)).reshape(B, n_blk * Q_BLOCK, H_A, DH_A)
    return out[:, :T]

def causal_depthwise_conv_silu(x, w):
    y = lax.conv_general_dilated(x, w[:, None, :].astype(x.dtype), window_strides=(1,),
                                 padding=[(CONV_K - 1, 0)],
                                 dimension_numbers=('NWC', 'WIO', 'NWC'),
                                 feature_group_count=x.shape[-1])
    return jax.nn.silu(y)

def gated_delta_rule(q, k, v, g, beta):
    B, T, H, dk = k.shape
    dv = v.shape[-1]
    pad = (-T) % CHUNK

    def lpad(a):
        return jnp.pad(a, [(0, 0), (pad, 0)] + [(0, 0)] * (a.ndim - 2))

    N = (T + pad) // CHUNK

    def chunkify(a):
        return lpad(a).reshape(B, N, CHUNK, H, -1).transpose(0, 3, 1, 2, 4)

    def chunkify_s(a):
        return lpad(a).reshape(B, N, CHUNK, H).transpose(0, 3, 1, 2)

    q = chunkify(q) * (dk ** -0.5)
    k = chunkify(k)
    v = chunkify(v)
    g = chunkify_s(g)
    beta = chunkify_s(beta)
    gc = jnp.cumsum(g, axis=-1)
    incl = jnp.tril(jnp.ones((CHUNK, CHUNK), dtype=bool))
    strict = jnp.tril(jnp.ones((CHUNK, CHUNK), dtype=bool), -1)
    L = jnp.exp(jnp.where(incl, gc[..., :, None] - gc[..., None, :], -jnp.inf))
    kb = k * beta[..., None]
    A = jnp.where(strict, jnp.einsum('bhnid,bhnjd->bhnij', kb, k) * L, 0.0)
    eye = jnp.eye(CHUNK, dtype=A.dtype)
    Tm = lax.linalg.triangular_solve(eye + A, jnp.broadcast_to(eye, A.shape),
                                     left_side=True, lower=True, unit_diagonal=True)
    u = jnp.einsum('bhnij,bhnje->bhnie', Tm, v * beta[..., None])
    w = jnp.einsum('bhnij,bhnjd->bhnid', Tm, kb * jnp.exp(gc)[..., None])
    att = jnp.einsum('bhnid,bhnjd->bhnij', q, k) * L
    q_dec = q * jnp.exp(gc)[..., None]
    k_dec = k * jnp.exp(gc[..., -1:] - gc)[..., None]
    g_last = jnp.exp(gc[..., -1])

    def step(S, xs):
        u_n, w_n, qd_n, kd_n, att_n, gl_n = xs
        v_new = u_n - jnp.einsum('bhcd,bhde->bhce', w_n, S)
        o = jnp.einsum('bhcd,bhde->bhce', qd_n, S) + jnp.einsum('bhij,bhje->bhie', att_n, v_new)
        S = S * gl_n[..., None, None] + jnp.einsum('bhcd,bhce->bhde', kd_n, v_new)
        return S, o

    def n_first(a):
        return jnp.moveaxis(a, 2, 0)

    S0 = jnp.zeros((B, H, dk, dv), dtype=jnp.float32)
    _, o = lax.scan(step, S0, (n_first(u), n_first(w), n_first(q_dec), n_first(k_dec),
                               n_first(att), n_first(g_last)))
    o = jnp.transpose(o, (1, 0, 3, 2, 4)).reshape(B, N * CHUNK, H, dv)
    return o[:, pad:]

def hybrid_layer(x, rel_bias, norm_w, w_in, q_norm_w, k_norm_w, conv_w, a_log, dt_bias,
                 gdn_norm_w, w_proj_a, w_proj_b, w_out):
    B, T, _ = x.shape
    h = rms_norm(x, norm_w)
    p = h @ w_in.astype(x.dtype)
    (qa, ka, va, za, qi, ki, wi, qb, kb, vb, zb, bb, ab, ga, gb) = split_columns(p)

    ya = sparse_attention(qa.reshape(B, T, H_A, DH_A), ka.reshape(B, T, H_A, DH_A),
                          va.reshape(B, T, H_A, DH_A), qi.reshape(B, T, H_IDX, D_IDX), ki, wi,
                          rel_bias, q_norm_w, k_norm_w)
    ya = (ya.reshape(B, T, W_A) * jax.nn.silu(za)) @ w_proj_a.astype(x.dtype)

    qkv = causal_depthwise_conv_silu(jnp.concatenate([qb, kb, vb], axis=-1), conv_w)
    qg, kg, vg = jnp.split(qkv, [H_B * DK_B, 2 * H_B * DK_B], axis=-1)
    q_b = l2_norm(qg.reshape(B, T, H_B, DK_B))
    k_b = l2_norm(kg.reshape(B, T, H_B, DK_B))
    v_b = vg.reshape(B, T, H_B, DV_B).astype(jnp.float32)
    beta = jax.nn.sigmoid(bb.astype(jnp.float32))
    g = -jnp.exp(a_log.astype(jnp.float32)) * jax.nn.softplus(ab.astype(jnp.float32) + dt_bias.astype(jnp.float32))
    o_b = gated_delta_rule(q_b, k_b, v_b, g, beta)
    o_b = rms_norm(o_b, gdn_norm_w).reshape(B, T, W_B).astype(x.dtype)
    yb = (o_b * jax.nn.silu(zb)) @ w_proj_b.astype(x.dtype)

    m = jax.nn.sigmoid(ga) * ya + jax.nn.sigmoid(gb) * yb
    return x + m @ w_out.astype(x.dtype)

def setup_inputs(seed: int = 0) -> dict:
    key = jax.random.key(seed)
    ks = jax.random.split(key, 16)
    f32 = jnp.float32
    x = jax.random.normal(ks[0], (BATCH, SEQ, D_MODEL), f32)
    meta_tokens = jax.random.normal(ks[1], (N_META, D_MODEL), f32)
    rel_bias = 0.5 * jax.random.normal(ks[2], (N_BUCKETS, H_A), f32)
    norm_w = 1.0 + 0.02 * jax.random.normal(ks[3], (DEPTH, D_MODEL), f32)
    w_in = jax.random.normal(ks[4], (DEPTH, D_MODEL, N_IN), f32) * (D_MODEL ** -0.5)
    q_norm_w = 1.0 + 0.02 * jax.random.normal(ks[5], (DEPTH, DH_A), f32)
    k_norm_w = 1.0 + 0.02 * jax.random.normal(ks[6], (DEPTH, DH_A), f32)
    conv_w = jax.random.normal(ks[7], (DEPTH, CONV_K, 2 * H_B * DK_B + W_B), f32) * (CONV_K ** -0.5)
    a_log = jnp.log(jax.random.uniform(ks[8], (DEPTH, H_B), f32, 1.0, 16.0))
    dt = jnp.exp(jax.random.uniform(ks[9], (DEPTH, H_B), f32, math.log(1e-3), math.log(1e-1)))
    dt_bias = dt + jnp.log(-jnp.expm1(-dt))
    gdn_norm_w = 1.0 + 0.02 * jax.random.normal(ks[10], (DEPTH, DV_B), f32)
    w_proj_a = jax.random.normal(ks[11], (DEPTH, W_A, D_MODEL), f32) * (W_A ** -0.5)
    w_proj_b = jax.random.normal(ks[12], (DEPTH, W_B, D_MODEL), f32) * (W_B ** -0.5)
    w_out = jax.random.normal(ks[13], (DEPTH, D_MODEL, D_MODEL), f32) * (D_MODEL ** -0.5)
    return {'x': x, 'meta_tokens': meta_tokens, 'rel_bias': rel_bias, 'norm_w': norm_w,
            'w_in': w_in, 'q_norm_w': q_norm_w, 'k_norm_w': k_norm_w, 'conv_w': conv_w,
            'a_log': a_log, 'dt_bias': dt_bias, 'gdn_norm_w': gdn_norm_w,
            'w_proj_a': w_proj_a, 'w_proj_b': w_proj_b, 'w_out': w_out}

def reference(x, meta_tokens, rel_bias, norm_w, w_in, q_norm_w, k_norm_w, conv_w, a_log, dt_bias,
              gdn_norm_w, w_proj_a, w_proj_b, w_out):
    B = x.shape[0]
    meta = jnp.broadcast_to(meta_tokens[None].astype(x.dtype), (B, N_META, D_MODEL))
    hs = jnp.concatenate([meta, x], axis=1)
    for l in range(DEPTH):
        hs = hybrid_layer(hs, rel_bias, norm_w[l], w_in[l], q_norm_w[l], k_norm_w[l], conv_w[l],
                          a_log[l], dt_bias[l], gdn_norm_w[l], w_proj_a[l], w_proj_b[l], w_out[l])
    return hs[:, N_META:]


_drawn_inputs = setup_inputs


def setup_inputs(seed=0):
    import zlib

    import numpy as np

    out = dict(_drawn_inputs(seed))
    spreads = {}
    factors = {'rel_bias': 4.007, 'norm_w': 5.243, 'q_norm_w': 8.0, 'k_norm_w': 8.0, 'gdn_norm_w': 24.159}
    for name, (base, spread) in spreads.items():
        noise = np.random.default_rng([zlib.crc32(name.encode()), seed]).standard_normal(out[name].shape)
        drawn = base * np.exp(spread * noise) if base else spread * noise
        out[name] = __import__('jax').numpy.asarray(drawn.astype(out[name].dtype))
    for name, factor in factors.items():
        out[name] = (out[name] * factor).astype(out[name].dtype)
    return out
```

```python
import math
from contextlib import ExitStack

import concourse.bass as bass
from concourse import mybir

P = 128
D = 1024
SEQ = 1024
META = 16
T = META + SEQ
PAD = P - META
TP = PAD + T
KD = D // P
NQT = SEQ // P
NT = TP // P
H = 8
DH = 64
WA = H * DH
DK = 128
CHUNK = 64
TOPK = 256
EPS = 1e-6

OFF_QA, OFF_KA, OFF_VA, OFF_ZA = 0, WA, 2 * WA, 3 * WA
OFF_QI = 4 * WA
OFF_KI = OFF_QI + WA
OFF_WI = OFF_KI + DH
OFF_QB = OFF_WI + H
OFF_KB = OFF_QB + D
OFF_VB = OFF_KB + D
OFF_ZB = OFF_VB + D
OFF_BB = OFF_ZB + D
OFF_GA = OFF_BB + 2 * H
OFF_GB = OFF_GA + D
NSM = 3 * H

PICKED = -3.4028234663852886e38
AFTER = -3.0e38
HIDDEN = -1.0e30

ALU = mybir.AluOpType
ACT = mybir.ActivationFunctionType
AX = mybir.AxisListType
F32 = mybir.dt.float32


def keys_of(t):
    return META + P * (t + 1)


def make_constants(nc, ident, ones):
    with nc.semaphore("ident_zero") as ident_zero, nc.Block() as block:
        @block.gpsimd
        def _(pool):
            nc.gpsimd.memset(ones[:], 1.0)
            nc.gpsimd.memset(ident[:], 0.0).then_inc(ident_zero, 1)
            pool.wait_ge(ident_zero, 1)
            nc.gpsimd.affine_select(out=ident[:], in_=ident[:], compare_op=ALU.not_equal, fill=1.0,
                                    base=0, pattern=[[-1, P]], channel_multiplier=1)


def normed_tokens(nc, x, meta_tokens, norm_w, hT, ident):
    x_v = x.rearrange("b (t p) d -> (b t) p d", p=P)
    with ExitStack() as ctx:
        xt = ctx.enter_context(nc.sbuf_tensor("xt", [P, 2, D], F32))
        xn = ctx.enter_context(nc.sbuf_tensor("xn", [P, 2, D], F32))
        junk = ctx.enter_context(nc.sbuf_tensor("junk", [P, D], F32))
        nwT = ctx.enter_context(nc.sbuf_tensor("nwT", [P, KD], F32))
        ssq = ctx.enter_context(nc.sbuf_tensor("ssq", [P, NT], F32))
        mean = ctx.enter_context(nc.sbuf_tensor("mean", [P, NT], F32))
        root = ctx.enter_context(nc.sbuf_tensor("root", [P, NT], F32))
        rstd = ctx.enter_context(nc.sbuf_tensor("rstd", [P, NT], F32))
        tr = [ctx.enter_context(nc.psum_tensor(f"tr{i}", [P, 4, P], F32)) for i in range(4)]
        sem = lambda n: ctx.enter_context(nc.semaphore(n))
        x_loaded = [sem("x_loaded0"), sem("x_loaded1")]
        nw_loaded, squared, mean_ready, root_ready, rstd_ready = (
            sem(n) for n in ("nw_loaded", "squared", "mean_ready", "root_ready", "rstd_ready"))
        scaled, turned, stored, hpad = (sem(n) for n in ("scaled", "turned", "stored", "hpad"))
        block = ctx.enter_context(nc.Block())

        def rows(t):
            return META if t == 0 else P

        @block.sync
        def _(sp):
            with nc.allow_non_contiguous_dma(reason="norm_w by partition"):
                sp.dma_start(nwT[:], norm_w.rearrange("l (k p) -> p (l k)", p=P)).then_inc(nw_loaded, 16)
            for t in range(NT):
                if t >= 2:
                    sp.wait_ge(scaled, t - 1)
                src = meta_tokens if t == 0 else x_v[t - 1]
                sp.dma_start(xt[:rows(t), t % 2], src).then_inc(x_loaded[t % 2], 16)
            sp.wait_ge(nw_loaded, 16)

        @block.gpsimd
        def _(pool):
            nc.gpsimd.memset(hT[:, :, 0:PAD], 0.0).then_inc(hpad, 1)

        @block.scalar
        def _(act):
            for t in range(NT):
                n = rows(t)
                act.wait_ge(x_loaded[t % 2], 16 * (t // 2 + 1))
                if t:
                    act.wait_ge(squared, t)
                nc.scalar.activation(junk[:n], xt[:n, t % 2], ACT.Square,
                                     accum_out=ssq[:n, t:t + 1]).then_inc(squared, 1)
                act.wait_ge(mean_ready, t + 1)
                nc.scalar.activation(root[:n, t:t + 1], mean[:n, t:t + 1], ACT.Sqrt).then_inc(root_ready, 1)

        @block.vector
        def _(dve):
            dve.wait_ge(nw_loaded, 16)
            for t in range(NT + 1):
                if t < NT:
                    n = rows(t)
                    dve.wait_ge(squared, t + 1)
                    nc.vector.tensor_scalar(mean[:n, t:t + 1], ssq[:n, t:t + 1], 1.0 / D, EPS,
                                            ALU.mult, ALU.add).then_inc(mean_ready, 1)
                    dve.wait_ge(root_ready, t + 1)
                    nc.vector.reciprocal(rstd[:n, t:t + 1], root[:n, t:t + 1]).then_inc(rstd_ready, 1)
                    dve.wait_ge(rstd_ready, t + 1)
                    if t >= 2:
                        dve.wait_ge(turned, 2 * (t - 1))
                    nc.vector.tensor_scalar(xn[:n, t % 2], xt[:n, t % 2], rstd[:n, t:t + 1], None,
                                            ALU.mult).then_inc(scaled, 1)
                if t >= 1:
                    n, c = rows(t - 1), (PAD if t == 1 else P * (t - 1))
                    for g in range(2):
                        dve.wait_ge(turned, 2 * (t - 1) + g + 1)
                        nc.vector.tensor_tensor(
                            hT[:, 4 * g:4 * g + 4, c:c + n], tr[(2 * (t - 1) + g) % 4][:, :, 0:n],
                            nwT[:, 4 * g:4 * g + 4].unsqueeze(2).to_broadcast([P, 4, n]),
                            ALU.mult).then_inc(stored, 1)

        @block.tensor
        def _(pe):
            for t in range(NT):
                n = rows(t)
                pe.wait_ge(scaled, t + 1)
                for g in range(2):
                    if 2 * t + g >= 4:
                        pe.wait_ge(stored, 2 * t + g - 3)
                    for k in range(4):
                        f = (4 * g + k) * P
                        last = nc.tensor.transpose(tr[(2 * t + g) % 4][:, k, 0:n], xn[:n, t % 2, f:f + P],
                                                   ident[:n, :n])
                    last.then_inc(turned, 1)


def spans(w):
    step = -(-w // (16 * -(-w // 512))) * 16
    return [(a, min(w, a + step)) for a in range(0, w, step)]


def projections(nc, w_in, hT, small, score, qa, ka, va, qiT, kiT, rel, za_dram, zb_dram, gates_dram):
    w_v = w_in.rearrange("l (k p) n -> p (l k) n", p=P)
    BANKS, STAGES = 7, 3

    loads = [[(OFF_QI, 512, 0)],
             [(OFF_KI, DH, 0), (OFF_KI, DH, DH), (OFF_WI, H, P), (OFF_BB, 2 * H, P + H)],
             [(OFF_QA, 512, 0)], [(OFF_KA, 512, 0)], [(OFF_VA, 512, 0)], [(OFF_ZA, 512, 0)],
             [(OFF_ZB, 512, 0)], [(OFF_ZB + 512, 512, 0)],
             [(OFF_GA, 512, 0)], [(OFF_GA + 512, 512, 0)], [(OFF_GB, 512, 0)], [(OFF_GB + 512, 512, 0)]]

    fills = [("qi", f, 512 * c, 512 * c + 512, 0) for f in range(4) for c in range(2)]
    fills += [("ki", 0, a, b, 1) for a, b in spans(T)]
    fills += [("small", 0, 0, NT * NSM, 1)]
    fills += [("rel", (t, h), a, b, None) for t in range(1, NQT) for h in range(H) for a, b in spans(keys_of(t))]
    for load, what in ((2, "qa"), (3, "ka"), (4, "va"), (5, "za"), (6, "zb0"), (7, "zb1")):
        fills += [(what, t, 0, 512, load) for t in range(0 if what in ("ka", "va") else 1, NT)]
    fills += [("gate", f, 512 * c, 512 * c + 512, 8 + f // 4) for f in range(2 * KD) for c in range(2)]
    last_fill = [max(n for n, f in enumerate(fills) if f[4] == load) + 1 for load in range(len(loads))]
    first_rel = min(n for n, f in enumerate(fills) if f[0] == "rel")
    to_dram = ("za", "zb0", "zb1", "gate")

    with ExitStack() as ctx:
        ring = ctx.enter_context(nc.sbuf_tensor("ring", [P, 2, KD, 512], F32))
        stage = ctx.enter_context(nc.sbuf_tensor("stage", [P, STAGES, 512], F32))
        top8 = ctx.enter_context(nc.sbuf_tensor("top8", [P, 8], F32))
        pj = [ctx.enter_context(nc.psum_tensor(f"pj{i}", [P, 512], F32)) for i in range(BANKS)]
        sem = lambda n: ctx.enter_context(nc.semaphore(n))
        w_loaded = [sem("w_loaded0"), sem("w_loaded1")]
        filled, emptied = sem("filled"), sem("emptied")
        rel_used, summed, fenced, step, picked, masked = (
            sem(n) for n in ("rel_used", "summed", "fenced", "step", "picked", "masked"))
        saved = [sem(f"saved{i}") for i in range(STAGES)]
        block = ctx.enter_context(nc.Block())

        @block.sync
        def _(sp):
            for n, parts in enumerate(loads):
                if n >= 2:
                    sp.wait_ge(filled, last_fill[n - 2])
                for col, w, at in parts:
                    sp.dma_start(ring[:, n % 2, :, at:at + w],
                                 w_v[:, :, col:col + w]).then_inc(w_loaded[n % 2], 16)

        @block.tensor
        def _(pe):
            loaded = -1
            for n, (what, i, a, b, load) in enumerate(fills):
                bank = pj[n % BANKS]
                if n >= BANKS:
                    pe.wait_ge(emptied, n - BANKS + 1)
                if load is not None and load > loaded:
                    loaded = load
                    pe.wait_ge(w_loaded[load % 2], 16 * sum(len(x) for x in loads[load % 2:load + 1:2]))
                if what == "rel":
                    t, h = i
                    if n == first_rel:
                        pe.wait_ge(emptied, n)
                    r = slice(DH * (h % 2), DH * (h % 2) + DH)
                    last = nc.tensor.matmul(bank[:, 0:b - a], qiT[r, h // 2, P * t:P * t + P], kiT[r, a:b],
                                            start=True, stop=True)
                elif what == "small":
                    for t in range(NT):
                        for k in range(KD):
                            last = nc.tensor.matmul(bank[:, NSM * t:NSM * t + NSM], hT[:, k, P * t:P * t + P],
                                                    ring[:, load % 2, k, P:P + NSM],
                                                    start=(k == 0), stop=(k == KD - 1))
                elif what in ("qi", "ki", "gate"):
                    f = i % 4 * P
                    c = PAD if what == "ki" else P
                    for k in range(KD):
                        last = nc.tensor.matmul(bank[:, 0:b - a], ring[:, load % 2, k, f:f + P],
                                                hT[:, k, c + a:c + b], start=(k == 0), stop=(k == KD - 1))
                else:
                    c, m = (PAD, META) if i == 0 else (P * i, P)
                    for k in range(KD):
                        last = nc.tensor.matmul(bank[0:m, :], hT[:, k, c:c + m], ring[:, load % 2, k, :],
                                                start=(k == 0), stop=(k == KD - 1))
                last.then_inc(filled, 1)

        @block.scalar
        def _(act):
            n_out = 0
            for n, (what, i, a, b, _) in enumerate(fills):
                bank = pj[n % BANKS]
                func = ACT.Copy
                m = P
                if what == "qi":
                    dst = qiT[:, i, a:b]
                elif what == "ki":
                    dst = kiT[:, a:b]
                elif what == "small":
                    dst = small[:].rearrange("p t c -> p (t c)")
                elif what == "rel":
                    t, h = i
                    unit = H * (t - 1) + h
                    func, dst = ACT.Relu, rel[:, unit % 2, a:b]
                    if a == 0 and unit >= 2:
                        act.wait_ge(rel_used, unit - 1)
                elif what in to_dram:
                    func, dst = (ACT.Sigmoid if what == "gate" else ACT.Silu), stage[:, n_out % STAGES]
                    if n_out >= STAGES:
                        act.wait_ge(saved[n_out % STAGES], 16 * (n_out // STAGES))
                else:
                    m = META if i == 0 else P
                    dst = {"qa": qa, "ka": ka, "va": va}[what][0:m, i]
                act.wait_ge(filled, n + 1)
                nc.scalar.activation(dst, bank[0:m, 0:b - a], func).then_inc(emptied, 1)
                if what in to_dram:
                    if what == "gate":
                        out = gates_dram[i, :, a:b]
                    elif what == "za":
                        out = za_dram[i - 1]
                    else:
                        out = zb_dram[i - 1, :, 512 * (what == "zb1"):512 * (what == "zb1") + 512]
                    act.wait_ge(emptied, n + 1)
                    act.dma_start(out, stage[:, n_out % STAGES]).then_inc(saved[n_out % STAGES], 16)
                    n_out += 1
            for s in range(STAGES):
                act.wait_ge(saved[s], 16 * len(range(s, n_out, STAGES)))

        @block.vector
        def _(dve):
            steps = 0
            rel_fills = {}
            for n, f in enumerate(fills):
                if f[0] == "rel":
                    rel_fills[f[1]] = n + 1
            for t in range(1, NQT):
                w = keys_of(t)
                for h in range(H):
                    unit = H * (t - 1) + h
                    weight = small[:, t + 1, h:h + 1]
                    dve.wait_ge(emptied, rel_fills[(t, h)])
                    if h == 0:
                        nc.vector.tensor_scalar(score[t][:], rel[:, unit % 2, 0:w], weight, None,
                                                ALU.mult).then_inc(rel_used, 1)
                    else:
                        dve.wait_ge(rel_used, unit)
                        nc.vector.scalar_tensor_tensor(score[t][:], rel[:, unit % 2, 0:w], weight, score[t][:],
                                                       ALU.mult, ALU.add).then_inc(rel_used, 1)
            for t in range(1, NQT):
                dve.wait_ge(fenced, t)
                for r in range(TOPK // 8):
                    if r:
                        dve.wait_ge(step, steps)
                    nc.vector.max(top8[:], score[t][:]).then_inc(step, 1)
                    steps += 1
                    dve.wait_ge(step, steps)
                    nc.vector.match_replace(score[t][:], top8[:], score[t][:], PICKED).then_inc(step, 1)
                    steps += 1
                dve.wait_ge(step, steps)
                nc.vector.tensor_scalar(score[t][:], score[t][:], PICKED, HIDDEN,
                                        ALU.is_gt, ALU.mult).then_inc(picked, 1)

        @block.gpsimd
        def _(pool):
            nc.gpsimd.memset(score[0][:], 0.0).then_inc(masked, 1)
            pool.wait_ge(masked, 1)
            for t in range(NQT):
                tail = score[t][:, keys_of(t) - P:keys_of(t)]
                if t:
                    pool.wait_ge(rel_used, H * t)
                    nc.gpsimd.affine_select(out=tail, in_=tail, compare_op=ALU.is_ge, fill=AFTER, base=0,
                                            pattern=[[-1, P]], channel_multiplier=1).then_inc(fenced, 1)
                    pool.wait_ge(picked, t)
                nc.gpsimd.affine_select(out=tail, in_=tail, compare_op=ALU.is_ge, fill=HIDDEN, base=0,
                                        pattern=[[-1, P]], channel_multiplier=1).then_inc(masked, 1)


def band_table():
    import math
    import numpy as np
    d = np.maximum(np.arange(2 * P - 1, -P, -1), 0)
    ratio = np.maximum(d, 16).astype(np.float32) / np.float32(16)
    large = 16 + (np.log(ratio) / np.float32(math.log(128 / 16)) * np.float32(16)).astype(np.int32)
    bucket = np.where(d < 16, d, np.minimum(large, 31))
    table = np.zeros((32, d.size), np.float32)
    table[bucket, np.arange(d.size)] += 1
    table[31] -= 1
    return table


def key_chunks(t):
    w = keys_of(t)
    near = max(0, w - 2 * P)
    return (spans(near) if near else []) + [(near, w)]


def attention_operands(nc, ident, qa, ka, qT, kT, band, rel_bias, table, band_dram, q_norm_w, k_norm_w):
    NB = table.shape[1]
    with ExitStack() as early:
        esb = lambda name, shape: early.enter_context(nc.sbuf_tensor(name, shape, F32))
        esem = lambda n: early.enter_context(nc.semaphore(n))
        square = esb("square", [P, 2, WA])
        total, logs, rstd = (esb(n, [P, 2 * NT - 1, H]) for n in ("qk_total", "qk_log", "qk_rstd"))
        normed = esb("normed", [P, 2, WA])
        nw, eps = esb("nw", [P, 2]), esb("eps", [P, 1])
        bias_sb, table_sb, row_sb = esb("bias_sb", [32, H]), esb("table_sb", [32, NB]), esb("row_sb", [H, NB])
        flip, band_rev = esb("flip", [P, P]), esb("band_rev", [P, H, 2 * P])
        tr = [early.enter_context(nc.psum_tensor(f"tn{i}", [P, 4, P], F32)) for i in range(2)]
        bp = [early.enter_context(nc.psum_tensor(f"bp{i}", [P, 512], F32)) for i in range(2)]
        loaded, nw_ready, row_ready, row_saved, rev_loaded, row_made, made = (
            esem(n) for n in ("loaded", "nw_ready", "row_ready", "row_saved", "rev_loaded", "row_made", "made"))
        squared, added, logged, rooted, scaled, turned, kept, band_filled, band_kept = (
            esem(n) for n in ("a_squared", "a_added", "a_logged", "a_rooted", "a_scaled", "a_turned", "a_kept",
                              "band_filled", "band_kept"))
        units = [(ka, kT, i, 1) for i in range(NT)] + [(qa, qT, i, 0) for i in range(1, NT)]
        rows = lambda i: META if i == 0 else P
        block = early.enter_context(nc.Block())

        @block.sync
        def _(sp):
            sp.dma_start(bias_sb[:], rel_bias).then_inc(loaded, 16)
            sp.dma_start(table_sb[:], table).then_inc(loaded, 16)
            with nc.allow_non_contiguous_dma(reason="one weight per partition"):
                for j, w in enumerate((q_norm_w, k_norm_w)):
                    for half in range(2):
                        sp.dma_start(nw[DH * half:DH * half + DH, j:j + 1],
                                     w.rearrange("l d -> d l")).then_inc(loaded, 16)
            sp.wait_ge(row_ready, 1)
            sp.dma_start(band_dram, row_sb[:]).then_inc(row_saved, 16)
            sp.wait_ge(row_saved, 16)
            for h in range(H):
                src = bass.AP(band_dram.tensor, h * NB, [[1, P], [1, 2 * P]])
                sp.dma_start(band_rev[:, h], src).then_inc(rev_loaded, 16)

        @block.gpsimd
        def _(pool):
            nc.gpsimd.memset(total[:, 0], 1.0).then_inc(made, 1)
            nc.gpsimd.memset(eps[:], EPS).then_inc(made, 1)
            nc.gpsimd.memset(flip[:], 0.0).then_inc(made, 1)
            pool.wait_ge(made, 3)
            nc.gpsimd.affine_select(out=flip[:], in_=flip[:], compare_op=ALU.not_equal, fill=1.0,
                                    base=1 - P, pattern=[[1, P]], channel_multiplier=1).then_inc(made, 1)

        @block.scalar
        def _(act):
            for n, (raw, _, i, _) in enumerate(units):
                m = rows(i)
                if n >= 2:
                    act.wait_ge(added, n - 1)
                nc.scalar.activation(square[:m, n % 2], raw[:m, i], ACT.Square).then_inc(squared, 1)
            act.wait_ge(made, 4)
            act.wait_ge(added, len(units))
            nc.scalar.activation(logs[:], total[:, 0:len(units)], ACT.Ln, scale=1.0 / DH,
                                 bias=eps[:, 0:1]).then_inc(logged, 1)
            act.wait_ge(logged, 1)
            nc.scalar.activation(rstd[:], logs[:], ACT.Exp, scale=-0.5).then_inc(rooted, 1)

        @block.vector
        def _(dve):
            dve.wait_ge(loaded, 96)
            nc.vector.tensor_scalar(nw[:, 0:1], nw[:, 0:1], DH ** -0.5, None, ALU.mult).then_inc(nw_ready, 1)
            dve.wait_ge(row_made, 1)
            nc.vector.tensor_copy(row_sb[:], bp[0][0:H, 0:NB]).then_inc(row_ready, 1)
            dve.wait_ge(made, 1)
            for n, (raw, _, i, _) in enumerate(units):
                m = rows(i)
                dve.wait_ge(squared, n + 1)
                nc.vector.tensor_reduce(total[:m, n], square[:m, n % 2].rearrange("p (h d) -> p h d", d=DH),
                                        AX.X, ALU.add).then_inc(added, 1)
            dve.wait_ge(rooted, 1)
            for n in range(len(units) + 1):
                if n < len(units):
                    raw, _, i, _ = units[n]
                    m = rows(i)
                    if n >= 2:
                        dve.wait_ge(turned, n - 1)
                    nc.vector.tensor_tensor(normed[:m, n % 2].rearrange("p (h d) -> p h d", d=DH),
                                            raw[:m, i].rearrange("p (h d) -> p h d", d=DH),
                                            rstd[:m, n].unsqueeze(2).to_broadcast([m, H, DH]),
                                            ALU.mult).then_inc(scaled, 1)
                if n >= 1:
                    _, dst, i, j = units[n - 1]
                    m = rows(i)
                    c = 0 if i == 0 else P * (i - 1) + (META if j == 1 else 0)
                    dve.wait_ge(turned, n)
                    if n == 1:
                        dve.wait_ge(nw_ready, 1)
                    nc.vector.tensor_scalar(dst[:, :, c:c + m], tr[(n - 1) % 2][:, :, 0:m], nw[:, j:j + 1], None,
                                            ALU.mult).then_inc(kept, 1)
            for c in range(4):
                dve.wait_ge(band_filled, c + 1)
                nc.vector.tensor_copy(band[:, 2 * c:2 * c + 2].rearrange("p h j -> p (h j)"),
                                      bp[c % 2][:, :]).then_inc(band_kept, 1)

        @block.tensor
        def _(pe):
            pe.wait_ge(loaded, 96)
            nc.tensor.matmul(bp[0][0:H, 0:NB], bias_sb[:], table_sb[:], start=True, stop=True).then_inc(row_made, 1)
            for n, (_, _, i, _) in enumerate(units):
                m = rows(i)
                pe.wait_ge(scaled, n + 1)
                if n >= 2:
                    pe.wait_ge(kept, n - 1)
                for f in range(4):
                    last = nc.tensor.transpose(tr[n % 2][:, f, 0:m], normed[:m, n % 2, P * f:P * f + P],
                                               ident[:m, :m])
                last.then_inc(turned, 1)
            pe.wait_ge(rev_loaded, 16 * H)
            pe.wait_ge(made, 4)
            pe.wait_ge(row_ready, 1)
            for c in range(4):
                if c >= 2:
                    pe.wait_ge(band_kept, c - 1)
                nc.tensor.matmul(bp[c % 2][:, :], flip[:], band_rev[:, 2 * c:2 * c + 2].rearrange("p h j -> p (h j)"),
                                 start=True, stop=True).then_inc(band_filled, 1)


def attention(nc, ident, score, qT, kT, band, va, za_dram, g_dram):
    with ExitStack() as ctx:
        sb = lambda name, shape: ctx.enter_context(nc.sbuf_tensor(name, shape, F32))
        sem = lambda n: ctx.enter_context(nc.semaphore(n))
        hidden = sb("hidden", [P, 4, 2 * P])
        logit, prob, probT = sb("logit", [P, 2, T]), sb("prob", [P, 2, T]), sb("probT", [P, 2, NT, P])
        best, worst, mass, inv = sb("best", [P, 4 * H * NQT]), sb("worst", [P, H * NQT]), sb("mass", [P, H * NQT]), sb("inv", [P, H * NQT])
        gate, mixed, gated = sb("gate", [P, 2, WA]), sb("mixed", [P, 2, WA]), sb("gated", [P, 2, WA])
        LG, PT = 4, 2
        lg = [ctx.enter_context(nc.psum_tensor(f"lg{i}", [P, 512], F32)) for i in range(LG)]
        pt = [ctx.enter_context(nc.psum_tensor(f"pt{i}", [P, 4, P], F32)) for i in range(PT)]
        po = ctx.enter_context(nc.psum_tensor("po", [P, WA], F32))
        pg = ctx.enter_context(nc.psum_tensor("pg", [P, 4, P], F32))
        (near_ready, logit_made, logit_read, negated, exped, turned, kept, mixed_up, divided, out_ready, gated_up,
         g_turned, g_kept) = (sem(n) for n in (
            "near_ready", "logit_made", "logit_read", "negated", "exped", "p_turned", "p_kept", "mixed_up", "divided",
            "out_ready", "gated_up", "g_turned", "g_kept"))
        gate_loaded = [sem("gate_loaded0"), sem("gate_loaded1")]
        gT, g_saved = sb("gT", [P, 4, SEQ]), sem("g_saved")
        units = [(t, h) for t in range(NQT) for h in range(H)]
        chunks_to = [0]
        groups_to = [0]
        for t, h in units:
            chunks_to.append(chunks_to[-1] + len(key_chunks(t)))
            groups_to.append(groups_to[-1] + -(-(t + 2) // 4))
        key_rows = lambda b: META if b == 0 else P
        key_col = lambda b: 0 if b == 0 else META + P * (b - 1)
        block = ctx.enter_context(nc.Block())

        @block.sync
        def _(sp):
            for t in range(NQT):
                if t >= 2:
                    sp.wait_ge(gated_up, t - 1)
                sp.dma_start(gate[:, t % 2], za_dram[t]).then_inc(gate_loaded[t % 2], 16)
            sp.wait_ge(g_kept, NQT)
            sp.dma_start(g_dram.rearrange("k p t -> p k t"), gT[:]).then_inc(g_saved, 16)
            sp.wait_ge(g_saved, 16)

        @block.gpsimd
        def _(pool):
            for n, (t, h) in enumerate(units):
                a, b = key_chunks(t)[-1]
                if n >= 4:
                    pool.wait_ge(logit_read, chunks_to[n - 3])
                nc.gpsimd.tensor_tensor(hidden[:, n % 4, 0:b - a], score[t][:, a:b], band[:, h, 2 * P - (b - a):2 * P],
                                        ALU.add).then_inc(near_ready, 1)

        @block.tensor
        def _(pe):
            def logits(n):
                t, h = units[n]
                r = slice(DH * (h % 2), DH * (h % 2) + DH)
                for c, (a, b) in enumerate(key_chunks(t)):
                    m = chunks_to[n] + c
                    if m >= LG:
                        pe.wait_ge(logit_read, m - LG + 1)
                    nc.tensor.matmul(lg[m % LG][:, 0:b - a], qT[r, h // 2, P * t:P * t + P], kT[r, h // 2, a:b],
                                     start=True, stop=True).then_inc(logit_made, 1)

            def turn(n):
                t, h = units[n]
                pe.wait_ge(exped, n + 1)
                for g in range(groups_to[n + 1] - groups_to[n]):
                    m = groups_to[n] + g
                    if m >= PT:
                        pe.wait_ge(kept, m - PT + 1)
                    for b in range(4 * g, min(4 * g + 4, t + 2)):
                        k, c = key_rows(b), key_col(b)
                        last = nc.tensor.transpose(pt[m % PT][0:k, b - 4 * g, :], prob[:, n % 2, c:c + k], ident[:])
                    last.then_inc(turned, 1)

            def mix(n):
                t, h = units[n]
                pe.wait_ge(kept, groups_to[n + 1])
                if h == 0 and t >= 1:
                    pe.wait_ge(divided, t)
                for b in range(t + 2):
                    k = key_rows(b)
                    last = nc.tensor.matmul(po[:, DH * h:DH * h + DH], probT[0:k, n % 2, b, :],
                                            va[0:k, b, DH * h:DH * h + DH], start=(b == 0), stop=(b == t + 1))
                last.then_inc(mixed_up, 1)

            def turn_gated(t):
                pe.wait_ge(gated_up, t + 1)
                if t >= 1:
                    pe.wait_ge(g_kept, t)
                for f in range(4):
                    last = nc.tensor.transpose(pg[:, f, :], gated[:, t % 2, P * f:P * f + P], ident[:])
                last.then_inc(g_turned, 1)

            for n in range(len(units) + 3):
                if n < len(units):
                    logits(n)
                if 1 <= n <= len(units):
                    turn(n - 1)
                if 2 <= n <= len(units) + 1:
                    mix(n - 2)
                if n >= 12 and (n - 12) % H == 0 and (n - 12) // H < NQT - 1:
                    turn_gated((n - 12) // H)
            turn_gated(NQT - 1)

        @block.vector
        def _(dve):
            def masked_max(n):
                t, h = units[n]
                chunks = key_chunks(t)
                if n >= 2:
                    dve.wait_ge(exped, n - 1)
                for c, (a, b) in enumerate(chunks):
                    m = chunks_to[n] + c
                    near = c == len(chunks) - 1
                    dve.wait_ge(logit_made, m + 1)
                    if near:
                        dve.wait_ge(near_ready, n + 1)
                    if c:
                        dve.wait_ge(logit_read, m)
                    nc.vector.tensor_tensor_reduce(
                        out=logit[:, n % 2, a:b], in0=lg[m % LG][:, 0:b - a],
                        in1=hidden[:, n % 4, 0:b - a] if near else score[t][:, a:b],
                        scale=1.0, scalar=best[:, 4 * n + c - 1:4 * n + c] if c else -3.0e38, op0=ALU.add, op1=ALU.max,
                        accum_out=best[:, 4 * n + c:4 * n + c + 1]).then_inc(logit_read, 1)
                dve.wait_ge(logit_read, chunks_to[n + 1])
                c = 4 * n + len(chunks) - 1
                nc.vector.tensor_scalar(worst[:, n:n + 1], best[:, c:c + 1], -1.0, None, ALU.mult).then_inc(negated, 1)

            def finish(t):
                dve.wait_ge(exped, H * t + H)
                nc.vector.reciprocal(inv[:, H * t:H * t + H], mass[:, H * t:H * t + H]).then_inc(out_ready, 1)
                dve.wait_ge(out_ready, t + 1)
                dve.wait_ge(mixed_up, H * t + H)
                nc.vector.tensor_tensor(mixed[:, t % 2].rearrange("p (h d) -> p h d", d=DH),
                                        po[:].rearrange("p (h d) -> p h d", d=DH),
                                        inv[:, H * t:H * t + H].unsqueeze(2).to_broadcast([P, H, DH]),
                                        ALU.mult).then_inc(divided, 1)
                dve.wait_ge(divided, t + 1)
                dve.wait_ge(gate_loaded[t % 2], 16 * (t // 2 + 1))
                if t >= 2:
                    dve.wait_ge(g_turned, t - 1)
                nc.vector.tensor_tensor(gated[:, t % 2], mixed[:, t % 2], gate[:, t % 2],
                                        ALU.mult).then_inc(gated_up, 1)

            for n in range(len(units)):
                masked_max(n)
                if n >= 10 and (n - 10) % H == 0:
                    finish((n - 10) // H)
            finish(NQT - 1)

        @block.scalar
        def _(act):
            def exp(n):
                t, h = units[n]
                w = keys_of(t)
                act.wait_ge(negated, n + 1)
                if n >= 2:
                    act.wait_ge(turned, groups_to[n - 1])
                nc.scalar.activation(prob[:, n % 2, 0:w], logit[:, n % 2, 0:w], ACT.Exp, bias=worst[:, n:n + 1],
                                     accum_out=mass[:, n:n + 1]).then_inc(exped, 1)

            def keep(n):
                t, h = units[n]
                if n >= 2:
                    act.wait_ge(mixed_up, n - 1)
                for g in range(groups_to[n + 1] - groups_to[n]):
                    m = groups_to[n] + g
                    act.wait_ge(turned, m + 1)
                    lo, hi = 4 * g, min(4 * g + 4, t + 2)
                    if g == 0:
                        nc.scalar.activation(probT[0:META, n % 2, 0, :], pt[m % PT][0:META, 0, :], ACT.Copy)
                        lo = 1
                    nc.scalar.activation(probT[:, n % 2, lo:hi, :], pt[m % PT][:, lo - 4 * g:hi - 4 * g, :],
                                         ACT.Copy).then_inc(kept, 1)

            def keep_gated(t):
                act.wait_ge(g_turned, t + 1)
                nc.scalar.activation(gT[:, :, P * t:P * t + P], pg[:], ACT.Copy).then_inc(g_kept, 1)

            for n in range(len(units) + 1):
                if n < len(units):
                    exp(n)
                if n >= 1:
                    keep(n - 1)
                if n >= 13 and (n - 13) % H == 0 and (n - 13) // H < NQT - 1:
                    keep_gated((n - 13) // H)
            keep_gated(NQT - 1)


def chunk_table():
    import numpy as np
    i, j = np.arange(P)[:, None], np.arange(P)[None, :]
    same = i // CHUNK == j // CHUNK
    parts = [same & (i <= j), same, (i < CHUNK) & (j >= 0), (i >= CHUNK) & (j >= 0)]
    table = [p.astype(np.float32) for p in parts]
    for l in range(6):
        table.append(np.eye(P, dtype=np.float32) - ((i >> l) % 2 == 1) * ((i >> l) - 1 == j >> l))
    return np.ascontiguousarray(np.stack(table, 1)).astype(np.float32)


def decays(nc, small, chunk, chunk_tab, a_log, dt_bias, beta, nbeta, gates, gsum, to_here, to_end, whole):
    with ExitStack() as ctx:
        sb = lambda name, shape: ctx.enter_context(nc.sbuf_tensor(name, shape, F32))
        sem = lambda n: ctx.enter_context(nc.semaphore(n))
        alog, dtb, nega = sb("alog", [P, H]), sb("dtb", [P, H]), sb("nega", [P, H])
        z, mag, e, ln, pos = (sb(n, [P, NT, H]) for n in ("z", "mag", "e", "ln", "pos"))
        sums = ctx.enter_context(nc.psum_tensor("sums", [P, 4, NT * H], F32))
        vloaded, cloaded, d, a, p = sem("vloaded"), sem("cloaded"), sem("d_dve"), sem("d_act"), sem("d_pe")
        block = ctx.enter_context(nc.Block())

        @block.sync
        def _(sp):
            sp.dma_start(alog[:], a_log.to_broadcast([P, H])).then_inc(vloaded, 16)
            sp.dma_start(dtb[:], dt_bias.to_broadcast([P, H])).then_inc(vloaded, 16)
            sp.dma_start(chunk[:], chunk_tab).then_inc(cloaded, 16)

        @block.scalar
        def _(act):
            nc.scalar.activation(beta[:], small[:, :, H:2 * H], ACT.Sigmoid).then_inc(a, 1)
            act.wait_ge(vloaded, 32)
            nc.scalar.activation(nega[:], alog[:], ACT.Exp).then_inc(a, 1)
            act.wait_ge(d, 1)
            nc.scalar.activation(mag[:], z[:], ACT.Abs).then_inc(a, 1)
            act.wait_ge(a, 3)
            nc.scalar.activation(e[:], mag[:], ACT.Exp, scale=-1.0).then_inc(a, 1)
            act.wait_ge(d, 2)
            nc.scalar.activation(ln[:], mag[:], ACT.Ln).then_inc(a, 1)
            act.wait_ge(d, 8)
            nc.scalar.activation(to_here[:], gsum[:], ACT.Exp).then_inc(a, 1)
            nc.scalar.activation(to_end[:], z[:], ACT.Exp).then_inc(a, 1)
            nc.scalar.activation(whole[:], sums[:, 2:4].rearrange("p c (t h) -> p c t h", h=H), ACT.Exp).then_inc(a, 1)

        @block.vector
        def _(dve):
            dve.wait_ge(vloaded, 32)
            nc.vector.tensor_tensor(z[:], small[:, :, 2 * H:3 * H],
                                    dtb[:].unsqueeze(1).to_broadcast([P, NT, H]), ALU.add).then_inc(d, 1)
            dve.wait_ge(a, 4)
            nc.vector.tensor_scalar(mag[:], e[:], 1.0, None, ALU.add).then_inc(d, 1)
            nc.vector.tensor_scalar(pos[:], z[:], 0.0, None, ALU.max).then_inc(d, 1)
            nc.vector.tensor_scalar(nbeta[:], beta[:], -1.0, None, ALU.mult).then_inc(d, 1)
            dve.wait_ge(a, 5)
            dve.wait_ge(d, 3)
            nc.vector.tensor_tensor(e[:], ln[:], pos[:], ALU.add).then_inc(d, 1)
            dve.wait_ge(d, 5)
            nc.vector.scalar_tensor_tensor(gates[:], e[:], -1.0, nega[:].unsqueeze(1).to_broadcast([P, NT, H]),
                                           ALU.mult, ALU.mult).then_inc(d, 1)
            dve.wait_ge(p, 1)
            nc.vector.tensor_copy(gsum[:], sums[:, 0].rearrange("p (t h) -> p t h", h=H)).then_inc(d, 1)
            dve.wait_ge(d, 7)
            nc.vector.tensor_tensor(z[:], sums[:, 1].rearrange("p (t h) -> p t h", h=H), gsum[:],
                                    ALU.subtract).then_inc(d, 1)

        @block.tensor
        def _(pe):
            pe.wait_ge(cloaded, 16)
            pe.wait_ge(d, 6)
            for c in range(4):
                last = nc.tensor.matmul(sums[:, c], chunk[:, c], gates[:].rearrange("p t h -> p (t h)"),
                                        start=True, stop=True)
            last.then_inc(p, 1)


GROUPS, GT = 3, 3
GW = GT * P
LEVELS = 6
CHUNKS = 2 * NT


def delta_heads(nc, w_in, conv_w, gdn_norm_w, hT, ident, ones, chunk, beta, nbeta, gates, gsum, to_here, to_end,
                whole, zb_dram, og_dram):
    w_v = w_in.rearrange("l (k p) n -> p (l k) n", p=P)
    PK, PQ, PV = range(3)
    offs = {PK: OFF_KB, PQ: OFF_QB, PV: OFF_VB}
    wide = {PK: D, PQ: 0, PV: 2 * D}
    with ExitStack() as ctx:
        sb = lambda name, shape: ctx.enter_context(nc.sbuf_tensor(name, shape, F32))
        sem = lambda n: ctx.enter_context(nc.semaphore(n))
        w3 = sb("w3", [P, 3, KD, P])
        xs, ys = sb("xs", [P, 3, TP]), sb("ys", [P, 3, TP])
        rk, rq = sb("rk", [P, TP]), sb("rq", [P, TP])
        grow, LA, LB = sb("grow", [P, TP]), sb("LA", [P, TP]), sb("LB", [P, TP])
        tiled = lambda name: sb(name, [P, NT, P])
        kt, ke, kd, vt, U, at, W, X, u = (tiled(n) for n in ("kt", "ke", "kd", "vt", "U", "at", "W", "X", "u"))
        R = sb("R", [P, 2, NT, P])
        wq = sb("wq", [P, NT, 4, CHUNK])
        vnew, S = sb("vnew", [P, 2, P]), sb("S", [P, 2, P])
        o, zb = tiled("o"), sb("zb_head", [P, NQT, P])
        osq, ovar, oln, orstd = sb("osq", [P, NQT, P]), sb("ovar", [P, NQT]), sb("oln", [P, NQT]), sb("orstd", [P, NQT])
        og = sb("og_head", [P, SEQ])
        cw, gw, consts = sb("cw", [P, 4, 3 * H]), sb("gw", [P, 1]), sb("consts", [P, 3])
        pr = [ctx.enter_context(nc.psum_tensor(f"pr{i}", [P, 512], F32)) for i in range(2)]
        so = [ctx.enter_context(nc.psum_tensor(f"so{i}", [P, P], F32)) for i in range(2)]
        skv = ctx.enter_context(nc.psum_tensor("skv", [P, P], F32))
        WB = 3
        wk = [ctx.enter_context(nc.psum_tensor(f"wk{i}", [P, 512], F32)) for i in range(WB)]

        work = []
        for h in range(H + 1):
            if h < H:
                work += [("grow", h, 0, g) for g in range(GROUPS)]
                work += [("sum", h, j, g) for j in (PK, PQ) for g in range(GROUPS)]
            if h >= 1:
                work += [("post", h - 1, 0, g) for g in range(2)]
            if h < H:
                work += [(x, h, 0, g) for x in ("kk", "kt", "vt", "at") for g in range(GROUPS)]
                for l in range(LEVELS):
                    work += [("Q", h, l, g) for g in range(GROUPS)]
                    for g in range(GROUPS):
                        work += ([("X", h, l, g)] if 0 < l < LEVELS - 1 else []) + [("W", h, l, g)]
                work += [("wT", h, 0, g) for g in range(GROUPS)] + [("u", h, 0, g) for g in range(GROUPS)]
        by_dve = ("kk", "at", "Q", "u")
        place, read_no = {}, {}
        counts = [0, 0]
        for n, key in enumerate(work):
            who = key[0] in by_dve
            counts[who] += 1
            place[key], read_no[key] = n, counts[who]

        (worked, read_act, read_dve) = (sem(n) for n in ("worked", "read_act", "read_dve"))
        (const_made, zeroed, cw_loaded, w_loaded, proj_made, proj_kept, conved, rough, activated, squared, rooted,
         normed, ldiff, growexp, lexp, lmasked, lbeta, udiag, kscaled, qdec) = (sem(n) for n in (
            "const_made", "zeroed", "cw_loaded", "w3_loaded", "proj_made", "proj_kept", "conved", "rough", "activated",
            "squared", "rooted", "normed", "ldiff", "growexp", "lexp", "lmasked", "lbeta", "udiag", "kscaled", "qdec"))
        (s_made, v_new, kv_made, o_made, s_kept, o_kept, o_squared, o_summed, o_ln, o_root, o_scaled, z_loaded,
         og_saved) = (sem(n) for n in (
            "s_made", "v_new", "kv_made", "o_made", "s_kept", "o_kept", "o_squared", "o_summed", "o_ln", "o_root",
            "o_scaled", "z_loaded", "og_saved"))
        block = ctx.enter_context(nc.Block())

        def read(eng, key):
            eng.wait_ge(read_dve if key[0] in by_dve else read_act, read_no[key])

        steps = CHUNKS - 1
        PS = spans(T)
        NP = 3 * len(PS)

        @block.sync
        def _(sp):
            with nc.allow_non_contiguous_dma(reason="per-feature weights on partitions"):
                for k in range(4):
                    sp.dma_start(cw[:, k], conv_w[0, k].rearrange("(f p) -> p f", p=P)).then_inc(cw_loaded, 16)
                sp.dma_start(gw[:], gdn_norm_w.rearrange("l d -> d l")).then_inc(cw_loaded, 16)
            for h in range(H):
                if h >= 1:
                    sp.wait_ge(proj_made, NP * h)
                for j in range(3):
                    c = offs[j] + P * h
                    sp.dma_start(w3[:, j], w_v[:, :, c:c + P]).then_inc(w_loaded, 16)
                if h >= 1:
                    sp.wait_ge(o_scaled, 2 * h)
                for half in range(2):
                    src = zb_dram[:, CHUNK * (1 - half):CHUNK * (2 - half), P * h:P * h + P].rearrange("t p c -> p t c")
                    sp.dma_start(zb[CHUNK * half:CHUNK * half + CHUNK], src).then_inc(z_loaded, 16)
                if h >= 1:
                    read(sp, ("post", h - 1, 0, 1))
                    sp.dma_start(og_dram[h - 1], og[:]).then_inc(og_saved, 16)
            read(sp, ("post", H - 1, 0, 1))
            sp.dma_start(og_dram[H - 1], og[:]).then_inc(og_saved, 16)
            sp.wait_ge(og_saved, 16 * H)

        @block.gpsimd
        def _(pool):
            nc.gpsimd.memset(consts[:, 0:1], EPS)
            nc.gpsimd.memset(consts[:, 1:2], 0.0)
            nc.gpsimd.memset(consts[:, 2:3], -0.5 * math.log(DK)).then_inc(const_made, 1)
            nc.gpsimd.memset(xs[:, :, 0:PAD], 0.0).then_inc(zeroed, 1)
            nc.gpsimd.memset(ys[:, :, 0:PAD], 0.0).then_inc(zeroed, 1)
            tri = chunk[:, 0:1].to_broadcast([P, NT, P])
            for h in range(H):
                pool.wait_ge(lexp, h + 1)
                nc.gpsimd.tensor_tensor(LA[:].rearrange("p (t i) -> p t i", i=P), LA[:].rearrange("p (t i) -> p t i", i=P),
                                        tri, ALU.mult).then_inc(lmasked, 1)
                pool.wait_ge(lmasked, h + 1)
                nc.gpsimd.tensor_tensor(LB[:].rearrange("p (t i) -> p t i", i=P), LA[:].rearrange("p (t i) -> p t i", i=P),
                                        beta[:, :, h:h + 1].to_broadcast([P, NT, P]), ALU.mult).then_inc(lbeta, 1)
                for g in range(GROUPS):
                    read(pool, ("kk", h, 0, g))
                    part = U[:, GT * g:GT * g + GT]
                    nc.gpsimd.affine_select(out=part, in_=part, compare_op=ALU.not_equal, fill=1.0, base=0,
                                            pattern=[[0, GT], [-1, P]], channel_multiplier=1).then_inc(udiag, 1)
                read(pool, ("kt", h, 0, GROUPS - 1))
                if h >= 1:
                    pool.wait_ge(kv_made, steps * h)
                for dst, by in ((ke, to_here), (kd, to_end)):
                    nc.gpsimd.tensor_tensor(dst[:], kt[:], by[:, :, h:h + 1].to_broadcast([P, NT, P]),
                                            ALU.mult).then_inc(kscaled, 1)

        @block.tensor
        def _(pe):
            def project(h, n):
                j, s = divmod(n, len(PS))
                a, b = PS[s]
                if n == 0:
                    pe.wait_ge(w_loaded, 48 * (h + 1))
                m = NP * h + n
                if m >= 2:
                    pe.wait_ge(proj_kept, m - 1)
                for k in range(KD):
                    last = nc.tensor.matmul(pr[m % 2][:, 0:b - a], w3[:, j, k], hT[:, k, PAD + a:PAD + b],
                                            start=(k == 0), stop=(k == KD - 1))
                last.then_inc(proj_made, 1)

            def walk(h):
                done = 0
                for n in range(steps):
                    c = n + 1
                    t, half = c // 2, c % 2
                    r, r2 = CHUNK * half, CHUNK * (1 - half)
                    m = steps * h + n
                    bank = so[m % 2]
                    if n == 0:
                        read(pe, ("wT", h, 0, GROUPS - 1))
                        pe.wait_ge(qdec, h + 1)
                        pe.wait_ge(kscaled, 2 * h + 2)
                        read(pe, ("u", h, 0, GROUPS - 1))
                    if m >= 2:
                        pe.wait_ge(o_kept, m - 1)
                    pe.wait_ge(s_kept, m + h + 1)
                    nc.tensor.matmul(bank[:], wq[:, t, 2 * half:2 * half + 2].rearrange("p a b -> p (a b)"),
                                     S[:, n % 2], start=True, stop=True, skip_group_check=True).then_inc(s_made, 1)
                    pe.wait_ge(v_new, m + 1)
                    nc.tensor.matmul(skv[:], kd[r:r + CHUNK, t], vnew[r:r + CHUNK, n % 2],
                                     start=True, stop=True).then_inc(kv_made, 1)
                    nc.tensor.matmul(bank[r2:r2 + CHUNK], at[r:r + CHUNK, t, r:r + CHUNK], vnew[r:r + CHUNK, n % 2],
                                     start=False, stop=True, skip_group_check=True).then_inc(o_made, 1)
                    while h + 1 < H and done < NP * (n + 1) // steps:
                        project(h + 1, done)
                        done += 1

            for n in range(NP):
                project(0, n)
            for n, key in enumerate(work):
                what, h, l, g = key
                bank = wk[n % WB]
                out = bank[:, 0:GW]
                tiles = range(GT * g, GT * g + GT)
                if n >= WB:
                    read(pe, work[n - WB])
                if what == "grow":
                    for i, t in enumerate(tiles):
                        last = nc.tensor.matmul(out[:, P * i:P * i + P], gates[:, t, h:h + 1].to_broadcast([P, P]),
                                                chunk[:, 0], start=True, stop=True)
                elif what == "sum":
                    pe.wait_ge(squared, 2 * h + 1 + (l == PQ))
                    last = nc.tensor.matmul(out, ones[:], xs[:, l, GW * g:GW * g + GW], start=True, stop=True)
                elif what == "post":
                    pe.wait_ge(o_scaled, 2 * h + 2)
                    for i in range(4):
                        last = nc.tensor.transpose(bank[:, P * i:P * i + P], o[:, 1 + 4 * g + i], ident[:])
                elif what in ("kk", "at"):
                    pe.wait_ge(normed, 2 * h + 1 + (what == "at"))
                    for i, t in enumerate(tiles):
                        last = nc.tensor.matmul(out[:, P * i:P * i + P], ys[:, PK, P * t:P * t + P],
                                                ys[:, PK if what == "kk" else PQ, P * t:P * t + P], start=True, stop=True)
                elif what in ("kt", "vt"):
                    if what == "vt":
                        pe.wait_ge(activated, 3 * h + 3)
                    for i, t in enumerate(tiles):
                        last = nc.tensor.transpose(out[:, P * i:P * i + P],
                                                   ys[:, PK if what == "kt" else PV, P * t:P * t + P], ident[:])
                elif what == "Q":
                    if l == 0:
                        pe.wait_ge(udiag, GROUPS * h + g + 1)
                    elif l == 1:
                        read(pe, ("Q", h, 0, g))
                    else:
                        read(pe, ("X", h, l - 1, g))
                    for i, t in enumerate(tiles):
                        x = ident[:] if l == 0 else R[:, 0, t] if l == 1 else X[:, t]
                        last = nc.tensor.matmul(out[:, P * i:P * i + P], U[:, t], x, start=True, stop=True)
                elif what == "X":
                    read(pe, ("W", h, l - 1, g))
                    read(pe, ("Q", h, l, g))
                    for i, t in enumerate(tiles):
                        last = nc.tensor.matmul(out[:, P * i:P * i + P], W[:, t], R[:, l % 2, t], start=True, stop=True)
                elif what == "W":
                    read(pe, ("Q", h, l, g))
                    if l:
                        read(pe, ("W", h, l - 1, g))
                    for i, t in enumerate(tiles):
                        last = nc.tensor.matmul(out[:, P * i:P * i + P], R[:, l % 2, t], W[:, t] if l else ident[:],
                                                start=True, stop=True)
                elif what == "wT":
                    read(pe, ("W", h, LEVELS - 1, g))
                    pe.wait_ge(kscaled, 2 * h + 1)
                    for i, t in enumerate(tiles):
                        last = nc.tensor.matmul(out[:, P * i:P * i + P], ke[:, t], W[:, t], start=True, stop=True)
                elif what == "u":
                    read(pe, ("vt", h, 0, g))
                    for i, t in enumerate(tiles):
                        last = nc.tensor.matmul(out[:, P * i:P * i + P], W[:, t], vt[:, t], start=True, stop=True)
                last.then_inc(worked, 1)
                if what == "u" and g == GROUPS - 1:
                    walk(h)

        @block.vector
        def _(dve):
            def conv(h, j):
                c = 8 * (wide[j] // D) + h
                dve.wait_ge(proj_kept, NP * h + (j + 1) * len(PS))
                if h >= 1 and j == PV:
                    read(dve, ("vt", h - 1, 0, GROUPS - 1))
                for k in range(4):
                    src = xs[:, j, PAD - 3 + k:TP - 3 + k]
                    dst = ys[:, j, PAD:TP]
                    if k == 0:
                        nc.vector.tensor_scalar(dst, src, cw[:, k, c:c + 1], None, ALU.mult).then_inc(conved, 1)
                    else:
                        dve.wait_ge(conved, 12 * h + 4 * j + k)
                        nc.vector.scalar_tensor_tensor(dst, src, cw[:, k, c:c + 1], dst, ALU.mult,
                                                       ALU.add).then_inc(conved, 1)

            def post(h):
                dve.wait_ge(o_squared, h + 1)
                nc.vector.tensor_reduce(ovar[:], osq[:], AX.X, ALU.add).then_inc(o_summed, 1)
                dve.wait_ge(o_root, h + 1)
                nc.vector.tensor_tensor(o[:, 1:], o[:, 1:], orstd[:].unsqueeze(2).to_broadcast([P, NQT, P]),
                                        ALU.mult).then_inc(o_scaled, 1)
                dve.wait_ge(o_scaled, 2 * h + 1)
                dve.wait_ge(z_loaded, 32 * h + 32)
                nc.vector.tensor_tensor(o[:, 1:], o[:, 1:], zb[:], ALU.mult).then_inc(o_scaled, 1)

            def prepare(h):
                tile3 = lambda x, g: x[:, GW * g:GW * g + GW]
                for i, j, r in ((0, PK, rk), (1, PQ, rq)):
                    dve.wait_ge(rooted, 2 * h + i + 1)
                    nc.vector.tensor_tensor(ys[:, j], ys[:, j], r[:], ALU.mult).then_inc(normed, 1)
                read(dve, ("grow", h, 0, GROUPS - 1))
                for t in range(NT):
                    last = nc.vector.tensor_scalar(LA[:, P * t:P * t + P], grow[:, P * t:P * t + P],
                                                   gsum[:, t, h:h + 1], 0.0, ALU.subtract, ALU.min)
                last.then_inc(ldiff, 1)
                dve.wait_ge(growexp, h + 1)
                dve.wait_ge(normed, 2 * h + 2)
                nc.vector.tensor_tensor(wq[:, :, 1:3].rearrange("p t a b -> p t (a b)"),
                                        ys[:, PQ].rearrange("p (t i) -> p t i", i=P),
                                        grow[:].rearrange("p (t i) -> p t i", i=P), ALU.mult).then_inc(qdec, 1)
                for x, sc, dst in (("kk", LB, U), ("at", LA, at)):
                    dve.wait_ge(lbeta, h + 1)
                    for g in range(GROUPS):
                        key = (x, h, 0, g)
                        dve.wait_ge(worked, place[key] + 1)
                        nc.vector.tensor_tensor(dst[:, GT * g:GT * g + GT].rearrange("p t i -> p (t i)"),
                                                wk[place[key] % WB][:, 0:GW], tile3(sc, g), ALU.mult).then_inc(read_dve, 1)
                for l in range(LEVELS):
                    for g in range(GROUPS):
                        key = ("Q", h, l, g)
                        dve.wait_ge(worked, place[key] + 1)
                        nc.vector.tensor_tensor(R[:, l % 2, GT * g:GT * g + GT],
                                                wk[place[key] % WB][:, 0:GW].rearrange("p (t i) -> p t i", i=P),
                                                chunk[:, 4 + l:5 + l].to_broadcast([P, GT, P]), ALU.mult).then_inc(read_dve, 1)
                for g in range(GROUPS):
                    key = ("u", h, 0, g)
                    dve.wait_ge(worked, place[key] + 1)
                    nc.vector.tensor_tensor(u[:, GT * g:GT * g + GT],
                                            wk[place[key] % WB][:, 0:GW].rearrange("p (t i) -> p t i", i=P),
                                            beta[:, GT * g:GT * g + GT, h:h + 1].to_broadcast([P, GT, P]),
                                            ALU.mult).then_inc(read_dve, 1)

            def walk(h):
                nc.vector.memset(S[:, 0], 0.0).then_inc(s_kept, 1)
                done = 0
                for n in range(steps):
                    c = n + 1
                    t, half = c // 2, c % 2
                    r = slice(CHUNK * half, CHUNK * half + CHUNK)
                    m = steps * h + n
                    dve.wait_ge(s_made, m + 1)
                    if n == 0:
                        read(dve, ("u", h, 0, GROUPS - 1))
                    nc.vector.scalar_tensor_tensor(vnew[r, n % 2], so[m % 2][r, :], nbeta[r, t, h:h + 1], u[r, t],
                                                   ALU.mult, ALU.add).then_inc(v_new, 1)
                    dve.wait_ge(kv_made, m + 1)
                    dve.wait_ge(s_kept, m + h + 1)
                    nc.vector.scalar_tensor_tensor(S[:, (n + 1) % 2], S[:, n % 2], whole[:, half, t, h:h + 1], skv[:],
                                                   ALU.mult, ALU.add).then_inc(s_kept, 1)
                    if h + 1 < H and n in (7, 13):
                        conv(h + 1, done)
                        done += 1

            dve.wait_ge(cw_loaded, 80)
            dve.wait_ge(zeroed, 2)
            for j in range(3):
                conv(0, j)
            for h in range(H):
                prepare(h)
                walk(h)
                if h + 1 < H:
                    conv(h + 1, PV)
                post(h)

        @block.scalar
        def _(act):
            def keep_projected(h, n):
                j, s = divmod(n, len(PS))
                a, b = PS[s]
                m = NP * h + n
                act.wait_ge(proj_made, m + 1)
                if h >= 1 and n == 0:
                    act.wait_ge(worked, place[("sum", h - 1, PQ, GROUPS - 1)] + 1)
                nc.scalar.activation(xs[:, j, PAD + a:PAD + b], pr[m % 2][:, 0:b - a], ACT.Copy).then_inc(proj_kept, 1)

            def swish(h):
                for j in range(3):
                    act.wait_ge(conved, 12 * h + 4 * j + 4)
                    nc.scalar.activation(ys[:, j, PAD:TP], ys[:, j, PAD:TP], ACT.Silu).then_inc(activated, 1)
                    if j != PV:
                        act.wait_ge(activated, 3 * h + j + 1)
                        nc.scalar.activation(xs[:, j, PAD:TP], ys[:, j, PAD:TP], ACT.Square).then_inc(squared, 1)

            def take(key, dst, func=ACT.Copy, w=GW, **kw):
                bank = wk[place[key] % WB][:, 0:w]
                if len(dst.shape) == 3:
                    bank = bank.rearrange("p (t i) -> p t i", t=dst.shape[1])
                if len(dst.shape) == 4:
                    bank = bank.rearrange("p (t a b) -> p t a b", t=dst.shape[1], a=2)
                act.wait_ge(worked, place[key] + 1)
                nc.scalar.activation(dst, bank, func, **kw).then_inc(read_act, 1)

            def root(h):
                for g in range(GROUPS):
                    take(("grow", h, 0, g), grow[:, GW * g:GW * g + GW])
                for j, r in ((PK, rk), (PQ, rq)):
                    for g in range(GROUPS):
                        take(("sum", h, j, g), r[:, GW * g:GW * g + GW], ACT.Ln, bias=consts[:, 0:1])
                for i, r in enumerate((rk, rq)):
                    read(act, ("sum", h, (PK, PQ)[i], GROUPS - 1))
                    nc.scalar.activation(r[:], r[:], ACT.Exp, scale=-0.5, bias=consts[:, 1 + i:2 + i]).then_inc(rooted, 1)

            def post_norm(h):
                act.wait_ge(o_kept, steps * (h + 1))
                nc.scalar.activation(osq[:], o[:, 1:], ACT.Square).then_inc(o_squared, 1)
                act.wait_ge(o_summed, h + 1)
                nc.scalar.activation(oln[:], ovar[:], ACT.Ln, scale=1.0 / DK, bias=consts[:, 0:1]).then_inc(o_ln, 1)
                act.wait_ge(o_ln, h + 1)
                nc.scalar.activation(orstd[:], oln[:], ACT.Exp, scale=-0.5).then_inc(o_root, 1)

            def post_keep(h):
                if h >= 1:
                    act.wait_ge(og_saved, 16 * h)
                for g in range(2):
                    key = ("post", h, 0, g)
                    act.wait_ge(worked, place[key] + 1)
                    src = wk[place[key] % WB][:].rearrange("p (t a b) -> p t a b", t=4, a=2)
                    dst = og[:, 512 * g:512 * g + 512].rearrange("p (t a b) -> p t a b", t=4, a=2)
                    nc.scalar.activation(dst[:, :, 0], src[:, :, 1], ACT.Copy, scale=gw[:, 0:1])
                    nc.scalar.activation(dst[:, :, 1], src[:, :, 0], ACT.Copy, scale=gw[:, 0:1]).then_inc(read_act, 1)

            def prepare(h):
                act.wait_ge(ldiff, h + 1)
                nc.scalar.activation(grow[:], grow[:], ACT.Exp).then_inc(growexp, 1)
                nc.scalar.activation(LA[:], LA[:], ACT.Exp).then_inc(lexp, 1)
                for x, dst in (("kt", kt), ("vt", vt)):
                    for g in range(GROUPS):
                        if x == "kt" and h >= 1 and g == 0:
                            act.wait_ge(kscaled, 2 * h)
                        take((x, h, 0, g), dst[:, GT * g:GT * g + GT])
                for l in range(LEVELS):
                    for g in range(GROUPS):
                        if 0 < l < LEVELS - 1:
                            take(("X", h, l, g), X[:, GT * g:GT * g + GT])
                        take(("W", h, l, g), W[:, GT * g:GT * g + GT])
                for g in range(GROUPS):
                    take(("wT", h, 0, g), wq[:, GT * g:GT * g + GT, 0:4:3])

            def walk(h):
                done = 0
                for n in range(steps):
                    c = n + 1
                    t, half = c // 2, c % 2
                    r2 = slice(CHUNK * (1 - half), CHUNK * (2 - half))
                    m = steps * h + n
                    act.wait_ge(o_made, m + 1)
                    nc.scalar.activation(o[r2, t], so[m % 2][r2, :], ACT.Copy).then_inc(o_kept, 1)
                    while h + 1 < H and done < NP * (n + 1) // steps:
                        keep_projected(h + 1, done)
                        done += 1

            act.wait_ge(const_made, 1)
            act.wait_ge(zeroed, 2)
            act.wait_ge(cw_loaded, 80)
            for n in range(NP):
                keep_projected(0, n)
            swish(0)
            for h in range(H + 1):
                if h < H:
                    root(h)
                if h >= 1:
                    post_keep(h - 1)
                if h < H:
                    prepare(h)
                    walk(h)
                    if h + 1 < H:
                        swish(h + 1)
                    post_norm(h)


def merge(nc, x, g_dram, og_dram, gates_dram, w_proj_a, w_proj_b, w_out, out):
    KA = WA // P
    x_v, out_v = (a.rearrange("b (t p) d -> (b t) p d", p=P) for a in (x, out))
    with ExitStack() as ctx:
        sb = lambda name, shape: ctx.enter_context(nc.sbuf_tensor(name, shape, F32))
        sem = lambda n: ctx.enter_context(nc.semaphore(n))
        wa, wb, wo = sb("wa", [P, KA, D]), sb("wb", [P, KD, D]), sb("wo", [P, KD, D])
        ga_in, gb_in = sb("ga_in", [P, KA, SEQ]), sb("gb_in", [P, KD, SEQ])
        gate = sb("mgate", [P, 2, 2, SEQ])
        part, mT = sb("part", [P, 2, 512]), sb("mT", [P, KD, SEQ])
        xin, res = sb("xin", [P, 2, D]), sb("res", [P, 2, 512])
        NB = 8
        ps = [ctx.enter_context(nc.psum_tensor(f"mp{i}", [P, 512], F32)) for i in range(NB)]
        a_in, b_in, wo_in = sem("a_in"), sem("b_in"), sem("wo_in")
        gate_in = [sem("gate_in0"), sem("gate_in1")]
        x_in = [sem("x_in0"), sem("x_in1")]
        made, taken, mixed, added = sem("m_made"), sem("m_taken"), sem("m_mixed"), sem("m_added")
        out_saved = [sem("out_saved0"), sem("out_saved1")]
        pairs = [(f, c) for f in range(KD) for c in range(2)]
        outs = [(t, c) for t in range(NQT) for c in range(2)]
        block = ctx.enter_context(nc.Block())

        @block.sync
        def _(sp):
            sp.dma_start(wa[:], w_proj_a.rearrange("l (k p) n -> p (l k) n", p=P)).then_inc(a_in, 16)
            sp.dma_start(ga_in[:], g_dram.rearrange("k p t -> p k t")).then_inc(a_in, 16)
            sp.dma_start(wb[:], w_proj_b.rearrange("l (k p) n -> p (l k) n", p=P)).then_inc(b_in, 16)
            sp.dma_start(gb_in[:], og_dram.rearrange("k p t -> p k t")).then_inc(b_in, 16)
            for f in range(KD):
                if f >= 2:
                    sp.wait_ge(mixed, 2 * (f - 1))
                for j in range(2):
                    sp.dma_start(gate[:, f % 2, j], gates_dram[KD * j + f]).then_inc(gate_in[f % 2], 16)
                if f == 1:
                    sp.dma_start(wo[:], w_out.rearrange("l (k p) n -> p (l k) n", p=P)).then_inc(wo_in, 16)
            for t in range(NQT):
                if t >= 2:
                    sp.wait_ge(added, 2 * (t - 1))
                sp.dma_start(xin[:, t % 2], x_v[t]).then_inc(x_in[t % 2], 16)

        @block.tensor
        def _(pe):
            for n, (f, c) in enumerate(pairs):
                for j, (w, src, ks) in enumerate(((wa, ga_in, KA), (wb, gb_in, KD))):
                    m = 2 * n + j
                    if n == 0:
                        pe.wait_ge((a_in, b_in)[j], 32)
                    if m >= NB:
                        pe.wait_ge(taken, m - NB + 1)
                    for k in range(ks):
                        last = nc.tensor.matmul(ps[m % NB][:], w[:, k, P * f:P * f + P], src[:, k, 512 * c:512 * c + 512],
                                                start=(k == 0), stop=(k == ks - 1))
                    last.then_inc(made, 1)
            pe.wait_ge(wo_in, 16)
            pe.wait_ge(mixed, len(pairs))
            for n, (t, c) in enumerate(outs):
                m = 2 * len(pairs) + n
                if n >= NB:
                    pe.wait_ge(added, n - NB + 1)
                for k in range(KD):
                    last = nc.tensor.matmul(ps[m % NB][:], mT[:, k, P * t:P * t + P], wo[:, k, 512 * c:512 * c + 512],
                                            start=(k == 0), stop=(k == KD - 1))
                last.then_inc(made, 1)

        @block.vector
        def _(dve):
            for n, (f, c) in enumerate(pairs):
                s = slice(512 * c, 512 * c + 512)
                dve.wait_ge(gate_in[f % 2], 32 * (f // 2 + 1))
                dve.wait_ge(made, 2 * n + 1)
                if n >= 2:
                    dve.wait_ge(mixed, n - 1)
                nc.vector.tensor_tensor(part[:, n % 2], ps[2 * n % NB][:], gate[:, f % 2, 0, s], ALU.mult).then_inc(taken, 1)
                dve.wait_ge(made, 2 * n + 2)
                nc.vector.tensor_tensor(mT[:, f, s], ps[(2 * n + 1) % NB][:], gate[:, f % 2, 1, s], ALU.mult).then_inc(taken, 1)
                dve.wait_ge(taken, 2 * n + 2)
                nc.vector.tensor_tensor(mT[:, f, s], mT[:, f, s], part[:, n % 2], ALU.add).then_inc(mixed, 1)
            for n, (t, c) in enumerate(outs):
                m = 2 * len(pairs) + n
                dve.wait_ge(x_in[t % 2], 16 * (t // 2 + 1))
                dve.wait_ge(made, m + 1)
                if n >= 2:
                    dve.wait_ge(out_saved[n % 2], 16 * (n // 2))
                nc.vector.tensor_tensor(res[:, n % 2], ps[m % NB][:], xin[:, t % 2, 512 * c:512 * c + 512],
                                        ALU.add).then_inc(added, 1)

        @block.scalar
        def _(act):
            for n, (t, c) in enumerate(outs):
                act.wait_ge(added, n + 1)
                act.dma_start(out_v[t, :, 512 * c:512 * c + 512], res[:, n % 2]).then_inc(out_saved[n % 2], 16)
            for s in range(2):
                act.wait_ge(out_saved[s], 16 * len(outs) // 2)


def hybrid_layer(nc, x, meta_tokens, rel_bias, norm_w, w_in, q_norm_w, k_norm_w, conv_w, a_log, dt_bias, gdn_norm_w,
                 w_proj_a, w_proj_b, w_out, band_tab, chunk_tab, out):
    dram = lambda name, shape: nc.dram_tensor(name, shape, F32, kind="Internal").ap()
    za_dram, zb_dram = dram("za_dram", (NQT, P, WA)), dram("zb_dram", (NQT, P, D))
    gates_dram, band_dram = dram("gates_dram", (2 * KD, P, SEQ)), dram("band_dram", (H, band_tab.shape[1]))
    g_dram, og_dram = dram("g_dram", (WA // P, P, SEQ)), dram("og_dram", (H, P, SEQ))
    sb = lambda stack, name, shape: stack.enter_context(nc.sbuf_tensor(name, shape, F32))
    with ExitStack() as whole_layer:
        ident, ones = sb(whole_layer, "ident", [P, P]), sb(whole_layer, "ones", [P, P])
        hT, small = sb(whole_layer, "hT", [P, KD, TP]), sb(whole_layer, "small", [P, NT, NSM])
        make_constants(nc, ident, ones)
        normed_tokens(nc, x, meta_tokens, norm_w, hT, ident)
        with ExitStack() as branch_a:
            score = [sb(branch_a, f"score{t}", [P, keys_of(t)]) for t in range(NQT)]
            va = sb(branch_a, "va", [P, NT, WA])
            qT, kT, band = sb(branch_a, "qT", [P, 4, SEQ]), sb(branch_a, "kT", [P, 4, T]), sb(branch_a, "band", [P, H, 2 * P])
            with ExitStack() as raw:
                qa, ka = sb(raw, "qa", [P, NT, WA]), sb(raw, "ka", [P, NT, WA])
                projections(nc, w_in, hT, small, score, qa, ka, va, qT, kT[:, 0], kT[:, 1:3], za_dram, zb_dram, gates_dram)
                attention_operands(nc, ident, qa, ka, qT, kT, band, rel_bias, band_tab, band_dram, q_norm_w, k_norm_w)
            attention(nc, ident, score, qT, kT, band, va, za_dram, g_dram)
        with ExitStack() as branch_b:
            chunk = sb(branch_b, "chunk", [P, 10, P])
            per_token = [sb(branch_b, n, [P, NT, H]) for n in ("beta", "nbeta", "gates", "gsum", "to_here", "to_end")]
            whole = sb(branch_b, "whole", [P, 2, NT, H])
            decays(nc, small, chunk, chunk_tab, a_log, dt_bias, *per_token, whole)
            delta_heads(nc, w_in, conv_w, gdn_norm_w, hT, ident, ones, chunk, *per_token, whole, zb_dram, og_dram)
    merge(nc, x, g_dram, og_dram, gates_dram, w_proj_a, w_proj_b, w_out, out)


_INS = ["x", "meta_tokens", "rel_bias", "norm_w", "w_in", "q_norm_w", "k_norm_w", "conv_w", "a_log", "dt_bias",
        "gdn_norm_w", "w_proj_a", "w_proj_b", "w_out"]


def kernel(**inputs):
    import concourse.bacc as bacc
    import numpy as np
    from concourse.bass_utils import run_bass_kernel_spmd

    nc = bacc.Bacc("TRN2", target_bir_lowering=False, num_devices=1)
    arrays = {name: np.ascontiguousarray(inputs[name]) for name in _INS}
    arrays["band_tab"], arrays["chunk_tab"] = band_table(), chunk_table()
    args = {name: nc.dram_tensor(f"in_{name}", a.shape, mybir.dt.from_np(a.dtype), kind="ExternalInput").ap()
            for name, a in arrays.items()}
    out = nc.dram_tensor("layer_out", (1, SEQ, D), F32, kind="ExternalOutput").ap()
    hybrid_layer(nc, **args, out=out)
    r = run_bass_kernel_spmd(nc, [{f"in_{name}": a for name, a in arrays.items()}], core_ids=[0])
    return r.results[0]["layer_out"]
```

```python
import math
from contextlib import ExitStack

import concourse.bass as bass
from concourse import mybir

P = 128
D = 1024
SEQ = 1024
META = 16
T = META + SEQ
PAD = P - META
TP = PAD + T
KD = D // P
NQT = SEQ // P
NT = TP // P
H = 8
DH = 64
WA = H * DH
DK = 128
CHUNK = 64
CONV = 4
TOPK = 256
EPS = 1e-6

OFF_QA, OFF_KA, OFF_VA, OFF_ZA = 0, WA, 2 * WA, 3 * WA
OFF_QI = 4 * WA
OFF_KI = OFF_QI + WA
OFF_WI = OFF_KI + DH
OFF_QB = OFF_WI + H
OFF_KB = OFF_QB + D
OFF_VB = OFF_KB + D
OFF_ZB = OFF_VB + D
OFF_BB = OFF_ZB + D
OFF_GA = OFF_BB + 2 * H
OFF_GB = OFF_GA + D
NSM = 3 * H

PICKED = -3.4028234663852886e38
AFTER = -3.0e38
HIDDEN = -1.0e30

ALU = mybir.AluOpType
ACT = mybir.ActivationFunctionType
AX = mybir.AxisListType
F32 = mybir.dt.float32
F32R = mybir.dt.float32r


def keys_of(t):
    return META + P * (t + 1)


def product(nc, out, ws, xs):
    for k, ((w_high, w_low), (x_high, x_low)) in enumerate(zip(ws, xs)):
        nc.tensor.matmul(out, w_high, x_high, start=(k == 0), stop=False)
        nc.tensor.matmul(out, w_high, x_low, start=False, stop=False)
        last = nc.tensor.matmul(out, w_low, x_high, start=False, stop=(k == len(ws) - 1))
    return last


def make_constants(nc, ident, ones):
    with nc.semaphore("ident_zero") as ident_zero, nc.Block() as block:
        @block.gpsimd
        def _(pool):
            nc.gpsimd.memset(ones[:], 1.0)
            nc.gpsimd.memset(ident[:], 0.0).then_inc(ident_zero, 1)
            pool.wait_ge(ident_zero, 1)
            nc.gpsimd.affine_select(out=ident[:], in_=ident[:], compare_op=ALU.not_equal, fill=1.0,
                                    base=0, pattern=[[-1, P]], channel_multiplier=1)


def normed_tokens(nc, x, meta_tokens, norm_w, h_high, h_low, ident):
    x_v = x.rearrange("b (t p) d -> (b t) p d", p=P)
    with ExitStack() as ctx:
        xt = ctx.enter_context(nc.sbuf_tensor("xt", [P, 2, D], F32))
        xn = ctx.enter_context(nc.sbuf_tensor("xn", [P, 2, D], F32))
        junk = ctx.enter_context(nc.sbuf_tensor("junk", [P, D], F32))
        h = ctx.enter_context(nc.sbuf_tensor("h", [P, 2, 4, P], F32))
        nwT = ctx.enter_context(nc.sbuf_tensor("nwT", [P, KD], F32))
        ssq = ctx.enter_context(nc.sbuf_tensor("ssq", [P, NT], F32))
        mean = ctx.enter_context(nc.sbuf_tensor("mean", [P, NT], F32))
        root = ctx.enter_context(nc.sbuf_tensor("root", [P, NT], F32))
        rstd = ctx.enter_context(nc.sbuf_tensor("rstd", [P, NT], F32))
        tr = [ctx.enter_context(nc.psum_tensor(f"tr{i}", [P, 4, P], F32)) for i in range(4)]
        sem = lambda n: ctx.enter_context(nc.semaphore(n))
        x_loaded = [sem("x_loaded0"), sem("x_loaded1")]
        nw_loaded, squared, mean_ready, root_ready, rstd_ready = (
            sem(n) for n in ("nw_loaded", "squared", "mean_ready", "root_ready", "rstd_ready"))
        scaled, turned, weighted, high_ready, low_ready = (
            sem(n) for n in ("scaled", "turned", "weighted", "high_ready", "low_ready"))
        block = ctx.enter_context(nc.Block())

        def rows(t):
            return META if t == 0 else P

        def place(m):
            t, g = m // 2, m % 2
            c = P * t if t else PAD
            return (slice(None), slice(4 * g, 4 * g + 4), slice(c, c + rows(t))), h[:, g, :, 0:rows(t)]

        @block.sync
        def _(sp):
            with nc.allow_non_contiguous_dma(reason="norm_w by partition"):
                sp.dma_start(nwT[:], norm_w.rearrange("l (k p) -> p (l k)", p=P)).then_inc(nw_loaded, 16)
            for t in range(NT):
                if t >= 2:
                    sp.wait_ge(scaled, t - 1)
                src = meta_tokens if t == 0 else x_v[t - 1]
                sp.dma_start(xt[:rows(t), t % 2], src).then_inc(x_loaded[t % 2], 16)
            sp.wait_ge(nw_loaded, 16)

        @block.gpsimd
        def _(pool):
            nc.gpsimd.memset(h_high[:, :, 0:PAD].bitcast(F32), 0.0)
            nc.gpsimd.memset(h_low[:, :, 0:PAD].bitcast(F32), 0.0)
            for m in range(2 * NT):
                at, src = place(m)
                pool.wait_ge(high_ready, m + 1)
                nc.gpsimd.tensor_tensor(h_low[at], src, h_high[at], ALU.subtract).then_inc(low_ready, 1)

        @block.scalar
        def _(act):
            for t in range(NT + 1):
                if t < NT:
                    n = rows(t)
                    act.wait_ge(x_loaded[t % 2], 16 * (t // 2 + 1))
                    if t:
                        act.wait_ge(squared, t)
                    nc.scalar.activation(junk[:n], xt[:n, t % 2], ACT.Square,
                                         accum_out=ssq[:n, t:t + 1]).then_inc(squared, 1)
                    act.wait_ge(mean_ready, t + 1)
                    nc.scalar.activation(root[:n, t:t + 1], mean[:n, t:t + 1], ACT.Sqrt).then_inc(root_ready, 1)
                if t >= 1:
                    for m in (2 * t - 2, 2 * t - 1):
                        at, src = place(m)
                        act.wait_ge(weighted, m + 1)
                        nc.scalar.activation(h_high[at], src, ACT.Copy).then_inc(high_ready, 1)

        @block.vector
        def _(dve):
            dve.wait_ge(nw_loaded, 16)
            for t in range(NT + 1):
                if t < NT:
                    n = rows(t)
                    dve.wait_ge(squared, t + 1)
                    nc.vector.tensor_scalar(mean[:n, t:t + 1], ssq[:n, t:t + 1], 1.0 / D, EPS,
                                            ALU.mult, ALU.add).then_inc(mean_ready, 1)
                    dve.wait_ge(root_ready, t + 1)
                    nc.vector.reciprocal(rstd[:n, t:t + 1], root[:n, t:t + 1]).then_inc(rstd_ready, 1)
                    dve.wait_ge(rstd_ready, t + 1)
                    if t >= 2:
                        dve.wait_ge(turned, 2 * (t - 1))
                    nc.vector.tensor_scalar(xn[:n, t % 2], xt[:n, t % 2], rstd[:n, t:t + 1], None,
                                            ALU.mult).then_inc(scaled, 1)
                if t >= 1:
                    n = rows(t - 1)
                    for g in range(2):
                        m = 2 * (t - 1) + g
                        dve.wait_ge(turned, m + 1)
                        if m >= 2:
                            dve.wait_ge(low_ready, m - 1)
                        nc.vector.tensor_tensor(
                            h[:, g, :, 0:n], tr[m % 4][:, :, 0:n],
                            nwT[:, 4 * g:4 * g + 4].unsqueeze(2).to_broadcast([P, 4, n]),
                            ALU.mult).then_inc(weighted, 1)

        @block.tensor
        def _(pe):
            for t in range(NT):
                n = rows(t)
                pe.wait_ge(scaled, t + 1)
                for g in range(2):
                    if 2 * t + g >= 4:
                        pe.wait_ge(weighted, 2 * t + g - 3)
                    for k in range(4):
                        f = (4 * g + k) * P
                        last = nc.tensor.transpose(tr[(2 * t + g) % 4][:, k, 0:n], xn[:n, t % 2, f:f + P],
                                                   ident[:n, :n])
                    last.then_inc(turned, 1)


def spans(w):
    step = -(-w // (16 * -(-w // 512))) * 16
    return [(a, min(w, a + step)) for a in range(0, w, step)]


def projections(nc, w_in, conv_w, h_high, h_low, small, score, qkv_dram, za_dram, zb_dram, gates_dram, conv_dram):
    w_v = w_in.rearrange("l (k p) n -> p (l k) n", p=P)
    BANKS, STAGES = 7, 3
    LOAD = 2 * P

    columns = lambda off, n: [[(off + c, LOAD, 0)] for c in range(0, n, LOAD)]
    loads = columns(OFF_QI, WA)
    small_load = len(loads)
    loads += [[(OFF_KI, DH, 0), (OFF_KI, DH, DH), (OFF_WI, H, P), (OFF_BB, 2 * H, P + H)]]
    rows = [("qa", OFF_QA, WA), ("ka", OFF_KA, WA), ("va", OFF_VA, WA), ("za", OFF_ZA, WA), ("zb", OFF_ZB, D)]
    conv_loads = columns(OFF_KB, D) + columns(OFF_QB, D) + columns(OFF_VB, D)
    other_loads = [("gate", n) for n in range(2 * D // LOAD)]
    other_loads += [(what, n) for what, _, w in rows for n in range(w // LOAD)]
    offset = {what: off for what, off, _ in rows}
    offset["gate"] = OFF_GA
    order = []
    for n, other in enumerate(other_loads):
        if n < len(conv_loads):
            order.append(("conv", n))
        order.append(other)
    load_of = {}
    for what, n in order:
        load_of[what, n] = len(loads)
        loads.append(conv_loads[n] if what == "conv" else [(offset[what] + LOAD * n, LOAD, 0)])
    width = [sum(w for _, w, _ in parts) for parts in loads]

    HALF = (SEQ - P) // 2
    fills = [("qi", f, HALF * c, HALF * c + HALF, f // 2) for f in range(4) for c in range(2)]
    fills += [("ki", 0, a, b, small_load) for a, b in spans(T)]
    n_split = len(fills)
    fills += [("small", 0, 0, NT * NSM, small_load)]
    fills += [("rel", (t, h), a, b, None) for t in range(1, NQT) for h in range(H) for a, b in spans(keys_of(t))]
    for what, n in order:
        load = load_of[what, n]
        if what == "conv":
            fills += [("conv", f, a, b, load) for f in (2 * n, 2 * n + 1) for a, b in spans(T)]
        elif what == "gate":
            fills += [("gate", f, 512 * c, 512 * c + 512, load) for f in (2 * n, 2 * n + 1) for c in range(2)]
        else:
            fills += [(what, t, LOAD * n, LOAD * n + LOAD, load) for t in range(0 if what in ("ka", "va") else 1, NT)]
    last_fill = [max(n for n, f in enumerate(fills) if f[4] == load) + 1 for load in range(len(loads))]
    first_rel = min(n for n, f in enumerate(fills) if f[0] == "rel")
    done_by = {}
    for n, f in enumerate(fills):
        done_by[f[0], f[1]] = n + 1
    swish_at = {done_by["conv", f] + 3: f for f in range(3 * H)}

    with ExitStack() as ctx:
        sb = lambda name, shape, kind=F32: ctx.enter_context(nc.sbuf_tensor(name, shape, kind))
        w_raw = sb("w_raw", [P, 2, KD, LOAD])
        w_high, w_low = sb("w_high", [P, 2, KD, LOAD], F32R), sb("w_low", [P, 2, KD, LOAD], F32R)
        qi_high, qi_low = sb("qi_high", [P, 4, SEQ - P], F32R), sb("qi_low", [P, 4, SEQ - P], F32R)
        ki_high, ki_low = sb("ki_high", [P, T], F32R), sb("ki_low", [P, T], F32R)
        raw, smooth, cw = sb("raw", [P, 2, CONV - 1 + T]), sb("smooth", [P, 2, T]), sb("cw", [P, CONV, 3 * H])
        rel = raw
        stage = sb("stage", [P, STAGES, 512])
        top8 = sb("top8", [P, 8])
        fence = sb("fence", [P, P])
        pj = [ctx.enter_context(nc.psum_tensor(f"pj{i}", [P, 512], F32)) for i in range(BANKS)]
        sem = lambda n: ctx.enter_context(nc.semaphore(n))
        w_loaded = [sem("w_loaded0"), sem("w_loaded1")]
        w_high_ready, w_low_ready = sem("w_high_ready"), sem("w_low_ready")
        filled, emptied, low_kept = sem("filled"), sem("emptied"), sem("low_kept")
        rel_used, fenced, step, picked, masked = (sem(n) for n in ("rel_used", "fenced", "step", "picked", "masked"))
        fence_ready = sem("fence_ready")
        cw_loaded, raw_start, conved, swished = (sem(n) for n in ("cw_loaded", "raw_start", "conved", "swished"))
        saved = [sem(f"saved{i}") for i in range(STAGES)]
        smooth_saved = [sem("smooth_saved0"), sem("smooth_saved1")]
        block = ctx.enter_context(nc.Block())

        @block.sync
        def _(sp):
            for n, parts in enumerate(loads):
                if n >= 2:
                    sp.wait_ge(w_low_ready, n - 1)
                for col, w, at in parts:
                    sp.dma_start(w_raw[:, n % 2, :, at:at + w],
                                 w_v[:, :, col:col + w]).then_inc(w_loaded[n % 2], 16)
                if n == 1:
                    with nc.allow_non_contiguous_dma(reason="per-feature weights on partitions"):
                        for k in range(CONV):
                            sp.dma_start(cw[:, k], conv_w[0, k].rearrange("(f p) -> p f", p=P)).then_inc(cw_loaded, 16)

        @block.gpsimd
        def _(pool):
            nc.gpsimd.memset(score[0][:], 0.0).then_inc(masked, 1)
            nc.gpsimd.memset(fence[:], -AFTER).then_inc(fence_ready, 1)
            pool.wait_ge(masked, 1)
            diagonal = score[0][:, META:META + P]
            nc.gpsimd.affine_select(out=diagonal, in_=diagonal, compare_op=ALU.is_ge, fill=HIDDEN, base=0,
                                    pattern=[[-1, P]], channel_multiplier=1).then_inc(masked, 1)
            pool.wait_ge(fence_ready, 1)
            nc.gpsimd.affine_select(out=fence[:], in_=fence[:], compare_op=ALU.is_ge, fill=AFTER, base=0,
                                    pattern=[[-1, P]], channel_multiplier=1).then_inc(fence_ready, 1)
            for n, parts in enumerate(loads):
                raw_w, high, low = (a[:, n % 2, :, 0:width[n]] for a in (w_raw, w_high, w_low))
                pool.wait_ge(w_loaded[n % 2], 16 * sum(len(x) for x in loads[n % 2:n + 1:2]))
                if n >= 2:
                    pool.wait_ge(filled, last_fill[n - 2])
                nc.gpsimd.tensor_copy(high, raw_w).then_inc(w_high_ready, 1)
                pool.wait_ge(w_high_ready, n + 1)
                nc.gpsimd.tensor_tensor(low, raw_w, high, ALU.subtract).then_inc(w_low_ready, 1)

        @block.tensor
        def _(pe):
            loaded = -1
            for n, (what, i, a, b, load) in enumerate(fills):
                bank = pj[n % BANKS]
                if n >= BANKS:
                    if n - BANKS < n_split:
                        pe.wait_ge(low_kept, n - BANKS + 1)
                    else:
                        pe.wait_ge(emptied, n - BANKS + 1)
                if load is not None and load > loaded:
                    loaded = load
                    pe.wait_ge(w_low_ready, load + 1)
                both = lambda high, low, *at: (high[at], low[at])
                every = slice(None)
                if what == "rel":
                    t, h = i
                    if n == first_rel:
                        pe.wait_ge(low_kept, n_split)
                    r, q = slice(DH * (h % 2), DH * (h % 2) + DH), slice(P * (t - 1), P * t)
                    last = product(nc, bank[:, 0:b - a], [both(qi_high, qi_low, r, h // 2, q)],
                                   [both(ki_high, ki_low, r, slice(a, b))])
                elif what == "small":
                    for t in range(NT):
                        last = product(nc, bank[:, NSM * t:NSM * t + NSM],
                                       [both(h_high, h_low, every, k, slice(P * t, P * t + P)) for k in range(KD)],
                                       [both(w_high, w_low, every, load % 2, k, slice(P, P + NSM)) for k in range(KD)])
                elif what in ("qi", "ki", "gate", "conv"):
                    f = 0 if what == "ki" else i % 2 * P
                    c = a + {"qi": 2 * P, "gate": P}.get(what, PAD)
                    last = product(nc, bank[:, 0:b - a],
                                   [both(w_high, w_low, every, load % 2, k, slice(f, f + P)) for k in range(KD)],
                                   [both(h_high, h_low, every, k, slice(c, c + b - a)) for k in range(KD)])
                else:
                    last = product(nc, bank[:, 0:LOAD],
                                   [both(h_high, h_low, every, k, slice(P * i, P * i + P)) for k in range(KD)],
                                   [both(w_high, w_low, every, load % 2, k, slice(0, LOAD)) for k in range(KD)])
                last.then_inc(filled, 1)

        @block.scalar
        def _(act):
            n_out = 0

            def swish(f):
                act.wait_ge(conved, CONV * (f + 1))
                nc.scalar.activation(smooth[:, f % 2], smooth[:, f % 2], ACT.Silu).then_inc(swished, 1)
                act.wait_ge(swished, f + 1)
                act.dma_start(conv_dram[f // H, f % H], smooth[:, f % 2]).then_inc(smooth_saved[f % 2], 16)

            for n, (what, i, a, b, _) in enumerate(fills):
                bank = pj[n % BANKS]
                func = ACT.Copy
                to_dram = None
                if what == "qi":
                    dst = qi_high[:, i, a:b]
                elif what == "ki":
                    dst = ki_high[:, a:b]
                elif what == "small":
                    dst = small[:].rearrange("p t c -> p (t c)")
                elif what == "rel":
                    t, h = i
                    unit = H * (t - 1) + h
                    func, dst = ACT.Relu, rel[:, unit % 2, a:b]
                    if a == 0 and unit >= 2:
                        act.wait_ge(rel_used, unit - 1)
                elif what == "conv":
                    dst = raw[:, i % 2, CONV - 1 + a:CONV - 1 + b]
                    if a == 0 and i == 0:
                        act.wait_ge(raw_start, 1)
                    if a == 0 and i >= 2:
                        act.wait_ge(conved, CONV * (i - 1))
                else:
                    func = {"gate": ACT.Sigmoid, "za": ACT.Silu, "zb": ACT.Silu}.get(what, ACT.Copy)
                    dst = stage[:, n_out % STAGES, 0:b - a]
                    kept = stage[PAD if i == 0 and what != "gate" else 0:P, n_out % STAGES, 0:b - a]
                    to_dram = {"gate": lambda: gates_dram[i, :, a:b], "za": lambda: za_dram[i - 1, :, a:b],
                               "zb": lambda: zb_dram[i - 1, :, a:b],
                               "qa": lambda: qkv_dram[0, i, :, a:b], "ka": lambda: qkv_dram[1, i, :, a:b],
                               "va": lambda: qkv_dram[2, i, :, a:b]}[what]()
                    if i == 0 and what != "gate":
                        to_dram = to_dram[PAD:P]
                    if n_out >= STAGES:
                        act.wait_ge(saved[n_out % STAGES], 16 * (n_out // STAGES))
                act.wait_ge(filled, n + 1)
                nc.scalar.activation(dst, bank[:, 0:b - a], func).then_inc(emptied, 1)
                if to_dram is not None:
                    act.wait_ge(emptied, n + 1)
                    act.dma_start(to_dram, kept).then_inc(saved[n_out % STAGES], 16)
                    n_out += 1
                if n in swish_at:
                    swish(swish_at[n])
            for s in range(STAGES):
                act.wait_ge(saved[s], 16 * len(range(s, n_out, STAGES)))
            for s in range(2):
                act.wait_ge(smooth_saved[s], 16 * 3 * H // 2)

        @block.vector
        def _(dve):
            diagonal = lambda t: score[t][:, keys_of(t) - P:keys_of(t)]
            for n, (what, i, a, b, _) in enumerate(fills[:n_split]):
                high, low = (qi_high[:, i, a:b], qi_low[:, i, a:b]) if what == "qi" else (ki_high[:, a:b], ki_low[:, a:b])
                dve.wait_ge(emptied, n + 1)
                nc.vector.tensor_tensor(low, pj[n % BANKS][:, 0:b - a], high, ALU.subtract).then_inc(low_kept, 1)
            dve.wait_ge(fence_ready, 2)
            for t in range(1, NQT):
                w = keys_of(t)
                for h in range(H):
                    unit = H * (t - 1) + h
                    weight = small[:, t + 1, h:h + 1]
                    dve.wait_ge(emptied, done_by["rel", (t, h)])
                    if h == 0:
                        nc.vector.tensor_scalar(score[t][:], rel[:, unit % 2, 0:w], weight, None,
                                                ALU.mult).then_inc(rel_used, 1)
                    else:
                        dve.wait_ge(rel_used, unit)
                        nc.vector.scalar_tensor_tensor(score[t][:], rel[:, unit % 2, 0:w], weight, score[t][:],
                                                       ALU.mult, ALU.add).then_inc(rel_used, 1)
                dve.wait_ge(rel_used, H * t)
                nc.vector.tensor_tensor(diagonal(t), diagonal(t), fence[:], ALU.min).then_inc(fenced, 1)
            nc.vector.memset(raw[:, :, 0:CONV - 1], 0.0).then_inc(raw_start, 1)
            dve.wait_ge(fenced, NQT - 1)
            nc.vector.tensor_scalar(fence[:], fence[:], 0.0, HIDDEN, ALU.is_lt, ALU.mult).then_inc(fenced, 1)

            def conv(f):
                dve.wait_ge(emptied, done_by["conv", f])
                if f >= 2:
                    dve.wait_ge(smooth_saved[f % 2], 16 * (f // 2))
                kind = {0: 1, 1: 0, 2: 2}[f // H]
                for k in range(CONV):
                    src, dst, w = raw[:, f % 2, k:k + T], smooth[:, f % 2], cw[:, k, H * kind + f % H:H * kind + f % H + 1]
                    if k == 0:
                        nc.vector.tensor_scalar(dst, src, w, None, ALU.mult).then_inc(conved, 1)
                    else:
                        dve.wait_ge(conved, CONV * f + k)
                        nc.vector.scalar_tensor_tensor(dst, src, w, dst, ALU.mult, ALU.add).then_inc(conved, 1)

            ROUNDS = TOPK // 8
            total = sum(keys_of(t) for t in range(1, NQT)) * ROUNDS
            dve.wait_ge(cw_loaded, 16 * CONV)
            steps, convs, searched = 0, 0, 0
            dve.wait_ge(fenced, NQT)
            for t in range(1, NQT):
                for r in range(ROUNDS):
                    if convs < 3 * H and searched * 3 * H >= total * convs:
                        conv(convs)
                        convs += 1
                    searched += keys_of(t)
                    if r:
                        dve.wait_ge(step, steps)
                    nc.vector.max(top8[:], score[t][:]).then_inc(step, 1)
                    steps += 1
                    dve.wait_ge(step, steps)
                    nc.vector.match_replace(score[t][:], top8[:], score[t][:], PICKED).then_inc(step, 1)
                    steps += 1
                dve.wait_ge(step, steps)
                nc.vector.tensor_scalar(score[t][:], score[t][:], PICKED, HIDDEN,
                                        ALU.is_gt, ALU.mult).then_inc(picked, 1)
                dve.wait_ge(picked, t)
                nc.vector.tensor_tensor(diagonal(t), diagonal(t), fence[:], ALU.min).then_inc(masked, 1)


def band_table():
    import math
    import numpy as np
    d = np.maximum(np.arange(2 * P - 1, -P, -1), 0)
    ratio = np.maximum(d, 16).astype(np.float32) / np.float32(16)
    large = 16 + (np.log(ratio) / np.float32(math.log(128 / 16)) * np.float32(16)).astype(np.int32)
    bucket = np.where(d < 16, d, np.minimum(large, 31))
    table = np.zeros((32, d.size), np.float32)
    table[bucket, np.arange(d.size)] += 1
    table[31] -= 1
    return table


def key_chunks(t):
    w = keys_of(t)
    near = max(0, w - 2 * P)
    return (spans(near) if near else []) + [(near, w)]


def attention_operands(nc, ident, qkv_dram, qT, kT, band, rel_bias, table, band_dram, q_norm_w, k_norm_w):
    NB = table.shape[1]
    with ExitStack() as early:
        esb = lambda name, shape: early.enter_context(nc.sbuf_tensor(name, shape, F32))
        esem = lambda n: early.enter_context(nc.semaphore(n))
        square = esb("square", [P, 2, WA])
        raw = esb("qk_raw", [P, 2 * NT - 1, WA])
        total, logs, rstd = (esb(n, [P, 2 * NT - 1, H]) for n in ("qk_total", "qk_log", "qk_rstd"))
        normed = esb("normed", [P, 2, WA])
        nw, eps = esb("nw", [P, 2]), esb("eps", [P, 1])
        bias_sb, table_sb, row_sb = esb("bias_sb", [32, H]), esb("table_sb", [32, NB]), esb("row_sb", [H, NB])
        flip, band_rev = esb("flip", [P, P]), esb("band_rev", [P, H, 2 * P])
        tr = [early.enter_context(nc.psum_tensor(f"tn{i}", [P, 4, P], F32)) for i in range(2)]
        bp = [early.enter_context(nc.psum_tensor(f"bp{i}", [P, 512], F32)) for i in range(2)]
        loaded, nw_ready, row_ready, row_saved, rev_loaded, row_made, made = (
            esem(n) for n in ("loaded", "nw_ready", "row_ready", "row_saved", "rev_loaded", "row_made", "made"))
        squared, added, logged, rooted, scaled, turned, kept, band_filled, band_kept = (
            esem(n) for n in ("a_squared", "a_added", "a_logged", "a_rooted", "a_scaled", "a_turned", "a_kept",
                              "band_filled", "band_kept"))
        raw_in = [esem(f"raw_in{i}") for i in range(3)]
        units = [(1, kT, i, 1) for i in range(NT)] + [(0, qT, i, 0) for i in range(1, NT)]
        rows = lambda i: META if i == 0 else P
        block = early.enter_context(nc.Block())

        @block.sync
        def _(sp):
            sp.dma_start(bias_sb[:], rel_bias).then_inc(loaded, 16)
            sp.dma_start(table_sb[:], table).then_inc(loaded, 16)
            rest = qkv_dram[:, 1:].rearrange("j t p c -> j p t c")
            sp.dma_start(raw[0:META, 0], qkv_dram[1, 0, PAD:P]).then_inc(raw_in[0], 16)
            sp.dma_start(raw[:, 1:NT], rest[1]).then_inc(raw_in[1], 16)
            sp.dma_start(raw[:, NT:], rest[0]).then_inc(raw_in[2], 16)
            with nc.allow_non_contiguous_dma(reason="one weight per partition"):
                for j, w in enumerate((q_norm_w, k_norm_w)):
                    for half in range(2):
                        sp.dma_start(nw[DH * half:DH * half + DH, j:j + 1],
                                     w.rearrange("l d -> d l")).then_inc(loaded, 16)
            sp.wait_ge(row_ready, 1)
            sp.dma_start(band_dram, row_sb[:]).then_inc(row_saved, 16)
            sp.wait_ge(row_saved, 16)
            for h in range(H):
                src = bass.AP(band_dram.tensor, h * NB, [[1, P], [1, 2 * P]])
                sp.dma_start(band_rev[:, h], src).then_inc(rev_loaded, 16)

        @block.gpsimd
        def _(pool):
            nc.gpsimd.memset(total[:, 0], 1.0).then_inc(made, 1)
            nc.gpsimd.memset(eps[:], EPS).then_inc(made, 1)
            nc.gpsimd.memset(flip[:], 0.0).then_inc(made, 1)
            pool.wait_ge(made, 3)
            nc.gpsimd.affine_select(out=flip[:], in_=flip[:], compare_op=ALU.not_equal, fill=1.0,
                                    base=1 - P, pattern=[[1, P]], channel_multiplier=1).then_inc(made, 1)

        @block.scalar
        def _(act):
            for n, (_, _, i, _) in enumerate(units):
                m = rows(i)
                if n in (0, 1, NT):
                    act.wait_ge(raw_in[0 if n == 0 else 1 if n == 1 else 2], 16)
                if n >= 2:
                    act.wait_ge(added, n - 1)
                nc.scalar.activation(square[:m, n % 2], raw[:m, n], ACT.Square).then_inc(squared, 1)
            act.wait_ge(made, 4)
            act.wait_ge(added, len(units))
            nc.scalar.activation(logs[:], total[:, 0:len(units)], ACT.Ln, scale=1.0 / DH,
                                 bias=eps[:, 0:1]).then_inc(logged, 1)
            act.wait_ge(logged, 1)
            nc.scalar.activation(rstd[:], logs[:], ACT.Exp, scale=-0.5).then_inc(rooted, 1)

        @block.vector
        def _(dve):
            dve.wait_ge(loaded, 96)
            nc.vector.tensor_scalar(nw[:, 0:1], nw[:, 0:1], DH ** -0.5, None, ALU.mult).then_inc(nw_ready, 1)
            dve.wait_ge(row_made, 1)
            nc.vector.tensor_copy(row_sb[:], bp[0][0:H, 0:NB]).then_inc(row_ready, 1)
            dve.wait_ge(made, 1)
            for n, (_, _, i, _) in enumerate(units):
                m = rows(i)
                dve.wait_ge(squared, n + 1)
                nc.vector.tensor_reduce(total[:m, n], square[:m, n % 2].rearrange("p (h d) -> p h d", d=DH),
                                        AX.X, ALU.add).then_inc(added, 1)
            dve.wait_ge(rooted, 1)
            for n in range(len(units) + 1):
                if n < len(units):
                    _, _, i, _ = units[n]
                    m = rows(i)
                    if n >= 2:
                        dve.wait_ge(turned, n - 1)
                    nc.vector.tensor_tensor(normed[:m, n % 2].rearrange("p (h d) -> p h d", d=DH),
                                            raw[:m, n].rearrange("p (h d) -> p h d", d=DH),
                                            rstd[:m, n].unsqueeze(2).to_broadcast([m, H, DH]),
                                            ALU.mult).then_inc(scaled, 1)
                if n >= 1:
                    _, dst, i, j = units[n - 1]
                    m = rows(i)
                    c = 0 if i == 0 else P * (i - 1) + (META if j == 1 else 0)
                    dve.wait_ge(turned, n)
                    if n == 1:
                        dve.wait_ge(nw_ready, 1)
                    nc.vector.tensor_scalar(dst[:, :, c:c + m], tr[(n - 1) % 2][:, :, 0:m], nw[:, j:j + 1], None,
                                            ALU.mult).then_inc(kept, 1)
            for c in range(4):
                dve.wait_ge(band_filled, c + 1)
                nc.vector.tensor_copy(band[:, 2 * c:2 * c + 2].rearrange("p h j -> p (h j)"),
                                      bp[c % 2][:, :]).then_inc(band_kept, 1)

        @block.tensor
        def _(pe):
            pe.wait_ge(loaded, 96)
            nc.tensor.matmul(bp[0][0:H, 0:NB], bias_sb[:], table_sb[:], start=True, stop=True).then_inc(row_made, 1)
            for n, (_, _, i, _) in enumerate(units):
                m = rows(i)
                pe.wait_ge(scaled, n + 1)
                if n >= 2:
                    pe.wait_ge(kept, n - 1)
                for f in range(4):
                    last = nc.tensor.transpose(tr[n % 2][:, f, 0:m], normed[:m, n % 2, P * f:P * f + P],
                                               ident[:m, :m])
                last.then_inc(turned, 1)
            pe.wait_ge(rev_loaded, 16 * H)
            pe.wait_ge(made, 4)
            pe.wait_ge(row_ready, 1)
            for c in range(4):
                if c >= 2:
                    pe.wait_ge(band_kept, c - 1)
                nc.tensor.matmul(bp[c % 2][:, :], flip[:], band_rev[:, 2 * c:2 * c + 2].rearrange("p h j -> p (h j)"),
                                 start=True, stop=True).then_inc(band_filled, 1)


def attention(nc, ident, score, qT, kT, band, qkv_dram, za_dram, g_dram):
    with ExitStack() as ctx:
        sb = lambda name, shape: ctx.enter_context(nc.sbuf_tensor(name, shape, F32))
        sem = lambda n: ctx.enter_context(nc.semaphore(n))
        hidden = sb("hidden", [P, 4, 2 * P])
        logit, prob, probT = sb("logit", [P, 2, T]), sb("prob", [P, 2, T]), sb("probT", [P, 2, NT, P])
        best, worst, mass, inv = sb("best", [P, 4 * H * NQT]), sb("worst", [P, H * NQT]), sb("mass", [P, H * NQT]), sb("inv", [P, H * NQT])
        gate, mixed, gated = sb("gate", [P, 2, WA]), sb("mixed", [P, 2, WA]), sb("gated", [P, 2, WA])
        LG, PT = 4, 2
        lg = [ctx.enter_context(nc.psum_tensor(f"lg{i}", [P, 512], F32)) for i in range(LG)]
        pt = [ctx.enter_context(nc.psum_tensor(f"pt{i}", [P, 4, P], F32)) for i in range(PT)]
        po = ctx.enter_context(nc.psum_tensor("po", [P, WA], F32))
        pg = ctx.enter_context(nc.psum_tensor("pg", [P, 4, P], F32))
        (near_ready, logit_made, logit_read, negated, exped, turned, kept, mixed_up, divided, out_ready, gated_up,
         g_turned, g_kept) = (sem(n) for n in (
            "near_ready", "logit_made", "logit_read", "negated", "exped", "p_turned", "p_kept", "mixed_up", "divided",
            "out_ready", "gated_up", "g_turned", "g_kept"))
        gate_loaded = [sem("gate_loaded0"), sem("gate_loaded1")]
        gT, g_saved = sb("gT", [P, 4, SEQ]), sem("g_saved")
        va, va_loaded = sb("va", [P, NT, WA]), sem("va_loaded")
        units = [(t, h) for t in range(NQT) for h in range(H)]
        chunks_to = [0]
        groups_to = [0]
        for t, h in units:
            chunks_to.append(chunks_to[-1] + len(key_chunks(t)))
            groups_to.append(groups_to[-1] + -(-(t + 2) // 4))
        key_rows = lambda b: META if b == 0 else P
        key_col = lambda b: 0 if b == 0 else META + P * (b - 1)
        block = ctx.enter_context(nc.Block())

        @block.sync
        def _(sp):
            sp.dma_start(va[0:META, 0], qkv_dram[2, 0, PAD:P]).then_inc(va_loaded, 16)
            sp.dma_start(va[:, 1:], qkv_dram[2, 1:].rearrange("t p c -> p t c")).then_inc(va_loaded, 16)
            for t in range(NQT):
                if t >= 2:
                    sp.wait_ge(gated_up, t - 1)
                sp.dma_start(gate[:, t % 2], za_dram[t]).then_inc(gate_loaded[t % 2], 16)
            sp.wait_ge(g_kept, NQT)
            sp.dma_start(g_dram.rearrange("k p t -> p k t"), gT[:]).then_inc(g_saved, 16)
            sp.wait_ge(g_saved, 16)

        @block.gpsimd
        def _(pool):
            for n, (t, h) in enumerate(units):
                a, b = key_chunks(t)[-1]
                if n >= 4:
                    pool.wait_ge(logit_read, chunks_to[n - 3])
                nc.gpsimd.tensor_tensor(hidden[:, n % 4, 0:b - a], score[t][:, a:b], band[:, h, 2 * P - (b - a):2 * P],
                                        ALU.add).then_inc(near_ready, 1)

        @block.tensor
        def _(pe):
            def logits(n):
                t, h = units[n]
                r = slice(DH * (h % 2), DH * (h % 2) + DH)
                for c, (a, b) in enumerate(key_chunks(t)):
                    m = chunks_to[n] + c
                    if m >= LG:
                        pe.wait_ge(logit_read, m - LG + 1)
                    nc.tensor.matmul(lg[m % LG][:, 0:b - a], qT[r, h // 2, P * t:P * t + P], kT[r, h // 2, a:b],
                                     start=True, stop=True).then_inc(logit_made, 1)

            def turn(n):
                t, h = units[n]
                pe.wait_ge(exped, n + 1)
                for g in range(groups_to[n + 1] - groups_to[n]):
                    m = groups_to[n] + g
                    if m >= PT:
                        pe.wait_ge(kept, m - PT + 1)
                    for b in range(4 * g, min(4 * g + 4, t + 2)):
                        k, c = key_rows(b), key_col(b)
                        last = nc.tensor.transpose(pt[m % PT][0:k, b - 4 * g, :], prob[:, n % 2, c:c + k], ident[:])
                    last.then_inc(turned, 1)

            def mix(n):
                t, h = units[n]
                if n == 0:
                    pe.wait_ge(va_loaded, 32)
                pe.wait_ge(kept, groups_to[n + 1])
                if h == 0 and t >= 1:
                    pe.wait_ge(divided, t)
                for b in range(t + 2):
                    k = key_rows(b)
                    last = nc.tensor.matmul(po[:, DH * h:DH * h + DH], probT[0:k, n % 2, b, :],
                                            va[0:k, b, DH * h:DH * h + DH], start=(b == 0), stop=(b == t + 1))
                last.then_inc(mixed_up, 1)

            def turn_gated(t):
                pe.wait_ge(gated_up, t + 1)
                if t >= 1:
                    pe.wait_ge(g_kept, t)
                for f in range(4):
                    last = nc.tensor.transpose(pg[:, f, :], gated[:, t % 2, P * f:P * f + P], ident[:])
                last.then_inc(g_turned, 1)

            for n in range(len(units) + 3):
                if n < len(units):
                    logits(n)
                if 1 <= n <= len(units):
                    turn(n - 1)
                if 2 <= n <= len(units) + 1:
                    mix(n - 2)
                if n >= 12 and (n - 12) % H == 0 and (n - 12) // H < NQT - 1:
                    turn_gated((n - 12) // H)
            turn_gated(NQT - 1)

        @block.vector
        def _(dve):
            def masked_max(n):
                t, h = units[n]
                chunks = key_chunks(t)
                if n >= 2:
                    dve.wait_ge(exped, n - 1)
                for c, (a, b) in enumerate(chunks):
                    m = chunks_to[n] + c
                    near = c == len(chunks) - 1
                    dve.wait_ge(logit_made, m + 1)
                    if near:
                        dve.wait_ge(near_ready, n + 1)
                    if c:
                        dve.wait_ge(logit_read, m)
                    nc.vector.tensor_tensor_reduce(
                        out=logit[:, n % 2, a:b], in0=lg[m % LG][:, 0:b - a],
                        in1=hidden[:, n % 4, 0:b - a] if near else score[t][:, a:b],
                        scale=1.0, scalar=best[:, 4 * n + c - 1:4 * n + c] if c else -3.0e38, op0=ALU.add, op1=ALU.max,
                        accum_out=best[:, 4 * n + c:4 * n + c + 1]).then_inc(logit_read, 1)
                dve.wait_ge(logit_read, chunks_to[n + 1])
                c = 4 * n + len(chunks) - 1
                nc.vector.tensor_scalar(worst[:, n:n + 1], best[:, c:c + 1], -1.0, None, ALU.mult).then_inc(negated, 1)

            def finish(t):
                dve.wait_ge(exped, H * t + H)
                nc.vector.reciprocal(inv[:, H * t:H * t + H], mass[:, H * t:H * t + H]).then_inc(out_ready, 1)
                dve.wait_ge(out_ready, t + 1)
                dve.wait_ge(mixed_up, H * t + H)
                nc.vector.tensor_tensor(mixed[:, t % 2].rearrange("p (h d) -> p h d", d=DH),
                                        po[:].rearrange("p (h d) -> p h d", d=DH),
                                        inv[:, H * t:H * t + H].unsqueeze(2).to_broadcast([P, H, DH]),
                                        ALU.mult).then_inc(divided, 1)
                dve.wait_ge(divided, t + 1)
                dve.wait_ge(gate_loaded[t % 2], 16 * (t // 2 + 1))
                if t >= 2:
                    dve.wait_ge(g_turned, t - 1)
                nc.vector.tensor_tensor(gated[:, t % 2], mixed[:, t % 2], gate[:, t % 2],
                                        ALU.mult).then_inc(gated_up, 1)

            for n in range(len(units)):
                masked_max(n)
                if n >= 10 and (n - 10) % H == 0:
                    finish((n - 10) // H)
            finish(NQT - 1)

        @block.scalar
        def _(act):
            def exp(n):
                t, h = units[n]
                w = keys_of(t)
                act.wait_ge(negated, n + 1)
                if n >= 2:
                    act.wait_ge(turned, groups_to[n - 1])
                nc.scalar.activation(prob[:, n % 2, 0:w], logit[:, n % 2, 0:w], ACT.Exp, bias=worst[:, n:n + 1],
                                     accum_out=mass[:, n:n + 1]).then_inc(exped, 1)

            def keep(n):
                t, h = units[n]
                if n >= 2:
                    act.wait_ge(mixed_up, n - 1)
                for g in range(groups_to[n + 1] - groups_to[n]):
                    m = groups_to[n] + g
                    act.wait_ge(turned, m + 1)
                    lo, hi = 4 * g, min(4 * g + 4, t + 2)
                    if g == 0:
                        nc.scalar.activation(probT[0:META, n % 2, 0, :], pt[m % PT][0:META, 0, :], ACT.Copy)
                        lo = 1
                    nc.scalar.activation(probT[:, n % 2, lo:hi, :], pt[m % PT][:, lo - 4 * g:hi - 4 * g, :],
                                         ACT.Copy).then_inc(kept, 1)

            def keep_gated(t):
                act.wait_ge(g_turned, t + 1)
                nc.scalar.activation(gT[:, :, P * t:P * t + P], pg[:], ACT.Copy).then_inc(g_kept, 1)

            for n in range(len(units) + 1):
                if n < len(units):
                    exp(n)
                if n >= 1:
                    keep(n - 1)
                if n >= 13 and (n - 13) % H == 0 and (n - 13) // H < NQT - 1:
                    keep_gated((n - 13) // H)
            keep_gated(NQT - 1)


def chunk_table():
    import numpy as np
    i, j = np.arange(P)[:, None], np.arange(P)[None, :]
    same = i // CHUNK == j // CHUNK
    parts = [same & (i <= j), same, (i < CHUNK) & (j >= 0), (i >= CHUNK) & (j >= 0)]
    table = [p.astype(np.float32) for p in parts]
    for l in range(6):
        table.append(np.eye(P, dtype=np.float32) - ((i >> l) % 2 == 1) * ((i >> l) - 1 == j >> l))
    return np.ascontiguousarray(np.stack(table, 1)).astype(np.float32)


def decays(nc, small, chunk, chunk_tab, a_log, dt_bias, beta, nbeta, gates, gsum, to_here, to_end, whole):
    with ExitStack() as ctx:
        sb = lambda name, shape: ctx.enter_context(nc.sbuf_tensor(name, shape, F32))
        sem = lambda n: ctx.enter_context(nc.semaphore(n))
        alog, dtb, nega = sb("alog", [P, H]), sb("dtb", [P, H]), sb("nega", [P, H])
        z, mag, e, ln, pos = (sb(n, [P, NT, H]) for n in ("z", "mag", "e", "ln", "pos"))
        sums = ctx.enter_context(nc.psum_tensor("sums", [P, 4, NT * H], F32))
        vloaded, cloaded, d, a, p = sem("vloaded"), sem("cloaded"), sem("d_dve"), sem("d_act"), sem("d_pe")
        block = ctx.enter_context(nc.Block())

        @block.sync
        def _(sp):
            sp.dma_start(alog[:], a_log.to_broadcast([P, H])).then_inc(vloaded, 16)
            sp.dma_start(dtb[:], dt_bias.to_broadcast([P, H])).then_inc(vloaded, 16)
            sp.dma_start(chunk[:], chunk_tab).then_inc(cloaded, 16)

        @block.scalar
        def _(act):
            nc.scalar.activation(beta[:], small[:, :, H:2 * H], ACT.Sigmoid).then_inc(a, 1)
            act.wait_ge(vloaded, 32)
            nc.scalar.activation(nega[:], alog[:], ACT.Exp).then_inc(a, 1)
            act.wait_ge(d, 1)
            nc.scalar.activation(mag[:], z[:], ACT.Abs).then_inc(a, 1)
            act.wait_ge(a, 3)
            nc.scalar.activation(e[:], mag[:], ACT.Exp, scale=-1.0).then_inc(a, 1)
            act.wait_ge(d, 2)
            nc.scalar.activation(ln[:], mag[:], ACT.Ln).then_inc(a, 1)
            act.wait_ge(d, 8)
            nc.scalar.activation(to_here[:], gsum[:], ACT.Exp).then_inc(a, 1)
            nc.scalar.activation(to_end[:], z[:], ACT.Exp).then_inc(a, 1)
            nc.scalar.activation(whole[:], sums[:, 2:4].rearrange("p c (t h) -> p c t h", h=H), ACT.Exp).then_inc(a, 1)

        @block.vector
        def _(dve):
            dve.wait_ge(vloaded, 32)
            nc.vector.tensor_tensor(z[:], small[:, :, 2 * H:3 * H],
                                    dtb[:].unsqueeze(1).to_broadcast([P, NT, H]), ALU.add).then_inc(d, 1)
            dve.wait_ge(a, 4)
            nc.vector.tensor_scalar(mag[:], e[:], 1.0, None, ALU.add).then_inc(d, 1)
            nc.vector.tensor_scalar(pos[:], z[:], 0.0, None, ALU.max).then_inc(d, 1)
            nc.vector.tensor_scalar(nbeta[:], beta[:], -1.0, None, ALU.mult).then_inc(d, 1)
            dve.wait_ge(a, 5)
            dve.wait_ge(d, 3)
            nc.vector.tensor_tensor(e[:], ln[:], pos[:], ALU.add).then_inc(d, 1)
            dve.wait_ge(d, 5)
            nc.vector.scalar_tensor_tensor(gates[:], e[:], -1.0, nega[:].unsqueeze(1).to_broadcast([P, NT, H]),
                                           ALU.mult, ALU.mult).then_inc(d, 1)
            dve.wait_ge(p, 1)
            nc.vector.tensor_copy(gsum[:], sums[:, 0].rearrange("p (t h) -> p t h", h=H)).then_inc(d, 1)
            dve.wait_ge(d, 7)
            nc.vector.tensor_tensor(z[:], sums[:, 1].rearrange("p (t h) -> p t h", h=H), gsum[:],
                                    ALU.subtract).then_inc(d, 1)

        @block.tensor
        def _(pe):
            pe.wait_ge(cloaded, 16)
            pe.wait_ge(d, 6)
            for c in range(4):
                last = nc.tensor.matmul(sums[:, c], chunk[:, c], gates[:].rearrange("p t h -> p (t h)"),
                                        start=True, stop=True)
            last.then_inc(p, 1)


GROUPS, GT = 3, 3
GW = GT * P
LEVELS = 6
CHUNKS = 2 * NT
STEPS = CHUNKS - 1


def delta_plan():
    def prepare(h):
        fills = lambda *whats: [("fill", (x, h, 0, g)) for x in whats for g in range(GROUPS)]
        items = [("squares", h)] + fills("grow", "sum_k", "sum_q") + [("scale", h)] + fills("vt", "kt", "kk")
        for l in range(LEVELS):
            items += [("fill", ("Q", h, l, g)) for g in range(GROUPS)]
            if l == 0:
                items += fills("at")
            items += [("fill", ("W", h, l, g)) for g in range(GROUPS)]
        return items + fills("wT", "u")

    def walk(h):
        return [(half, h, n) for n in range(STEPS) for half in ("state", "update")]

    plan = prepare(0)
    for h in range(H):
        between = prepare(h + 1) if h + 1 < H else []
        if h >= 1:
            between[len(between) // 4:len(between) // 4] = [("fill", ("post", h - 1, 0, g)) for g in range(2)]
            between[:0] = [("norm", h - 1)]
        steps = walk(h)
        at = 0
        for n, item in enumerate(steps):
            plan.append(item)
            upto = len(between) * (n + 1) // len(steps)
            plan += between[at:upto]
            at = upto
    return plan + [("norm", H - 1)] + [("fill", ("post", H - 1, 0, g)) for g in range(2)]


def delta_heads(nc, conv_dram, gdn_norm_w, ident, ones, chunk, beta, nbeta, gates, gsum, to_here, to_end,
                whole, zb_dram, og_dram):
    PK, PQ, PV = range(3)
    with ExitStack() as ctx:
        sb = lambda name, shape: ctx.enter_context(nc.sbuf_tensor(name, shape, F32))
        sem = lambda n: ctx.enter_context(nc.semaphore(n))
        ys, sq = sb("ys", [P, 3, TP]), sb("sq", [P, 2, TP])
        rk, rq = sb("rk", [P, TP]), sb("rq", [P, TP])
        grow, LA, LB = sb("grow", [P, TP]), sb("LA", [P, TP]), sb("LB", [P, TP])
        tiled = lambda name: sb(name, [P, NT, P])
        kt, ke, vt, U, W, X, R = (tiled(n) for n in ("kt", "ke", "vt", "U", "W", "X", "R"))
        twice = lambda name: [tiled(name + "0"), tiled(name + "1")]
        kd, at, u, o = (twice(n) for n in ("kd", "at", "u", "o"))
        wq = [sb(f"wq{i}", [P, NT, 4, CHUNK]) for i in range(2)]
        vnew, S = sb("vnew", [P, 2, P]), sb("S", [P, 2, P])
        zb, osq = sb("zb_head", [P, NQT, P]), sb("osq", [P, NQT, P])
        ovar, oln, orstd = sb("ovar", [P, NQT]), sb("oln", [P, NQT]), sb("orstd", [P, NQT])
        og = sb("og_head", [P, SEQ])
        gw, consts = sb("gw", [P, 1]), sb("consts", [P, 3])
        so = [ctx.enter_context(nc.psum_tensor(f"so{i}", [P, P], F32)) for i in range(2)]
        skv = ctx.enter_context(nc.psum_tensor("skv", [P, P], F32))
        WB = 5
        wk = [ctx.enter_context(nc.psum_tensor(f"wk{i}", [P, 512], F32)) for i in range(WB)]

        plan = delta_plan()
        fills = [item[1] for item in plan if item[0] == "fill"]
        by_dve = ("kk", "at", "Q", "u")
        place, read_no, counts = {}, {}, [0, 0]
        for n, key in enumerate(fills):
            counts[key[0] in by_dve] += 1
            place[key], read_no[key] = n, counts[key[0] in by_dve]

        (worked, read_act, read_dve) = (sem(n) for n in ("worked", "read_act", "read_dve"))
        (const_made, zeroed, gw_loaded, y_loaded, squared, rooted, normed, ldiff, growexp, lexp, lmasked, lbeta, udiag,
         kscaled, qdec, x_turned) = (sem(n) for n in (
            "const_made", "zeroed", "gw_loaded", "y_loaded", "squared", "rooted", "normed", "ldiff", "growexp",
            "lexp", "lmasked", "lbeta", "udiag", "kscaled", "qdec", "x_turned"))
        (s_made, v_new, kv_made, o_made, s_kept, o_kept, o_squared, o_summed, o_ln, o_root, o_scaled, z_loaded,
         og_saved) = (sem(n) for n in (
            "s_made", "v_new", "kv_made", "o_made", "s_kept", "o_kept", "o_squared", "o_summed", "o_ln", "o_root",
            "o_scaled", "z_loaded", "og_saved"))
        block = ctx.enter_context(nc.Block())

        def read(eng, key):
            eng.wait_ge(read_dve if key[0] in by_dve else read_act, read_no[key])

        def bank_of(key):
            return wk[place[key] % WB]

        def by_tile(ap):
            return ap.rearrange("p (t i) -> p t i", i=P)

        def group(x, g):
            return x[:, GT * g:GT * g + GT]

        def chunk_at(n):
            t, half = divmod(n + 1, 2)
            return t, half, slice(CHUNK * half, CHUNK * half + CHUNK), slice(CHUNK * (1 - half), CHUNK * (2 - half))

        x_no = lambda h, l, g: GROUPS * ((LEVELS - 2) * h + l - 1) + g + 1

        @block.sync
        def _(sp):
            with nc.allow_non_contiguous_dma(reason="one weight per partition"):
                sp.dma_start(gw[:], gdn_norm_w.rearrange("l d -> d l")).then_inc(gw_loaded, 16)
            for h in range(H):
                if h >= 1:
                    read(sp, ("at", h - 1, 0, GROUPS - 1))
                    read(sp, ("kk", h - 1, 0, GROUPS - 1))
                    read(sp, ("kt", h - 1, 0, GROUPS - 1))
                    sp.wait_ge(qdec, h)
                sp.dma_start(ys[:, :, PAD:TP], conv_dram[:, h].rearrange("j p t -> p j t")).then_inc(y_loaded, 16)
                if h >= 1:
                    sp.wait_ge(o_scaled, 2 * h)
                for half in range(2):
                    src = zb_dram[:, CHUNK * (1 - half):CHUNK * (2 - half), P * h:P * h + P].rearrange("t p c -> p t c")
                    sp.dma_start(zb[CHUNK * half:CHUNK * half + CHUNK], src).then_inc(z_loaded, 16)

        @block.gpsimd
        def _(pool):
            nc.gpsimd.memset(consts[:, 0:1], EPS)
            nc.gpsimd.memset(consts[:, 1:2], 0.0)
            nc.gpsimd.memset(consts[:, 2:3], -0.5 * math.log(DK)).then_inc(const_made, 1)
            nc.gpsimd.memset(ys[:, :, 0:PAD], 0.0).then_inc(zeroed, 1)
            tri = chunk[:, 0:1].to_broadcast([P, NT, P])
            for h in range(H):
                pool.wait_ge(lexp, h + 1)
                nc.gpsimd.tensor_tensor(by_tile(LA[:]), by_tile(LA[:]), tri, ALU.mult).then_inc(lmasked, 1)
                pool.wait_ge(lmasked, h + 1)
                nc.gpsimd.tensor_tensor(by_tile(LB[:]), by_tile(LA[:]), beta[:, :, h:h + 1].to_broadcast([P, NT, P]),
                                        ALU.mult).then_inc(lbeta, 1)
                for g in range(GROUPS):
                    read(pool, ("kk", h, 0, g))
                    nc.gpsimd.affine_select(out=group(U, g), in_=group(U, g), compare_op=ALU.not_equal, fill=1.0,
                                            base=0, pattern=[[0, GT], [-1, P]], channel_multiplier=1).then_inc(udiag, 1)
                read(pool, ("kt", h, 0, GROUPS - 1))
                if h >= 2:
                    pool.wait_ge(kv_made, STEPS * (h - 1))
                if h >= 1:
                    read(pool, ("wT", h - 1, 0, GROUPS - 1))
                for dst, by in ((ke, to_here), (kd[h % 2], to_end)):
                    nc.gpsimd.tensor_tensor(dst[:], kt[:], by[:, :, h:h + 1].to_broadcast([P, NT, P]),
                                            ALU.mult).then_inc(kscaled, 1)

        @block.tensor
        def _(pe):
            def fill(key):
                what, h, l, g = key
                n = place[key]
                bank, out = bank_of(key), bank_of(key)[:, 0:GW]
                tiles = list(enumerate(range(GT * g, GT * g + GT)))
                if n >= WB:
                    read(pe, fills[n - WB])
                if what == "grow":
                    for i, t in tiles:
                        last = nc.tensor.matmul(out[:, P * i:P * i + P], gates[:, t, h:h + 1].to_broadcast([P, P]),
                                                chunk[:, 0], start=True, stop=True)
                elif what in ("sum_k", "sum_q"):
                    j = int(what == "sum_q")
                    pe.wait_ge(squared, 2 * h + 1 + j)
                    last = nc.tensor.matmul(out, ones[:], sq[:, j, GW * g:GW * g + GW], start=True, stop=True)
                elif what == "post":
                    pe.wait_ge(o_scaled, 2 * h + 2)
                    for i in range(4):
                        last = nc.tensor.transpose(bank[:, P * i:P * i + P], o[h % 2][:, 1 + 4 * g + i], ident[:])
                elif what in ("kk", "at"):
                    pe.wait_ge(normed, 2 * h + 1 + (what == "at"))
                    for i, t in tiles:
                        last = nc.tensor.matmul(out[:, P * i:P * i + P], ys[:, PK, P * t:P * t + P],
                                                ys[:, PK if what == "kk" else PQ, P * t:P * t + P], start=True, stop=True)
                elif what in ("kt", "vt"):
                    if what == "kt":
                        pe.wait_ge(normed, 2 * h + 1)
                    for i, t in tiles:
                        last = nc.tensor.transpose(out[:, P * i:P * i + P],
                                                   ys[:, PK if what == "kt" else PV, P * t:P * t + P], ident[:])
                elif what == "Q":
                    if l == 0:
                        pe.wait_ge(udiag, GROUPS * h + g + 1)
                    elif l == 1:
                        read(pe, ("Q", h, 0, g))
                    else:
                        pe.wait_ge(x_turned, x_no(h, l - 1, g))
                    for i, t in tiles:
                        x = ident[:] if l == 0 else R[:, t] if l == 1 else X[:, t]
                        last = nc.tensor.matmul(out[:, P * i:P * i + P], U[:, t], x, start=True, stop=True)
                elif what == "W":
                    read(pe, ("Q", h, l, g))
                    if l:
                        read(pe, ("W", h, l - 1, g))
                    for i, t in tiles:
                        last = nc.tensor.matmul(out[:, P * i:P * i + P], R[:, t], W[:, t] if l else ident[:],
                                                start=True, stop=True)
                elif what == "wT":
                    read(pe, ("W", h, LEVELS - 1, g))
                    pe.wait_ge(kscaled, 2 * h + 1)
                    for i, t in tiles:
                        last = nc.tensor.matmul(out[:, P * i:P * i + P], ke[:, t], W[:, t], start=True, stop=True)
                elif what == "u":
                    read(pe, ("vt", h, 0, g))
                    for i, t in tiles:
                        last = nc.tensor.matmul(out[:, P * i:P * i + P], W[:, t], vt[:, t], start=True, stop=True)
                last.then_inc(worked, 1)

            def state(h, n):
                t, half, _, _ = chunk_at(n)
                m = STEPS * h + n
                if n == 0:
                    read(pe, ("wT", h, 0, GROUPS - 1))
                    pe.wait_ge(qdec, h + 1)
                if m >= 2:
                    pe.wait_ge(o_kept, m - 1)
                pe.wait_ge(s_kept, m + h + 1)
                nc.tensor.matmul(so[m % 2][:], wq[h % 2][:, t, 2 * half:2 * half + 2].rearrange("p a b -> p (a b)"),
                                 S[:, n % 2], start=True, stop=True, skip_group_check=True).then_inc(s_made, 1)

            def update(h, n):
                t, half, r, r2 = chunk_at(n)
                m = STEPS * h + n
                if n == 0:
                    pe.wait_ge(kscaled, 2 * h + 2)
                    read(pe, ("at", h, 0, GROUPS - 1))
                pe.wait_ge(v_new, m + 1)
                nc.tensor.matmul(skv[:], kd[h % 2][r, t], vnew[r, n % 2], start=True, stop=True).then_inc(kv_made, 1)
                nc.tensor.matmul(so[m % 2][r2], at[h % 2][r, t, r], vnew[r, n % 2],
                                 start=False, stop=True, skip_group_check=True).then_inc(o_made, 1)

            for item in plan:
                if item[0] == "fill":
                    fill(item[1])
                elif item[0] == "state":
                    state(*item[1:])
                elif item[0] == "update":
                    update(*item[1:])

        @block.vector
        def _(dve):
            def scale(h):
                for i, j, r in ((0, PK, rk), (1, PQ, rq)):
                    dve.wait_ge(rooted, 2 * h + i + 1)
                    nc.vector.tensor_tensor(ys[:, j], ys[:, j], r[:], ALU.mult).then_inc(normed, 1)
                    if i == 0:
                        read(dve, ("grow", h, 0, GROUPS - 1))
                        if h >= 1:
                            read(dve, ("at", h - 1, 0, GROUPS - 1))
                            dve.wait_ge(lbeta, h)
                        for t in range(NT):
                            last = nc.vector.tensor_scalar(LA[:, P * t:P * t + P], grow[:, P * t:P * t + P],
                                                           gsum[:, t, h:h + 1], 0.0, ALU.subtract, ALU.min)
                        last.then_inc(ldiff, 1)
                dve.wait_ge(growexp, h + 1)
                dve.wait_ge(normed, 2 * h + 2)
                if h >= 2:
                    dve.wait_ge(s_made, STEPS * (h - 1))
                nc.vector.tensor_tensor(wq[h % 2][:, :, 1:3].rearrange("p t a b -> p t (a b)"), by_tile(ys[:, PQ]),
                                        by_tile(grow[:]), ALU.mult).then_inc(qdec, 1)

            def take(key):
                what, h, l, g = key
                src = by_tile(bank_of(key)[:, 0:GW])
                if what == "kk":
                    dve.wait_ge(lbeta, h + 1)
                    dst, by = group(U, g), by_tile(LB[:, GW * g:GW * g + GW])
                elif what == "at":
                    dve.wait_ge(lmasked, h + 1)
                    if h >= 2:
                        dve.wait_ge(o_made, STEPS * (h - 1))
                    dst, by = group(at[h % 2], g), by_tile(LA[:, GW * g:GW * g + GW])
                elif what == "Q":
                    dst, by = group(R, g), chunk[:, 4 + l:5 + l].to_broadcast([P, GT, P])
                    if h >= 1 and l == 0:
                        dve.wait_ge(worked, place["W", h - 1, LEVELS - 1, g] + 1)
                else:
                    if h >= 2:
                        dve.wait_ge(v_new, STEPS * (h - 1))
                    dst, by = group(u[h % 2], g), group(beta, g)[:, :, h:h + 1].to_broadcast([P, GT, P])
                dve.wait_ge(worked, place[key] + 1)
                nc.vector.tensor_tensor(dst, src, by, ALU.mult).then_inc(read_dve, 1)

            def turn(h, l, g):
                read(dve, ("W", h, l, g))
                flat = lambda x: group(x, g).rearrange("p t i -> p (t i)")
                nc.vector.transpose(flat(X), flat(W)).then_inc(x_turned, 1)

            def state(h, n):
                t, half, r, _ = chunk_at(n)
                m = STEPS * h + n
                dve.wait_ge(s_made, m + 1)
                if n == 0:
                    read(dve, ("u", h, 0, GROUPS - 1))
                nc.vector.scalar_tensor_tensor(vnew[r, n % 2], so[m % 2][r, :], nbeta[r, t, h:h + 1], u[h % 2][r, t],
                                               ALU.mult, ALU.add).then_inc(v_new, 1)

            def update(h, n):
                t, half, _, _ = chunk_at(n)
                m = STEPS * h + n
                dve.wait_ge(kv_made, m + 1)
                dve.wait_ge(s_kept, m + h + 1)
                nc.vector.scalar_tensor_tensor(S[:, (n + 1) % 2], S[:, n % 2], whole[:, half, t, h:h + 1], skv[:],
                                               ALU.mult, ALU.add).then_inc(s_kept, 1)
                if n == STEPS - 1 and h + 1 < H:
                    dve.wait_ge(s_kept, m + h + 2)
                    nc.vector.memset(S[:, 0], 0.0).then_inc(s_kept, 1)

            def norm(h):
                x = o[h % 2][:, 1:]
                dve.wait_ge(o_squared, h + 1)
                nc.vector.tensor_reduce(ovar[:], osq[:], AX.X, ALU.add).then_inc(o_summed, 1)
                dve.wait_ge(o_root, h + 1)
                nc.vector.tensor_tensor(x, x, orstd[:].unsqueeze(2).to_broadcast([P, NQT, P]),
                                        ALU.mult).then_inc(o_scaled, 1)
                dve.wait_ge(o_scaled, 2 * h + 1)
                dve.wait_ge(z_loaded, 32 * h + 32)
                nc.vector.tensor_tensor(x, x, zb[:], ALU.mult).then_inc(o_scaled, 1)

            nc.vector.memset(S[:, 0], 0.0).then_inc(s_kept, 1)
            for item in plan:
                if item[0] == "scale":
                    scale(item[1])
                elif item[0] == "norm":
                    norm(item[1])
                elif item[0] == "state":
                    state(*item[1:])
                elif item[0] == "update":
                    update(*item[1:])
                elif item[0] == "fill":
                    what, h, l, g = key = item[1]
                    if what in by_dve:
                        take(key)
                    elif what == "W" and 0 < l < LEVELS - 1:
                        turn(h, l, g)

        @block.scalar
        def _(act):
            def squares(h):
                act.wait_ge(y_loaded, 16 * h + 16)
                for j in (PK, PQ):
                    if h >= 1:
                        act.wait_ge(worked, place["sum_q", h - 1, 0, GROUPS - 1] + 1)
                    nc.scalar.activation(sq[:, j], ys[:, j], ACT.Square).then_inc(squared, 1)

            def scale(h):
                for i, r in enumerate((rk, rq)):
                    read(act, (("sum_k", "sum_q")[i], h, 0, GROUPS - 1))
                    nc.scalar.activation(r[:], r[:], ACT.Exp, scale=-0.5, bias=consts[:, 1 + i:2 + i]).then_inc(rooted, 1)
                act.wait_ge(ldiff, h + 1)
                nc.scalar.activation(LA[:], LA[:], ACT.Exp).then_inc(lexp, 1)
                nc.scalar.activation(grow[:], grow[:], ACT.Exp).then_inc(growexp, 1)

            def take(key):
                what, h, l, g = key
                bank = bank_of(key)[:, 0:GW]
                flat = slice(GW * g, GW * g + GW)
                func, more = ACT.Copy, {}
                if what == "grow":
                    dst = grow[:, flat]
                    if h >= 1:
                        act.wait_ge(qdec, h)
                elif what in ("sum_k", "sum_q"):
                    dst, func, more = (rk if what == "sum_k" else rq)[:, flat], ACT.Ln, {"bias": consts[:, 0:1]}
                    if h >= 1:
                        act.wait_ge(normed, 2 * h)
                elif what == "wT":
                    dst, bank = group(wq[h % 2], g)[:, :, 0:4:3], bank.rearrange("p (t a b) -> p t a b", t=GT, a=2)
                    if h >= 2:
                        act.wait_ge(s_made, STEPS * (h - 1))
                else:
                    dst, bank = group({"kt": kt, "vt": vt, "W": W}[what], g), by_tile(bank)
                    if what == "kt" and h >= 1:
                        act.wait_ge(kscaled, 2 * h)
                    if what == "vt" and h >= 1:
                        act.wait_ge(worked, place["u", h - 1, 0, g] + 1)
                    if what == "W" and l >= 2:
                        act.wait_ge(x_turned, x_no(h, l - 1, g))
                act.wait_ge(worked, place[key] + 1)
                nc.scalar.activation(dst, bank, func, **more).then_inc(read_act, 1)

            def take_post(key):
                _, h, _, g = key
                if h >= 1 and g == 0:
                    act.wait_ge(og_saved, 16 * h)
                act.wait_ge(worked, place[key] + 1)
                src = bank_of(key)[:].rearrange("p (t a b) -> p t a b", t=4, a=2)
                dst = og[:, 512 * g:512 * g + 512].rearrange("p (t a b) -> p t a b", t=4, a=2)
                nc.scalar.activation(dst[:, :, 0], src[:, :, 1], ACT.Copy, scale=gw[:, 0:1])
                nc.scalar.activation(dst[:, :, 1], src[:, :, 0], ACT.Copy, scale=gw[:, 0:1]).then_inc(read_act, 1)
                if g == 1:
                    read(act, key)
                    act.dma_start(og_dram[h], og[:]).then_inc(og_saved, 16)

            def norm(h):
                act.wait_ge(o_kept, STEPS * (h + 1))
                if h >= 1:
                    act.wait_ge(o_summed, h)
                nc.scalar.activation(osq[:], o[h % 2][:, 1:], ACT.Square).then_inc(o_squared, 1)
                act.wait_ge(o_summed, h + 1)
                nc.scalar.activation(oln[:], ovar[:], ACT.Ln, scale=1.0 / DK, bias=consts[:, 0:1]).then_inc(o_ln, 1)
                act.wait_ge(o_ln, h + 1)
                nc.scalar.activation(orstd[:], oln[:], ACT.Exp, scale=-0.5).then_inc(o_root, 1)

            def keep_o(h, n):
                t, _, _, r2 = chunk_at(n)
                m = STEPS * h + n
                if n == 0 and h >= 2:
                    read(act, ("post", h - 2, 0, 1))
                act.wait_ge(o_made, m + 1)
                nc.scalar.activation(o[h % 2][r2, t], so[m % 2][r2, :], ACT.Copy).then_inc(o_kept, 1)

            act.wait_ge(const_made, 1)
            act.wait_ge(zeroed, 1)
            act.wait_ge(gw_loaded, 16)
            for item in plan:
                if item[0] == "squares":
                    squares(item[1])
                elif item[0] == "scale":
                    scale(item[1])
                elif item[0] == "norm":
                    norm(item[1])
                elif item[0] == "update":
                    keep_o(*item[1:])
                elif item[0] == "fill" and item[1][0] == "post":
                    take_post(item[1])
                elif item[0] == "fill" and item[1][0] not in by_dve:
                    take(item[1])
            act.wait_ge(og_saved, 16 * H)


def merge(nc, x, g_dram, og_dram, gates_dram, w_proj_a, w_proj_b, w_out, out):
    KA = WA // P
    x_v, out_v = (a.rearrange("b (t p) d -> (b t) p d", p=P) for a in (x, out))
    with ExitStack() as ctx:
        sb = lambda name, shape: ctx.enter_context(nc.sbuf_tensor(name, shape, F32))
        sem = lambda n: ctx.enter_context(nc.semaphore(n))
        wa, wb, wo = sb("wa", [P, KA, D]), sb("wb", [P, KD, D]), sb("wo", [P, KD, D])
        ga_in, gb_in = sb("ga_in", [P, KA, SEQ]), sb("gb_in", [P, KD, SEQ])
        gate = sb("mgate", [P, 2, 2, SEQ])
        part, mT = sb("part", [P, 2, 512]), sb("mT", [P, KD, SEQ])
        xin, res = sb("xin", [P, 2, D]), sb("res", [P, 2, 512])
        NB = 8
        ps = [ctx.enter_context(nc.psum_tensor(f"mp{i}", [P, 512], F32)) for i in range(NB)]
        a_in, b_in, wo_in = sem("a_in"), sem("b_in"), sem("wo_in")
        gate_in = [sem("gate_in0"), sem("gate_in1")]
        x_in = [sem("x_in0"), sem("x_in1")]
        made, taken, mixed, added = sem("m_made"), sem("m_taken"), sem("m_mixed"), sem("m_added")
        out_saved = [sem("out_saved0"), sem("out_saved1")]
        pairs = [(f, c) for f in range(KD) for c in range(2)]
        outs = [(t, c) for t in range(NQT) for c in range(2)]
        block = ctx.enter_context(nc.Block())

        @block.sync
        def _(sp):
            sp.dma_start(wa[:], w_proj_a.rearrange("l (k p) n -> p (l k) n", p=P)).then_inc(a_in, 16)
            sp.dma_start(ga_in[:], g_dram.rearrange("k p t -> p k t")).then_inc(a_in, 16)
            sp.dma_start(wb[:], w_proj_b.rearrange("l (k p) n -> p (l k) n", p=P)).then_inc(b_in, 16)
            sp.dma_start(gb_in[:], og_dram.rearrange("k p t -> p k t")).then_inc(b_in, 16)
            for f in range(KD):
                if f >= 2:
                    sp.wait_ge(mixed, 2 * (f - 1))
                for j in range(2):
                    sp.dma_start(gate[:, f % 2, j], gates_dram[KD * j + f]).then_inc(gate_in[f % 2], 16)
                if f == 1:
                    sp.dma_start(wo[:], w_out.rearrange("l (k p) n -> p (l k) n", p=P)).then_inc(wo_in, 16)
            for t in range(NQT):
                if t >= 2:
                    sp.wait_ge(added, 2 * (t - 1))
                sp.dma_start(xin[:, t % 2], x_v[t]).then_inc(x_in[t % 2], 16)

        @block.tensor
        def _(pe):
            for n, (f, c) in enumerate(pairs):
                for j, (w, src, ks) in enumerate(((wa, ga_in, KA), (wb, gb_in, KD))):
                    m = 2 * n + j
                    if n == 0:
                        pe.wait_ge((a_in, b_in)[j], 32)
                    if m >= NB:
                        pe.wait_ge(taken, m - NB + 1)
                    for k in range(ks):
                        last = nc.tensor.matmul(ps[m % NB][:], w[:, k, P * f:P * f + P], src[:, k, 512 * c:512 * c + 512],
                                                start=(k == 0), stop=(k == ks - 1))
                    last.then_inc(made, 1)
            pe.wait_ge(wo_in, 16)
            pe.wait_ge(mixed, len(pairs))
            for n, (t, c) in enumerate(outs):
                m = 2 * len(pairs) + n
                if n >= NB:
                    pe.wait_ge(added, n - NB + 1)
                for k in range(KD):
                    last = nc.tensor.matmul(ps[m % NB][:], mT[:, k, P * t:P * t + P], wo[:, k, 512 * c:512 * c + 512],
                                            start=(k == 0), stop=(k == KD - 1))
                last.then_inc(made, 1)

        @block.vector
        def _(dve):
            for n, (f, c) in enumerate(pairs):
                s = slice(512 * c, 512 * c + 512)
                dve.wait_ge(gate_in[f % 2], 32 * (f // 2 + 1))
                dve.wait_ge(made, 2 * n + 1)
                if n >= 2:
                    dve.wait_ge(mixed, n - 1)
                nc.vector.tensor_tensor(part[:, n % 2], ps[2 * n % NB][:], gate[:, f % 2, 0, s], ALU.mult).then_inc(taken, 1)
                dve.wait_ge(made, 2 * n + 2)
                nc.vector.tensor_tensor(mT[:, f, s], ps[(2 * n + 1) % NB][:], gate[:, f % 2, 1, s], ALU.mult).then_inc(taken, 1)
                dve.wait_ge(taken, 2 * n + 2)
                nc.vector.tensor_tensor(mT[:, f, s], mT[:, f, s], part[:, n % 2], ALU.add).then_inc(mixed, 1)
            for n, (t, c) in enumerate(outs):
                m = 2 * len(pairs) + n
                dve.wait_ge(x_in[t % 2], 16 * (t // 2 + 1))
                dve.wait_ge(made, m + 1)
                if n >= 2:
                    dve.wait_ge(out_saved[n % 2], 16 * (n // 2))
                nc.vector.tensor_tensor(res[:, n % 2], ps[m % NB][:], xin[:, t % 2, 512 * c:512 * c + 512],
                                        ALU.add).then_inc(added, 1)

        @block.scalar
        def _(act):
            for n, (t, c) in enumerate(outs):
                act.wait_ge(added, n + 1)
                act.dma_start(out_v[t, :, 512 * c:512 * c + 512], res[:, n % 2]).then_inc(out_saved[n % 2], 16)
            for s in range(2):
                act.wait_ge(out_saved[s], 16 * len(outs) // 2)


def hybrid_layer(nc, x, meta_tokens, rel_bias, norm_w, w_in, q_norm_w, k_norm_w, conv_w, a_log, dt_bias, gdn_norm_w,
                 w_proj_a, w_proj_b, w_out, band_tab, chunk_tab, out):
    dram = lambda name, shape: nc.dram_tensor(name, shape, F32, kind="Internal").ap()
    za_dram, zb_dram = dram("za_dram", (NQT, P, WA)), dram("zb_dram", (NQT, P, D))
    gates_dram, band_dram = dram("gates_dram", (2 * KD, P, SEQ)), dram("band_dram", (H, band_tab.shape[1]))
    g_dram, og_dram = dram("g_dram", (WA // P, P, SEQ)), dram("og_dram", (H, P, SEQ))
    qkv_dram, conv_dram = dram("qkv_dram", (3, NT, P, WA)), dram("conv_dram", (3, H, P, T))
    sb = lambda stack, name, shape: stack.enter_context(nc.sbuf_tensor(name, shape, F32))
    with ExitStack() as whole_layer:
        ident, ones = sb(whole_layer, "ident", [P, P]), sb(whole_layer, "ones", [P, P])
        small = sb(whole_layer, "small", [P, NT, NSM])
        make_constants(nc, ident, ones)
        with ExitStack() as branch_a:
            score = [sb(branch_a, f"score{t}", [P, keys_of(t)]) for t in range(NQT)]
            with ExitStack() as normed:
                h_high, h_low = (normed.enter_context(nc.sbuf_tensor(n, [P, KD, TP], F32R)) for n in ("h_high", "h_low"))
                normed_tokens(nc, x, meta_tokens, norm_w, h_high, h_low, ident)
                projections(nc, w_in, conv_w, h_high, h_low, small, score, qkv_dram, za_dram, zb_dram, gates_dram, conv_dram)
            qT, kT, band = sb(branch_a, "qT", [P, 4, SEQ]), sb(branch_a, "kT", [P, 4, T]), sb(branch_a, "band", [P, H, 2 * P])
            attention_operands(nc, ident, qkv_dram, qT, kT, band, rel_bias, band_tab, band_dram, q_norm_w, k_norm_w)
            attention(nc, ident, score, qT, kT, band, qkv_dram, za_dram, g_dram)
        with ExitStack() as branch_b:
            chunk = sb(branch_b, "chunk", [P, 10, P])
            per_token = [sb(branch_b, n, [P, NT, H]) for n in ("beta", "nbeta", "gates", "gsum", "to_here", "to_end")]
            whole = sb(branch_b, "whole", [P, 2, NT, H])
            decays(nc, small, chunk, chunk_tab, a_log, dt_bias, *per_token, whole)
            delta_heads(nc, conv_dram, gdn_norm_w, ident, ones, chunk, *per_token, whole, zb_dram, og_dram)
    merge(nc, x, g_dram, og_dram, gates_dram, w_proj_a, w_proj_b, w_out, out)


_INS = ["x", "meta_tokens", "rel_bias", "norm_w", "w_in", "q_norm_w", "k_norm_w", "conv_w", "a_log", "dt_bias",
        "gdn_norm_w", "w_proj_a", "w_proj_b", "w_out"]


def kernel(**inputs):
    import concourse.bacc as bacc
    import numpy as np
    from concourse.bass_utils import run_bass_kernel_spmd

    nc = bacc.Bacc("TRN2", target_bir_lowering=False, num_devices=1)
    arrays = {name: np.ascontiguousarray(inputs[name]) for name in _INS}
    arrays["band_tab"], arrays["chunk_tab"] = band_table(), chunk_table()
    args = {name: nc.dram_tensor(f"in_{name}", a.shape, mybir.dt.from_np(a.dtype), kind="ExternalInput").ap()
            for name, a in arrays.items()}
    out = nc.dram_tensor("layer_out", (1, SEQ, D), F32, kind="ExternalOutput").ap()
    hybrid_layer(nc, **args, out=out)
    r = run_bass_kernel_spmd(nc, [{f"in_{name}": a for name, a in arrays.items()}], core_ids=[0])
    return r.results[0]["layer_out"]
```

```python
import math
from contextlib import ExitStack

import concourse.bass as bass
from concourse import mybir

P = 128
D = 1024
SEQ = 1024
META = 16
T = META + SEQ
PAD = P - META
TP = PAD + T
KD = D // P
NQT = SEQ // P
NT = TP // P
H = 8
DH = 64
WA = H * DH
DK = 128
CHUNK = 64
CONV = 4
TOPK = 256
EPS = 1e-6

OFF_QA, OFF_KA, OFF_VA, OFF_ZA = 0, WA, 2 * WA, 3 * WA
OFF_QI = 4 * WA
OFF_KI = OFF_QI + WA
OFF_WI = OFF_KI + DH
OFF_QB = OFF_WI + H
OFF_KB = OFF_QB + D
OFF_VB = OFF_KB + D
OFF_ZB = OFF_VB + D
OFF_BB = OFF_ZB + D
OFF_GA = OFF_BB + 2 * H
OFF_GB = OFF_GA + D
NSM = 3 * H

PICKED = -3.4028234663852886e38
AFTER = -3.0e38
HIDDEN = -1.0e30

ALU = mybir.AluOpType
ACT = mybir.ActivationFunctionType
AX = mybir.AxisListType
F32 = mybir.dt.float32
F32R = mybir.dt.float32r


def keys_of(t):
    return META + P * (t + 1)


def product(nc, out, ws, xs, first=True, final=True):
    for k, ((w_high, w_low), (x_high, x_low)) in enumerate(zip(ws, xs)):
        nc.tensor.matmul(out, w_high, x_high, start=(first and k == 0), stop=False)
        nc.tensor.matmul(out, w_high, x_low, start=False, stop=False)
        last = nc.tensor.matmul(out, w_low, x_high, start=False, stop=(final and k == len(ws) - 1))
    return last


def make_constants(nc, ident, ones):
    with nc.semaphore("ident_zero") as ident_zero, nc.Block() as block:
        @block.gpsimd
        def _(pool):
            nc.gpsimd.memset(ones[:], 1.0)
            nc.gpsimd.memset(ident[:], 0.0).then_inc(ident_zero, 1)
            pool.wait_ge(ident_zero, 1)
            nc.gpsimd.affine_select(out=ident[:], in_=ident[:], compare_op=ALU.not_equal, fill=1.0,
                                    base=0, pattern=[[-1, P]], channel_multiplier=1)


LOAD = 2 * P


def normed_tokens(nc, x, meta_tokens, norm_w, h_high, h_low, ident, w_first, w_raw, w_high, w_low, w_split):
    x_v = x.rearrange("b (t p) d -> (b t) p d", p=P)
    with ExitStack() as ctx:
        xt = ctx.enter_context(nc.sbuf_tensor("xt", [P, NT, D], F32))
        xn = ctx.enter_context(nc.sbuf_tensor("xn", [P, 2, D], F32))
        junk = ctx.enter_context(nc.sbuf_tensor("junk", [P, D], F32))
        h = ctx.enter_context(nc.sbuf_tensor("h", [P, 2, 4, P], F32))
        nwT = ctx.enter_context(nc.sbuf_tensor("nwT", [P, KD], F32))
        ssq = ctx.enter_context(nc.sbuf_tensor("ssq", [P, NT], F32))
        mean = ctx.enter_context(nc.sbuf_tensor("mean", [P, NT], F32))
        root = ctx.enter_context(nc.sbuf_tensor("root", [P, NT], F32))
        rstd = ctx.enter_context(nc.sbuf_tensor("rstd", [P, NT], F32))
        tr = [ctx.enter_context(nc.psum_tensor(f"tr{i}", [P, 4, P], F32)) for i in range(4)]
        sem = lambda n: ctx.enter_context(nc.semaphore(n))
        x_loaded = [sem(f"x_loaded{t}") for t in range(NT)]
        nw_loaded, squared, mean_ready, root_ready, rstd_ready = (
            sem(n) for n in ("nw_loaded", "squared", "mean_ready", "root_ready", "rstd_ready"))
        scaled, turned, weighted, high_ready, low_ready = (
            sem(n) for n in ("scaled", "turned", "weighted", "high_ready", "low_ready"))
        first_loaded, first_high = sem("first_loaded"), sem("first_high")
        block = ctx.enter_context(nc.Block())

        def rows(t):
            return META if t == 0 else P

        def place(m):
            t, g = m // 2, m % 2
            c = P * t if t else PAD
            return (slice(None), slice(4 * g, 4 * g + 4), slice(c, c + rows(t))), h[:, g, :, 0:rows(t)]

        @block.sync
        def _(sp):
            for t in range(NT):
                src = meta_tokens if t == 0 else x_v[t - 1]
                sp.dma_start(xt[:rows(t), t], src).then_inc(x_loaded[t], 16)
                if t == 1:
                    with nc.allow_non_contiguous_dma(reason="norm_w by partition"):
                        sp.dma_start(nwT[:], norm_w.rearrange("l (k p) -> p (l k)", p=P)).then_inc(nw_loaded, 16)
            sp.dma_start(w_raw[:, 0], w_first).then_inc(first_loaded, 16)

        @block.gpsimd
        def _(pool):
            nc.gpsimd.memset(h_high[:, :, 0:PAD].bitcast(F32), 0.0)
            nc.gpsimd.memset(h_low[:, :, 0:PAD].bitcast(F32), 0.0)
            for m in range(2 * NT):
                at, src = place(m)
                pool.wait_ge(high_ready, m + 1)
                nc.gpsimd.tensor_tensor(h_low[at], src, h_high[at], ALU.subtract).then_inc(low_ready, 1)
                if m == NT:
                    pool.wait_ge(first_high, 1)
                    nc.gpsimd.tensor_tensor(w_low[:, 0], w_raw[:, 0], w_high[:, 0], ALU.subtract).then_inc(w_split, 1)

        @block.scalar
        def _(act):
            def square(t):
                n = rows(t)
                act.wait_ge(x_loaded[t], 16)
                if t:
                    act.wait_ge(squared, t)
                nc.scalar.activation(junk[:n], xt[:n, t], ACT.Square, accum_out=ssq[:n, t:t + 1]).then_inc(squared, 1)

            square(0)
            for t in range(NT + 1):
                if t + 1 < NT:
                    square(t + 1)
                if t < NT:
                    n = rows(t)
                    act.wait_ge(mean_ready, t + 1)
                    nc.scalar.activation(root[:n, t:t + 1], mean[:n, t:t + 1], ACT.Sqrt).then_inc(root_ready, 1)
                if t == 4:
                    act.wait_ge(first_loaded, 16)
                    nc.scalar.activation(w_high[:, 0], w_raw[:, 0], ACT.Copy).then_inc(first_high, 1)
                if t >= 1:
                    for m in (2 * t - 2, 2 * t - 1):
                        at, src = place(m)
                        act.wait_ge(weighted, m + 1)
                        nc.scalar.activation(h_high[at], src, ACT.Copy).then_inc(high_ready, 1)

        @block.vector
        def _(dve):
            def average(t):
                n = rows(t)
                dve.wait_ge(squared, t + 1)
                nc.vector.tensor_scalar(mean[:n, t:t + 1], ssq[:n, t:t + 1], 1.0 / D, EPS,
                                        ALU.mult, ALU.add).then_inc(mean_ready, 1)

            average(0)
            for t in range(NT + 1):
                if t + 1 < NT:
                    average(t + 1)
                if t < NT:
                    n = rows(t)
                    dve.wait_ge(root_ready, t + 1)
                    nc.vector.reciprocal(rstd[:n, t:t + 1], root[:n, t:t + 1]).then_inc(rstd_ready, 1)
                    dve.wait_ge(rstd_ready, t + 1)
                    if t >= 2:
                        dve.wait_ge(turned, 2 * (t - 1))
                    nc.vector.tensor_scalar(xn[:n, t % 2], xt[:n, t], rstd[:n, t:t + 1], None,
                                            ALU.mult).then_inc(scaled, 1)
                if t == 1:
                    dve.wait_ge(nw_loaded, 16)
                if t >= 1:
                    n = rows(t - 1)
                    for g in range(2):
                        m = 2 * (t - 1) + g
                        dve.wait_ge(turned, m + 1)
                        if m >= 2:
                            dve.wait_ge(low_ready, m - 1)
                        nc.vector.tensor_tensor(
                            h[:, g, :, 0:n], tr[m % 4][:, :, 0:n],
                            nwT[:, 4 * g:4 * g + 4].unsqueeze(2).to_broadcast([P, 4, n]),
                            ALU.mult).then_inc(weighted, 1)

        @block.tensor
        def _(pe):
            for t in range(NT):
                n = rows(t)
                pe.wait_ge(scaled, t + 1)
                for g in range(2):
                    if 2 * t + g >= 4:
                        pe.wait_ge(weighted, 2 * t + g - 3)
                    for k in range(4):
                        f = (4 * g + k) * P
                        last = nc.tensor.transpose(tr[(2 * t + g) % 4][:, k, 0:n], xn[:n, t % 2, f:f + P],
                                                   ident[:n, :n])
                    last.then_inc(turned, 1)


def spans(w):
    step = -(-w // (16 * -(-w // 512))) * 16
    return [(a, min(w, a + step)) for a in range(0, w, step)]


def projections(nc, w_in, conv_w, h_high, h_low, w_raw, w_high, w_low, w_low_ready, ident, small, score, qkv_dram, za_dram, zb_dram, gates_dram, conv_dram):
    w_v = w_in.rearrange("l (k p) n -> p (l k) n", p=P)
    BANKS, STAGES = 7, 3

    columns = lambda off, n: [[(off + c, LOAD, 0)] for c in range(0, n, LOAD)]
    loads = columns(OFF_QI, WA)
    small_load = len(loads)
    loads += [[(OFF_KI, DH, 0), (OFF_KI, DH, DH), (OFF_WI, H, P), (OFF_BB, P - H, P + H)]]
    rows = [("qa", OFF_QA, WA), ("ka", OFF_KA, WA), ("va", OFF_VA, WA), ("za", OFF_ZA, WA), ("zb", OFF_ZB, D)]
    conv_loads = columns(OFF_KB, D) + columns(OFF_QB, D) + columns(OFF_VB, D)
    other_loads = [("gate", n) for n in range(2 * D // LOAD)]
    other_loads += [(what, n) for what, _, w in rows for n in range(w // LOAD)]
    offset = {what: off for what, off, _ in rows}
    offset["gate"] = OFF_GA
    order = []
    for n, other in enumerate(other_loads):
        if n < len(conv_loads):
            order.append(("conv", n))
        order.append(other)
    load_of = {}
    for what, n in order:
        load_of[what, n] = len(loads)
        loads.append(conv_loads[n] if what == "conv" else [(offset[what] + LOAD * n, LOAD, 0)])
    width = [sum(w for _, w, _ in parts) for parts in loads]

    HALF = (SEQ - P) // 2
    fills = [("qi", f, HALF * c, HALF * c + HALF, f // 2) for f in range(4) for c in range(2)]
    fills += [("ki", 0, a, b, small_load) for a, b in spans(T)]
    n_split = len(fills)
    fills += [("smallT", 0, a, b, small_load) for a, b in spans(TP)]
    fills += [("small", 0, 0, NT * NSM, small_load)]
    fills += [("rel", (t, h), a, b, None) for t in range(1, NQT) for h in range(H) for a, b in spans(keys_of(t))]
    for what, n in order:
        load = load_of[what, n]
        if what == "conv":
            fills += [("conv", f, a, b, load) for f in (2 * n, 2 * n + 1) for a, b in spans(T)]
        elif what == "gate":
            fills += [("gate", f, 512 * c, 512 * c + 512, load) for f in (2 * n, 2 * n + 1) for c in range(2)]
        else:
            fills += [(what, t, LOAD * n, LOAD * n + LOAD, load) for t in range(0 if what in ("ka", "va") else 1, NT)]
    last_fill = [max(n for n, f in enumerate(fills) if f[4] == load) + 1 for load in range(len(loads))]
    first_rel = min(n for n, f in enumerate(fills) if f[0] == "rel")
    done_by = {}
    for n, f in enumerate(fills):
        done_by[f[0], f[1]] = n + 1
    swish_at = {done_by["conv", f] + 3: f for f in range(3 * H)}

    with ExitStack() as ctx:
        sb = lambda name, shape, kind=F32: ctx.enter_context(nc.sbuf_tensor(name, shape, kind))
        qi_high, qi_low = sb("qi_high", [P, 4, SEQ - P], F32R), sb("qi_low", [P, 4, SEQ - P], F32R)
        ki_high, ki_low = sb("ki_high", [P, T], F32R), sb("ki_low", [P, T], F32R)
        raw, smooth, cw = sb("raw", [P, 2, CONV - 1 + T]), sb("smooth", [P, 2, T]), sb("cw", [P, CONV, 3 * H])
        rel = raw
        smallT = smooth[:].rearrange("p s t -> p (s t)")
        stage = sb("stage", [P, STAGES, 512])
        top8 = sb("top8", [P, 8])
        fence = sb("fence", [P, P])
        pj = [ctx.enter_context(nc.psum_tensor(f"pj{i}", [P, 512], F32)) for i in range(BANKS)]
        sem = lambda n: ctx.enter_context(nc.semaphore(n))
        w_loaded = [sem("w_loaded0"), sem("w_loaded1")]
        w_high_ready = sem("w_high_ready")
        filled, emptied, low_kept = sem("filled"), sem("emptied"), sem("low_kept")
        rel_used, fenced, step, picked, masked = (sem(n) for n in ("rel_used", "fenced", "step", "picked", "masked"))
        fence_ready = sem("fence_ready")
        cw_loaded, raw_start, conved, swished = (sem(n) for n in ("cw_loaded", "raw_start", "conved", "swished"))
        saved = [sem(f"saved{i}") for i in range(STAGES)]
        smooth_saved = [sem("smooth_saved0"), sem("smooth_saved1")]
        block = ctx.enter_context(nc.Block())

        @block.sync
        def _(sp):
            for n, parts in enumerate(loads):
                if n == 0:
                    continue
                if n >= 2:
                    sp.wait_ge(w_low_ready, n - 1)
                for col, w, at in parts:
                    sp.dma_start(w_raw[:, n % 2, :, at:at + w],
                                 w_v[:, :, col:col + w]).then_inc(w_loaded[n % 2], 16)
                if n == 1:
                    with nc.allow_non_contiguous_dma(reason="per-feature weights on partitions"):
                        for k in range(CONV):
                            sp.dma_start(cw[:, k], conv_w[0, k].rearrange("(f p) -> p f", p=P)).then_inc(cw_loaded, 16)

        @block.gpsimd
        def _(pool):
            nc.gpsimd.memset(score[0][:], 0.0).then_inc(masked, 1)
            nc.gpsimd.memset(fence[:], -AFTER).then_inc(fence_ready, 1)
            for n, parts in enumerate(loads):
                if n == 0:
                    continue
                raw_w, high, low = (a[:, n % 2, :, 0:width[n]] for a in (w_raw, w_high, w_low))
                pool.wait_ge(w_loaded[n % 2], 16 * sum(len(x) for x in loads[n % 2 or 2:n + 1:2]))
                if n >= 2:
                    pool.wait_ge(filled, last_fill[n - 2])
                nc.gpsimd.tensor_copy(high, raw_w).then_inc(w_high_ready, 1)
                pool.wait_ge(w_high_ready, n)
                nc.gpsimd.tensor_tensor(low, raw_w, high, ALU.subtract).then_inc(w_low_ready, 1)
                if n == 1:
                    pool.wait_ge(masked, 1)
                    diagonal = score[0][:, META:META + P]
                    nc.gpsimd.affine_select(out=diagonal, in_=diagonal, compare_op=ALU.is_ge, fill=HIDDEN, base=0,
                                            pattern=[[-1, P]], channel_multiplier=1).then_inc(masked, 1)
                    pool.wait_ge(fence_ready, 1)
                    nc.gpsimd.affine_select(out=fence[:], in_=fence[:], compare_op=ALU.is_ge, fill=AFTER, base=0,
                                            pattern=[[-1, P]], channel_multiplier=1).then_inc(fence_ready, 1)

        @block.tensor
        def _(pe):
            loaded = -1
            for n, (what, i, a, b, load) in enumerate(fills):
                bank = pj[n % BANKS]
                if n >= BANKS:
                    if n - BANKS < n_split:
                        pe.wait_ge(low_kept, n - BANKS + 1)
                    else:
                        pe.wait_ge(emptied, n - BANKS + 1)
                if load is not None and load > loaded:
                    loaded = load
                    pe.wait_ge(w_low_ready, load + 1)
                both = lambda high, low, *at: (high[at], low[at])
                every = slice(None)
                if what == "rel":
                    t, h = i
                    if n == first_rel:
                        pe.wait_ge(low_kept, n_split)
                    r, q = slice(DH * (h % 2), DH * (h % 2) + DH), slice(P * (t - 1), P * t)
                    last = product(nc, bank[:, 0:b - a], [both(qi_high, qi_low, r, h // 2, q)],
                                   [both(ki_high, ki_low, r, slice(a, b))])
                elif what == "small":
                    pe.wait_ge(emptied, n)
                    for t in range(NT):
                        last = nc.tensor.transpose(bank[:, NSM * t:NSM * t + NSM], smallT[0:NSM, P * t:P * t + P],
                                                   ident[0:NSM, 0:NSM])
                elif what in ("qi", "ki", "smallT", "gate", "conv"):
                    f = {"ki": 0, "smallT": P}.get(what, i % 2 * P)
                    c = a + {"qi": 2 * P, "gate": P, "smallT": 0}.get(what, PAD)
                    last = product(nc, bank[:, 0:b - a],
                                   [both(w_high, w_low, every, load % 2, k, slice(f, f + P)) for k in range(KD)],
                                   [both(h_high, h_low, every, k, slice(c, c + b - a)) for k in range(KD)])
                else:
                    last = product(nc, bank[:, 0:LOAD],
                                   [both(h_high, h_low, every, k, slice(P * i, P * i + P)) for k in range(KD)],
                                   [both(w_high, w_low, every, load % 2, k, slice(0, LOAD)) for k in range(KD)])
                last.then_inc(filled, 1)

        @block.scalar
        def _(act):
            n_out = 0

            def swish(f):
                act.wait_ge(conved, CONV * (f + 1))
                nc.scalar.activation(smooth[:, f % 2], smooth[:, f % 2], ACT.Silu).then_inc(swished, 1)
                act.wait_ge(swished, f + 1)
                act.dma_start(conv_dram[f // H, f % H], smooth[:, f % 2]).then_inc(smooth_saved[f % 2], 16)

            for n, (what, i, a, b, _) in enumerate(fills):
                bank = pj[n % BANKS]
                func, m = ACT.Copy, P
                to_dram = None
                if what == "qi":
                    dst = qi_high[:, i, a:b]
                elif what == "ki":
                    dst = ki_high[:, a:b]
                elif what == "smallT":
                    m, dst = NSM, smallT[0:NSM, a:b]
                elif what == "small":
                    dst = small[:].rearrange("p t c -> p (t c)")
                elif what == "rel":
                    t, h = i
                    unit = H * (t - 1) + h
                    func, dst = ACT.Relu, rel[:, unit % 2, a:b]
                    if a == 0 and unit >= 2:
                        act.wait_ge(rel_used, unit - 1)
                elif what == "conv":
                    dst = raw[:, i % 2, CONV - 1 + a:CONV - 1 + b]
                    if a == 0 and i == 0:
                        act.wait_ge(raw_start, 1)
                    if a == 0 and i >= 2:
                        act.wait_ge(conved, CONV * (i - 1))
                else:
                    func = {"gate": ACT.Sigmoid, "za": ACT.Silu, "zb": ACT.Silu}.get(what, ACT.Copy)
                    dst = stage[:, n_out % STAGES, 0:b - a]
                    kept = stage[PAD if i == 0 and what != "gate" else 0:P, n_out % STAGES, 0:b - a]
                    to_dram = {"gate": lambda: gates_dram[i, :, a:b], "za": lambda: za_dram[i - 1, :, a:b],
                               "zb": lambda: zb_dram[i - 1, :, a:b],
                               "qa": lambda: qkv_dram[0, i, :, a:b], "ka": lambda: qkv_dram[1, i, :, a:b],
                               "va": lambda: qkv_dram[2, i, :, a:b]}[what]()
                    if i == 0 and what != "gate":
                        to_dram = to_dram[PAD:P]
                    if n_out >= STAGES:
                        act.wait_ge(saved[n_out % STAGES], 16 * (n_out // STAGES))
                act.wait_ge(filled, n + 1)
                nc.scalar.activation(dst, bank[0:m, 0:b - a], func).then_inc(emptied, 1)
                if to_dram is not None:
                    act.wait_ge(emptied, n + 1)
                    act.dma_start(to_dram, kept).then_inc(saved[n_out % STAGES], 16)
                    n_out += 1
                if n in swish_at:
                    swish(swish_at[n])
            for s in range(STAGES):
                act.wait_ge(saved[s], 16 * len(range(s, n_out, STAGES)))
            for s in range(2):
                act.wait_ge(smooth_saved[s], 16 * 3 * H // 2)

        @block.vector
        def _(dve):
            diagonal = lambda t: score[t][:, keys_of(t) - P:keys_of(t)]
            for n, (what, i, a, b, _) in enumerate(fills[:n_split]):
                high, low = (qi_high[:, i, a:b], qi_low[:, i, a:b]) if what == "qi" else (ki_high[:, a:b], ki_low[:, a:b])
                dve.wait_ge(emptied, n + 1)
                nc.vector.tensor_tensor(low, pj[n % BANKS][:, 0:b - a], high, ALU.subtract).then_inc(low_kept, 1)
            dve.wait_ge(fence_ready, 2)
            for t in range(1, NQT):
                w = keys_of(t)
                for h in range(H):
                    unit = H * (t - 1) + h
                    weight = small[:, t + 1, h:h + 1]
                    dve.wait_ge(emptied, done_by["rel", (t, h)])
                    if h == 0:
                        nc.vector.tensor_scalar(score[t][:], rel[:, unit % 2, 0:w], weight, None,
                                                ALU.mult).then_inc(rel_used, 1)
                    else:
                        dve.wait_ge(rel_used, unit)
                        nc.vector.scalar_tensor_tensor(score[t][:], rel[:, unit % 2, 0:w], weight, score[t][:],
                                                       ALU.mult, ALU.add).then_inc(rel_used, 1)
                dve.wait_ge(rel_used, H * t)
                nc.vector.tensor_tensor(diagonal(t), diagonal(t), fence[:], ALU.min).then_inc(fenced, 1)
            nc.vector.memset(raw[:, :, 0:CONV - 1], 0.0).then_inc(raw_start, 1)
            dve.wait_ge(fenced, NQT - 1)
            nc.vector.tensor_scalar(fence[:], fence[:], 0.0, HIDDEN, ALU.is_lt, ALU.mult).then_inc(fenced, 1)

            def conv(f):
                dve.wait_ge(emptied, done_by["conv", f])
                if f >= 2:
                    dve.wait_ge(smooth_saved[f % 2], 16 * (f // 2))
                kind = {0: 1, 1: 0, 2: 2}[f // H]
                for k in range(CONV):
                    src, dst, w = raw[:, f % 2, k:k + T], smooth[:, f % 2], cw[:, k, H * kind + f % H:H * kind + f % H + 1]
                    if k == 0:
                        nc.vector.tensor_scalar(dst, src, w, None, ALU.mult).then_inc(conved, 1)
                    else:
                        dve.wait_ge(conved, CONV * f + k)
                        nc.vector.scalar_tensor_tensor(dst, src, w, dst, ALU.mult, ALU.add).then_inc(conved, 1)

            ROUNDS = TOPK // 8
            total = sum(keys_of(t) for t in range(1, NQT)) * ROUNDS
            dve.wait_ge(cw_loaded, 16 * CONV)
            steps, convs, searched = 0, 0, 0
            dve.wait_ge(fenced, NQT)
            for t in range(1, NQT):
                for r in range(ROUNDS):
                    if convs < 3 * H and searched * 3 * H >= total * convs:
                        conv(convs)
                        convs += 1
                    searched += keys_of(t)
                    if r:
                        dve.wait_ge(step, steps)
                    nc.vector.max(top8[:], score[t][:]).then_inc(step, 1)
                    steps += 1
                    dve.wait_ge(step, steps)
                    nc.vector.match_replace(score[t][:], top8[:], score[t][:], PICKED).then_inc(step, 1)
                    steps += 1
                dve.wait_ge(step, steps)
                nc.vector.tensor_scalar(score[t][:], score[t][:], PICKED, HIDDEN,
                                        ALU.is_gt, ALU.mult).then_inc(picked, 1)
                dve.wait_ge(picked, t)
                nc.vector.tensor_tensor(diagonal(t), diagonal(t), fence[:], ALU.min).then_inc(masked, 1)


def band_table():
    import math
    import numpy as np
    d = np.maximum(np.arange(2 * P - 1, -P, -1), 0)
    ratio = np.maximum(d, 16).astype(np.float32) / np.float32(16)
    large = 16 + (np.log(ratio) / np.float32(math.log(128 / 16)) * np.float32(16)).astype(np.int32)
    bucket = np.where(d < 16, d, np.minimum(large, 31))
    table = np.zeros((32, d.size), np.float32)
    table[bucket, np.arange(d.size)] += 1
    table[31] -= 1
    return table


def key_chunks(t):
    w = keys_of(t)
    near = max(0, w - 2 * P)
    return (spans(near) if near else []) + [(near, w)]


def attention_operands(nc, small, chunk_tab, a_log, dt_bias, per_token, whole, ident, qkv_dram, qT, kT, band, rel_bias, table, band_dram, q_norm_w, k_norm_w):
    NB = table.shape[1]
    with ExitStack() as early:
        decay_steps = decays(nc, early, small, chunk_tab, a_log, dt_bias, *per_token, whole)
        esb = lambda name, shape: early.enter_context(nc.sbuf_tensor(name, shape, F32))
        esem = lambda n: early.enter_context(nc.semaphore(n))
        square = esb("square", [P, 2, WA])
        raw = esb("qk_raw", [P, 2 * NT - 1, WA])
        total, logs, rstd = (esb(n, [P, 2 * NT - 1, H]) for n in ("qk_total", "qk_log", "qk_rstd"))
        normed = esb("normed", [P, 2, WA])
        nw, eps = esb("nw", [P, 2]), esb("eps", [P, 1])
        bias_sb, table_sb, row_sb = esb("bias_sb", [32, H]), esb("table_sb", [32, NB]), esb("row_sb", [H, NB])
        flip, band_rev = esb("flip", [P, P]), esb("band_rev", [P, H, 2 * P])
        tr = [early.enter_context(nc.psum_tensor(f"tn{i}", [P, 4, P], F32)) for i in range(2)]
        bp = [early.enter_context(nc.psum_tensor(f"bp{i}", [P, 512], F32)) for i in range(2)]
        loaded, nw_ready, row_ready, row_saved, rev_loaded, row_made, made = (
            esem(n) for n in ("loaded", "nw_ready", "row_ready", "row_saved", "rev_loaded", "row_made", "made"))
        squared, added, logged, rooted, scaled, turned, kept, band_filled, band_kept = (
            esem(n) for n in ("a_squared", "a_added", "a_logged", "a_rooted", "a_scaled", "a_turned", "a_kept",
                              "band_filled", "band_kept"))
        RAW_PARTS = [(1, 1, 0), (5, 1, 4), (NT, 0, 0), (NT + 4, 0, 4)]
        raw_in = [esem(f"raw_in{i}") for i in range(1 + len(RAW_PARTS))]
        units = [(1, kT, i, 1) for i in range(NT)] + [(0, qT, i, 0) for i in range(1, NT)]
        rows = lambda i: META if i == 0 else P
        block = early.enter_context(nc.Block())

        @block.sync
        def _(sp):
            decay_steps["sync"](sp)
            sp.dma_start(bias_sb[:], rel_bias).then_inc(loaded, 16)
            sp.dma_start(table_sb[:], table).then_inc(loaded, 16)
            with nc.allow_non_contiguous_dma(reason="one weight per partition"):
                for j, w in enumerate((q_norm_w, k_norm_w)):
                    for half in range(2):
                        sp.dma_start(nw[DH * half:DH * half + DH, j:j + 1],
                                     w.rearrange("l d -> d l")).then_inc(loaded, 16)
            rest = qkv_dram[:, 1:].rearrange("j t p c -> j p t c")
            sp.dma_start(raw[0:META, 0], qkv_dram[1, 0, PAD:P]).then_inc(raw_in[0], 16)
            for part, (start, j, i) in enumerate(RAW_PARTS):
                sp.dma_start(raw[:, start:start + 4], rest[j, :, i:i + 4]).then_inc(raw_in[1 + part], 16)
            sp.wait_ge(row_ready, 1)
            sp.dma_start(band_dram, row_sb[:]).then_inc(row_saved, 16)
            sp.wait_ge(row_saved, 16)
            for h in range(H):
                src = bass.AP(band_dram.tensor, h * NB, [[1, P], [1, 2 * P]])
                sp.dma_start(band_rev[:, h], src).then_inc(rev_loaded, 16)

        @block.gpsimd
        def _(pool):
            nc.gpsimd.memset(total[:, 0], 1.0).then_inc(made, 1)
            nc.gpsimd.memset(eps[:], EPS).then_inc(made, 1)
            nc.gpsimd.memset(flip[:], 0.0).then_inc(made, 1)
            pool.wait_ge(made, 3)
            nc.gpsimd.affine_select(out=flip[:], in_=flip[:], compare_op=ALU.not_equal, fill=1.0,
                                    base=1 - P, pattern=[[1, P]], channel_multiplier=1).then_inc(made, 1)

        @block.scalar
        def _(act):
            decay_steps["scalar_begin"](act)
            for n, (_, _, i, _) in enumerate(units):
                m = rows(i)
                starts = [0] + [start for start, _, _ in RAW_PARTS]
                if n in starts:
                    act.wait_ge(raw_in[starts.index(n)], 16)
                if n >= 2:
                    act.wait_ge(added, n - 1)
                nc.scalar.activation(square[:m, n % 2], raw[:m, n], ACT.Square).then_inc(squared, 1)
                if n in (NT - 1, len(units) - 1):
                    these = slice(0, NT) if n == NT - 1 else slice(NT, len(units))
                    act.wait_ge(made, 4)
                    act.wait_ge(added, n + 1)
                    nc.scalar.activation(logs[:, these], total[:, these], ACT.Ln, scale=1.0 / DH,
                                         bias=eps[:, 0:1]).then_inc(logged, 1)
                    act.wait_ge(logged, 1 if n == NT - 1 else 2)
                    nc.scalar.activation(rstd[:, these], logs[:, these], ACT.Exp, scale=-0.5).then_inc(rooted, 1)
            decay_steps["scalar_end"](act)

        @block.vector
        def _(dve):
            def add_up(n):
                m = rows(units[n][2])
                dve.wait_ge(squared, n + 1)
                nc.vector.tensor_reduce(total[:m, n], square[:m, n % 2].rearrange("p (h d) -> p h d", d=DH),
                                        AX.X, ALU.add).then_inc(added, 1)

            decay_steps["vector_begin"](dve)
            dve.wait_ge(loaded, 96)
            nc.vector.tensor_scalar(nw[:, 0:1], nw[:, 0:1], DH ** -0.5, None, ALU.mult).then_inc(nw_ready, 1)
            dve.wait_ge(row_made, 1)
            nc.vector.tensor_copy(row_sb[:], bp[0][0:H, 0:NB]).then_inc(row_ready, 1)
            dve.wait_ge(made, 1)
            for n in range(NT):
                add_up(n)
            dve.wait_ge(rooted, 1)
            for n in range(len(units) + 1):
                if n == NT:
                    dve.wait_ge(rooted, 2)
                if NT + n < len(units):
                    add_up(NT + n)
                if n < len(units):
                    _, _, i, _ = units[n]
                    m = rows(i)
                    if n >= 2:
                        dve.wait_ge(turned, n - 1)
                    nc.vector.tensor_tensor(normed[:m, n % 2].rearrange("p (h d) -> p h d", d=DH),
                                            raw[:m, n].rearrange("p (h d) -> p h d", d=DH),
                                            rstd[:m, n].unsqueeze(2).to_broadcast([m, H, DH]),
                                            ALU.mult).then_inc(scaled, 1)
                if n >= 1:
                    _, dst, i, j = units[n - 1]
                    m = rows(i)
                    c = 0 if i == 0 else P * (i - 1) + (META if j == 1 else 0)
                    dve.wait_ge(turned, n)
                    if n == 1:
                        dve.wait_ge(nw_ready, 1)
                    nc.vector.tensor_scalar(dst[:, :, c:c + m], tr[(n - 1) % 2][:, :, 0:m], nw[:, j:j + 1], None,
                                            ALU.mult).then_inc(kept, 1)
            for c in range(4):
                dve.wait_ge(band_filled, c + 1)
                nc.vector.tensor_copy(band[:, 2 * c:2 * c + 2].rearrange("p h j -> p (h j)"),
                                      bp[c % 2][:, :]).then_inc(band_kept, 1)
            decay_steps["vector_end"](dve)

        @block.tensor
        def _(pe):
            pe.wait_ge(loaded, 96)
            nc.tensor.matmul(bp[0][0:H, 0:NB], bias_sb[:], table_sb[:], start=True, stop=True).then_inc(row_made, 1)
            decay_steps["tensor"](pe)
            for n, (_, _, i, _) in enumerate(units):
                m = rows(i)
                pe.wait_ge(scaled, n + 1)
                if n >= 2:
                    pe.wait_ge(kept, n - 1)
                for f in range(4):
                    last = nc.tensor.transpose(tr[n % 2][:, f, 0:m], normed[:m, n % 2, P * f:P * f + P],
                                               ident[:m, :m])
                last.then_inc(turned, 1)
            pe.wait_ge(rev_loaded, 16 * H)
            pe.wait_ge(made, 4)
            pe.wait_ge(row_ready, 1)
            for c in range(4):
                if c >= 2:
                    pe.wait_ge(band_kept, c - 1)
                nc.tensor.matmul(bp[c % 2][:, :], flip[:], band_rev[:, 2 * c:2 * c + 2].rearrange("p h j -> p (h j)"),
                                 start=True, stop=True).then_inc(band_filled, 1)


def attention(nc, ident, score, qT, kT, band, qkv_dram, za_dram, g_dram):
    with ExitStack() as ctx:
        sb = lambda name, shape: ctx.enter_context(nc.sbuf_tensor(name, shape, F32))
        sem = lambda n: ctx.enter_context(nc.semaphore(n))
        hidden = sb("hidden", [P, 4, 2 * P])
        logit, prob, probT = sb("logit", [P, 2, T]), sb("prob", [P, 2, T]), sb("probT", [P, 2, NT, P])
        best, worst, mass, inv = sb("best", [P, 4 * H * NQT]), sb("worst", [P, H * NQT]), sb("mass", [P, H * NQT]), sb("inv", [P, H * NQT])
        gate, mixed, gated = sb("gate", [P, 2, WA]), sb("mixed", [P, 2, WA]), sb("gated", [P, 2, WA])
        LG, PT = 4, 2
        lg = [ctx.enter_context(nc.psum_tensor(f"lg{i}", [P, 512], F32)) for i in range(LG)]
        pt = [ctx.enter_context(nc.psum_tensor(f"pt{i}", [P, 4, P], F32)) for i in range(PT)]
        po = ctx.enter_context(nc.psum_tensor("po", [P, WA], F32))
        pg = ctx.enter_context(nc.psum_tensor("pg", [P, 4, P], F32))
        (near_ready, logit_made, logit_read, negated, exped, turned, kept, mixed_up, divided, out_ready, gated_up,
         g_turned, g_kept) = (sem(n) for n in (
            "near_ready", "logit_made", "logit_read", "negated", "exped", "p_turned", "p_kept", "mixed_up", "divided",
            "out_ready", "gated_up", "g_turned", "g_kept"))
        gate_loaded = [sem("gate_loaded0"), sem("gate_loaded1")]
        gT, g_saved = sb("gT", [P, 4, SEQ]), sem("g_saved")
        va, va_loaded = sb("va", [P, NT, WA]), sem("va_loaded")
        units = [(t, h) for t in range(NQT) for h in range(H)]
        chunks_to = [0]
        groups_to = [0]
        for t, h in units:
            chunks_to.append(chunks_to[-1] + len(key_chunks(t)))
            groups_to.append(groups_to[-1] + -(-(t + 2) // 4))
        key_rows = lambda b: META if b == 0 else P
        key_col = lambda b: 0 if b == 0 else META + P * (b - 1)
        block = ctx.enter_context(nc.Block())

        @block.sync
        def _(sp):
            sp.dma_start(va[0:META, 0], qkv_dram[2, 0, PAD:P]).then_inc(va_loaded, 16)
            sp.dma_start(va[:, 1:], qkv_dram[2, 1:].rearrange("t p c -> p t c")).then_inc(va_loaded, 16)
            for t in range(NQT):
                if t >= 2:
                    sp.wait_ge(gated_up, t - 1)
                sp.dma_start(gate[:, t % 2], za_dram[t]).then_inc(gate_loaded[t % 2], 16)
            sp.wait_ge(g_kept, NQT)
            sp.dma_start(g_dram.rearrange("k p t -> p k t"), gT[:]).then_inc(g_saved, 16)
            sp.wait_ge(g_saved, 16)

        @block.gpsimd
        def _(pool):
            for n, (t, h) in enumerate(units):
                a, b = key_chunks(t)[-1]
                if n >= 4:
                    pool.wait_ge(logit_read, chunks_to[n - 3])
                nc.gpsimd.tensor_tensor(hidden[:, n % 4, 0:b - a], score[t][:, a:b], band[:, h, 2 * P - (b - a):2 * P],
                                        ALU.add).then_inc(near_ready, 1)

        @block.tensor
        def _(pe):
            def logits(n):
                t, h = units[n]
                r = slice(DH * (h % 2), DH * (h % 2) + DH)
                for c, (a, b) in enumerate(key_chunks(t)):
                    m = chunks_to[n] + c
                    if m >= LG:
                        pe.wait_ge(logit_read, m - LG + 1)
                    nc.tensor.matmul(lg[m % LG][:, 0:b - a], qT[r, h // 2, P * t:P * t + P], kT[r, h // 2, a:b],
                                     start=True, stop=True).then_inc(logit_made, 1)

            def turn(n):
                t, h = units[n]
                pe.wait_ge(exped, n + 1)
                for g in range(groups_to[n + 1] - groups_to[n]):
                    m = groups_to[n] + g
                    if m >= PT:
                        pe.wait_ge(kept, m - PT + 1)
                    for b in range(4 * g, min(4 * g + 4, t + 2)):
                        k, c = key_rows(b), key_col(b)
                        last = nc.tensor.transpose(pt[m % PT][0:k, b - 4 * g, :], prob[:, n % 2, c:c + k], ident[:])
                    last.then_inc(turned, 1)

            def mix(n):
                t, h = units[n]
                if n == 0:
                    pe.wait_ge(va_loaded, 32)
                pe.wait_ge(kept, groups_to[n + 1])
                if h == 0 and t >= 1:
                    pe.wait_ge(divided, t)
                for b in range(t + 2):
                    k = key_rows(b)
                    last = nc.tensor.matmul(po[:, DH * h:DH * h + DH], probT[0:k, n % 2, b, :],
                                            va[0:k, b, DH * h:DH * h + DH], start=(b == 0), stop=(b == t + 1))
                last.then_inc(mixed_up, 1)

            def turn_gated(t):
                pe.wait_ge(gated_up, t + 1)
                if t >= 1:
                    pe.wait_ge(g_kept, t)
                for f in range(4):
                    last = nc.tensor.transpose(pg[:, f, :], gated[:, t % 2, P * f:P * f + P], ident[:])
                last.then_inc(g_turned, 1)

            for _ in range(7):
                nc.tensor.matmul(pg[:].rearrange("p f i -> p (f i)"), ident[:], kT[:, 0, 0:512], start=True, stop=True)
            logits(0)
            for n in range(len(units) + 3):
                if n + 1 < len(units):
                    logits(n + 1)
                if 1 <= n <= len(units):
                    turn(n - 1)
                if 2 <= n <= len(units) + 1:
                    mix(n - 2)
                if n >= 12 and (n - 12) % H == 0 and (n - 12) // H < NQT - 1:
                    turn_gated((n - 12) // H)
            turn_gated(NQT - 1)

        @block.vector
        def _(dve):
            def masked_max(n):
                t, h = units[n]
                chunks = key_chunks(t)
                if n >= 2:
                    dve.wait_ge(exped, n - 1)
                for c, (a, b) in enumerate(chunks):
                    m = chunks_to[n] + c
                    near = c == len(chunks) - 1
                    dve.wait_ge(logit_made, m + 1)
                    if near:
                        dve.wait_ge(near_ready, n + 1)
                    if c:
                        dve.wait_ge(logit_read, m)
                    nc.vector.tensor_tensor_reduce(
                        out=logit[:, n % 2, a:b], in0=lg[m % LG][:, 0:b - a],
                        in1=hidden[:, n % 4, 0:b - a] if near else score[t][:, a:b],
                        scale=1.0, scalar=best[:, 4 * n + c - 1:4 * n + c] if c else -3.0e38, op0=ALU.add, op1=ALU.max,
                        accum_out=best[:, 4 * n + c:4 * n + c + 1]).then_inc(logit_read, 1)
                dve.wait_ge(logit_read, chunks_to[n + 1])
                c = 4 * n + len(chunks) - 1
                nc.vector.tensor_scalar(worst[:, n:n + 1], best[:, c:c + 1], -1.0, None, ALU.mult).then_inc(negated, 1)

            def finish(t):
                dve.wait_ge(exped, H * t + H)
                nc.vector.reciprocal(inv[:, H * t:H * t + H], mass[:, H * t:H * t + H]).then_inc(out_ready, 1)
                dve.wait_ge(out_ready, t + 1)
                dve.wait_ge(mixed_up, H * t + H)
                nc.vector.tensor_tensor(mixed[:, t % 2].rearrange("p (h d) -> p h d", d=DH),
                                        po[:].rearrange("p (h d) -> p h d", d=DH),
                                        inv[:, H * t:H * t + H].unsqueeze(2).to_broadcast([P, H, DH]),
                                        ALU.mult).then_inc(divided, 1)
                dve.wait_ge(divided, t + 1)
                dve.wait_ge(gate_loaded[t % 2], 16 * (t // 2 + 1))
                if t >= 2:
                    dve.wait_ge(g_turned, t - 1)
                nc.vector.tensor_tensor(gated[:, t % 2], mixed[:, t % 2], gate[:, t % 2],
                                        ALU.mult).then_inc(gated_up, 1)

            for n in range(len(units)):
                masked_max(n)
                if n >= 10 and (n - 10) % H == 0:
                    finish((n - 10) // H)
            finish(NQT - 1)

        @block.scalar
        def _(act):
            def exp(n):
                t, h = units[n]
                w = keys_of(t)
                act.wait_ge(negated, n + 1)
                if n >= 2:
                    act.wait_ge(turned, groups_to[n - 1])
                nc.scalar.activation(prob[:, n % 2, 0:w], logit[:, n % 2, 0:w], ACT.Exp, bias=worst[:, n:n + 1],
                                     accum_out=mass[:, n:n + 1]).then_inc(exped, 1)

            def keep(n):
                t, h = units[n]
                if n >= 2:
                    act.wait_ge(mixed_up, n - 1)
                for g in range(groups_to[n + 1] - groups_to[n]):
                    m = groups_to[n] + g
                    act.wait_ge(turned, m + 1)
                    lo, hi = 4 * g, min(4 * g + 4, t + 2)
                    if g == 0:
                        nc.scalar.activation(probT[0:META, n % 2, 0, :], pt[m % PT][0:META, 0, :], ACT.Copy)
                        lo = 1
                    nc.scalar.activation(probT[:, n % 2, lo:hi, :], pt[m % PT][:, lo - 4 * g:hi - 4 * g, :],
                                         ACT.Copy).then_inc(kept, 1)

            def keep_gated(t):
                act.wait_ge(g_turned, t + 1)
                nc.scalar.activation(gT[:, :, P * t:P * t + P], pg[:], ACT.Copy).then_inc(g_kept, 1)

            for n in range(len(units) + 1):
                if n < len(units):
                    exp(n)
                if n >= 1:
                    keep(n - 1)
                if n >= 13 and (n - 13) % H == 0 and (n - 13) // H < NQT - 1:
                    keep_gated((n - 13) // H)
            keep_gated(NQT - 1)


def chunk_table():
    import numpy as np
    i, j = np.arange(P)[:, None], np.arange(P)[None, :]
    same = i // CHUNK == j // CHUNK
    parts = [same & (i <= j), same, (i < CHUNK) & (j >= 0), (i >= CHUNK) & (j >= 0)]
    table = [p.astype(np.float32) for p in parts]
    for l in range(6):
        table.append(np.eye(P, dtype=np.float32) - ((i >> l) % 2 == 1) * ((i >> l) - 1 == j >> l))
    return np.ascontiguousarray(np.stack(table, 1)).astype(np.float32)


def decays(nc, ctx, small, chunk_tab, a_log, dt_bias, beta, nbeta, gates, gsum, to_here, to_end, whole):
    sb = lambda name, shape: ctx.enter_context(nc.sbuf_tensor(name, shape, F32))
    sem = lambda n: ctx.enter_context(nc.semaphore(n))
    alog, dtb, nega = sb("alog", [P, H]), sb("dtb", [P, H]), sb("nega", [P, H])
    z, mag, e, ln, pos = (sb(n, [P, NT, H]) for n in ("z", "mag", "e", "ln", "pos"))
    chunk_sums = sb("chunk_sums", [P, 4, P])
    sums = ctx.enter_context(nc.psum_tensor("sums", [P, 4, NT * H], F32))
    vectors_loaded, chunk_loaded = sem("vectors_loaded"), sem("chunk_loaded")
    decay_dve, decay_act, decay_pe = sem("decay_dve"), sem("decay_act"), sem("decay_pe")

    def sync(sp):
        sp.dma_start(alog[:], a_log.to_broadcast([P, H])).then_inc(vectors_loaded, 16)
        sp.dma_start(dtb[:], dt_bias.to_broadcast([P, H])).then_inc(vectors_loaded, 16)
        sp.dma_start(chunk_sums[:], chunk_tab[:, 0:4]).then_inc(chunk_loaded, 16)

    def scalar_begin(act):
        nc.scalar.activation(beta[:], small[:, :, H:2 * H], ACT.Sigmoid).then_inc(decay_act, 1)
        act.wait_ge(vectors_loaded, 32)
        nc.scalar.activation(nega[:], alog[:], ACT.Exp).then_inc(decay_act, 1)
        act.wait_ge(decay_dve, 1)
        nc.scalar.activation(mag[:], z[:], ACT.Abs).then_inc(decay_act, 1)
        act.wait_ge(decay_act, 3)
        nc.scalar.activation(e[:], mag[:], ACT.Exp, scale=-1.0).then_inc(decay_act, 1)
        act.wait_ge(decay_dve, 2)
        nc.scalar.activation(ln[:], mag[:], ACT.Ln).then_inc(decay_act, 1)

    def scalar_end(act):
        act.wait_ge(decay_dve, 8)
        nc.scalar.activation(to_here[:], gsum[:], ACT.Exp).then_inc(decay_act, 1)
        nc.scalar.activation(to_end[:], z[:], ACT.Exp).then_inc(decay_act, 1)
        nc.scalar.activation(whole[:], sums[:, 2:4].rearrange("p c (t h) -> p c t h", h=H), ACT.Exp).then_inc(decay_act, 1)

    def vector_begin(dve):
        dve.wait_ge(vectors_loaded, 32)
        nc.vector.tensor_tensor(z[:], small[:, :, 2 * H:3 * H],
                                dtb[:].unsqueeze(1).to_broadcast([P, NT, H]), ALU.add).then_inc(decay_dve, 1)
        dve.wait_ge(decay_act, 4)
        nc.vector.tensor_scalar(mag[:], e[:], 1.0, None, ALU.add).then_inc(decay_dve, 1)
        nc.vector.tensor_scalar(pos[:], z[:], 0.0, None, ALU.max).then_inc(decay_dve, 1)
        nc.vector.tensor_scalar(nbeta[:], beta[:], -1.0, None, ALU.mult).then_inc(decay_dve, 1)
        dve.wait_ge(decay_act, 5)
        dve.wait_ge(decay_dve, 3)
        nc.vector.tensor_tensor(e[:], ln[:], pos[:], ALU.add).then_inc(decay_dve, 1)
        dve.wait_ge(decay_dve, 5)
        nc.vector.scalar_tensor_tensor(gates[:], e[:], -1.0, nega[:].unsqueeze(1).to_broadcast([P, NT, H]),
                                       ALU.mult, ALU.mult).then_inc(decay_dve, 1)

    def vector_end(dve):
        dve.wait_ge(decay_pe, 1)
        nc.vector.tensor_copy(gsum[:], sums[:, 0].rearrange("p (t h) -> p t h", h=H)).then_inc(decay_dve, 1)
        dve.wait_ge(decay_dve, 7)
        nc.vector.tensor_tensor(z[:], sums[:, 1].rearrange("p (t h) -> p t h", h=H), gsum[:],
                                ALU.subtract).then_inc(decay_dve, 1)

    def tensor(pe):
        pe.wait_ge(chunk_loaded, 16)
        pe.wait_ge(decay_dve, 6)
        for c in range(4):
            last = nc.tensor.matmul(sums[:, c], chunk_sums[:, c], gates[:].rearrange("p t h -> p (t h)"),
                                    start=True, stop=True)
        last.then_inc(decay_pe, 1)

    return {"sync": sync, "scalar_begin": scalar_begin, "scalar_end": scalar_end, "vector_begin": vector_begin,
            "vector_end": vector_end, "tensor": tensor}


GROUPS, GT = 3, 3
GW = GT * P
LEVELS = 6
CHUNKS = 2 * NT
STEPS = CHUNKS - 1


def delta_plan():
    fill = lambda h, l, *whats: [("fill", (x, h, l, g)) for x in whats for g in range(GROUPS)]

    def solve(h):
        items = fill(h, 0, "kk", "at", "vt", "kt")
        for l in range(LEVELS):
            items += fill(h, l, "Q", "W")
        return items + fill(h, 0, "wT", "u")

    def begin(h):
        items = [(22, ("squares", h, 0)), (25, ("squares", h, 1))] + list(zip((26, 28, 30), fill(h, 0, "grow"))) + [(34, ("differences", h))]
        items += list(zip((34, 36, 38, 40, 42, 44), fill(h, 0, "sum_k", "sum_q")))
        items += [(p, ("exponential", h, i)) for i, p in enumerate((45, 47, 49, 51))]
        return items + [(50, ("normalise", h, 0)), (53, ("normalise", h, 1))]

    def end(h):
        return [(1, ("out_squares", h)), (5, ("out_root", h)), (10, ("out_gate", h))] + [
            (18, ("fill", ("post", h, 0, g))) for g in range(2)]

    only = lambda placed: [item for _, item in placed]
    plan = only(begin(0)) + [("decay_queries", 0)] + solve(0) + only(begin(1))
    for h in range(H):
        placed = end(h - 1) if h >= 1 else []
        if h + 1 < H:
            placed.append((3, ("decay_queries", h + 1)))
            placed += list(enumerate(solve(h + 1)))
        if h + 2 < H:
            placed += begin(h + 2)
        between = only(sorted(placed, key=lambda x: x[0]))
        at = 0
        for n in range(STEPS):
            for i, half in enumerate(("state", "update")):
                plan.append((half, h, n))
                upto = len(between) * (2 * n + i + 1) // (2 * STEPS)
                plan += between[at:upto]
                at = upto
    return plan + only(end(H - 1))


def delta_heads(nc, conv_dram, gdn_norm_w, ident, ones, chunk_tab, beta, nbeta, gates, gsum, to_here, to_end,
                whole, zb_dram, og_dram, early_loads):
    PK, PQ, PV = range(3)
    with ExitStack() as ctx:
        sb = lambda name, shape: ctx.enter_context(nc.sbuf_tensor(name, shape, F32))
        sem = lambda n: ctx.enter_context(nc.semaphore(n))
        chunk = sb("chunk", [P, 10, P])
        ys, sq = sb("ys", [P, 3, TP]), sb("sq", [P, 2, TP])
        rk, rq = sb("rk", [P, TP]), sb("rq", [P, TP])
        grow, LA, LB = sb("grow", [P, TP]), sb("LA", [P, TP]), sb("LB", [P, TP])
        tiled = lambda name: sb(name, [P, NT, P])
        kt, ke, vt, U, W, X, R = (tiled(n) for n in ("kt", "ke", "vt", "U", "W", "X", "R"))
        twice = lambda name: [tiled(name + "0"), tiled(name + "1")]
        kd, at, u, o = (twice(n) for n in ("kd", "at", "u", "o"))
        wq = [sb(f"wq{i}", [P, NT, 4, CHUNK]) for i in range(2)]
        vnew, S = sb("vnew", [P, 2, P]), sb("S", [P, 2, P])
        zb, osq = sb("zb_head", [P, NQT, P]), sb("osq", [P, NQT, P])
        ovar, oln, orstd = sb("ovar", [P, NQT]), sb("oln", [P, NQT]), sb("orstd", [P, NQT])
        og = sb("og_head", [P, SEQ])
        gw, consts = sb("gw", [P, 1]), sb("consts", [P, 3])
        so = [ctx.enter_context(nc.psum_tensor(f"so{i}", [P, P], F32)) for i in range(2)]
        skv = ctx.enter_context(nc.psum_tensor("skv", [P, P], F32))
        WB = 5
        wk = [ctx.enter_context(nc.psum_tensor(f"wk{i}", [P, 512], F32)) for i in range(WB)]

        plan = delta_plan()
        fills = [item[1] for item in plan if item[0] == "fill"]
        by_dve = ("kk", "at", "Q", "u")
        place, read_no, counts = {}, {}, [0, 0]
        for n, key in enumerate(fills):
            counts[key[0] in by_dve] += 1
            place[key], read_no[key] = n, counts[key[0] in by_dve]

        (worked, read_act, read_dve) = (sem(n) for n in ("worked", "read_act", "read_dve"))
        (const_made, zeroed, gw_loaded, y_loaded, squared, rooted, normed, ldiff, growexp, lexp, lmasked, lbeta, udiag,
         kscaled, qdec, x_turned) = (sem(n) for n in (
            "const_made", "zeroed", "gw_loaded", "y_loaded", "squared", "rooted", "normed", "ldiff", "growexp",
            "lexp", "lmasked", "lbeta", "udiag", "kscaled", "qdec", "x_turned"))
        (s_made, v_new, kv_made, o_made, s_kept, o_kept, o_squared, o_summed, o_ln, o_root, o_scaled, z_loaded,
         og_saved) = (sem(n) for n in (
            "s_made", "v_new", "kv_made", "o_made", "s_kept", "o_kept", "o_squared", "o_summed", "o_ln", "o_root",
            "o_scaled", "z_loaded", "og_saved"))
        chunk_in = sem("chunk_in")
        block = ctx.enter_context(nc.Block())

        def read(eng, key):
            eng.wait_ge(read_dve if key[0] in by_dve else read_act, read_no[key])

        def bank_of(key):
            return wk[place[key] % WB]

        def by_tile(ap):
            return ap.rearrange("p (t i) -> p t i", i=P)

        def group(x, g):
            return x[:, GT * g:GT * g + GT]

        def chunk_at(n):
            t, half = divmod(n + 1, 2)
            return t, half, slice(CHUNK * half, CHUNK * half + CHUNK), slice(CHUNK * (1 - half), CHUNK * (2 - half))

        x_no = lambda h, l, g: GROUPS * ((LEVELS - 2) * h + l - 1) + g + 1

        @block.sync
        def _(sp):
            with nc.allow_non_contiguous_dma(reason="one weight per partition"):
                sp.dma_start(gw[:], gdn_norm_w.rearrange("l d -> d l")).then_inc(gw_loaded, 16)
            sp.dma_start(chunk[:], chunk_tab).then_inc(chunk_in, 16)
            for h in range(H):
                if h >= 1:
                    read(sp, ("at", h - 1, 0, GROUPS - 1))
                    read(sp, ("kk", h - 1, 0, GROUPS - 1))
                    read(sp, ("kt", h - 1, 0, GROUPS - 1))
                    sp.wait_ge(qdec, h)
                sp.dma_start(ys[:, :, PAD:TP], conv_dram[:, h].rearrange("j p t -> p j t")).then_inc(y_loaded, 16)
            for dst, src, loaded in early_loads:
                sp.dma_start(dst, src).then_inc(loaded, 16)

        @block.gpsimd
        def _(pool):
            nc.gpsimd.memset(consts[:, 0:1], EPS)
            nc.gpsimd.memset(consts[:, 1:2], 0.0)
            nc.gpsimd.memset(consts[:, 2:3], -0.5 * math.log(DK)).then_inc(const_made, 1)
            nc.gpsimd.memset(ys[:, :, 0:PAD], 0.0).then_inc(zeroed, 1)
            pool.wait_ge(chunk_in, 16)
            tri = chunk[:, 0:1].to_broadcast([P, NT, P])
            for h in range(H):
                pool.wait_ge(lexp, h + 1)
                nc.gpsimd.tensor_tensor(by_tile(LA[:]), by_tile(LA[:]), tri, ALU.mult).then_inc(lmasked, 1)
                pool.wait_ge(lmasked, h + 1)
                nc.gpsimd.tensor_tensor(by_tile(LB[:]), by_tile(LA[:]), beta[:, :, h:h + 1].to_broadcast([P, NT, P]),
                                        ALU.mult).then_inc(lbeta, 1)
                for g in range(GROUPS):
                    read(pool, ("kk", h, 0, g))
                    nc.gpsimd.affine_select(out=group(U, g), in_=group(U, g), compare_op=ALU.not_equal, fill=1.0,
                                            base=0, pattern=[[0, GT], [-1, P]], channel_multiplier=1).then_inc(udiag, 1)
                read(pool, ("kt", h, 0, GROUPS - 1))
                if h >= 2:
                    pool.wait_ge(kv_made, STEPS * (h - 1))
                if h >= 1:
                    read(pool, ("wT", h - 1, 0, GROUPS - 1))
                for dst, by in ((ke, to_here), (kd[h % 2], to_end)):
                    nc.gpsimd.tensor_tensor(dst[:], kt[:], by[:, :, h:h + 1].to_broadcast([P, NT, P]),
                                            ALU.mult).then_inc(kscaled, 1)

        @block.tensor
        def _(pe):
            def fill(key):
                what, h, l, g = key
                n = place[key]
                bank, out = bank_of(key), bank_of(key)[:, 0:GW]
                tiles = list(enumerate(range(GT * g, GT * g + GT)))
                if n >= WB:
                    read(pe, fills[n - WB])
                if what == "grow":
                    for i, t in tiles:
                        last = nc.tensor.matmul(out[:, P * i:P * i + P], gates[:, t, h:h + 1].to_broadcast([P, P]),
                                                chunk[:, 0], start=True, stop=True)
                elif what in ("sum_k", "sum_q"):
                    j = int(what == "sum_q")
                    pe.wait_ge(squared, 2 * h + 1 + j)
                    last = nc.tensor.matmul(out, ones[:], sq[:, j, GW * g:GW * g + GW], start=True, stop=True)
                elif what == "post":
                    pe.wait_ge(o_scaled, 2 * h + 2)
                    for i in range(4):
                        last = nc.tensor.transpose(bank[:, P * i:P * i + P], o[h % 2][:, 1 + 4 * g + i], ident[:])
                elif what in ("kk", "at"):
                    pe.wait_ge(normed, 2 * h + 1 + (what == "at"))
                    for i, t in tiles:
                        last = nc.tensor.matmul(out[:, P * i:P * i + P], ys[:, PK, P * t:P * t + P],
                                                ys[:, PK if what == "kk" else PQ, P * t:P * t + P], start=True, stop=True)
                elif what in ("kt", "vt"):
                    if what == "kt":
                        pe.wait_ge(normed, 2 * h + 1)
                    for i, t in tiles:
                        last = nc.tensor.transpose(out[:, P * i:P * i + P],
                                                   ys[:, PK if what == "kt" else PV, P * t:P * t + P], ident[:])
                elif what == "Q":
                    if l == 0:
                        pe.wait_ge(udiag, GROUPS * h + g + 1)
                    elif l == 1:
                        read(pe, ("Q", h, 0, g))
                    else:
                        pe.wait_ge(x_turned, x_no(h, l - 1, g))
                    for i, t in tiles:
                        x = ident[:] if l == 0 else R[:, t] if l == 1 else X[:, t]
                        last = nc.tensor.matmul(out[:, P * i:P * i + P], U[:, t], x, start=True, stop=True)
                elif what == "W":
                    read(pe, ("Q", h, l, g))
                    if l:
                        read(pe, ("W", h, l - 1, g))
                    for i, t in tiles:
                        last = nc.tensor.matmul(out[:, P * i:P * i + P], R[:, t], W[:, t] if l else ident[:],
                                                start=True, stop=True)
                elif what == "wT":
                    read(pe, ("W", h, LEVELS - 1, g))
                    pe.wait_ge(kscaled, 2 * h + 1)
                    for i, t in tiles:
                        last = nc.tensor.matmul(out[:, P * i:P * i + P], ke[:, t], W[:, t], start=True, stop=True)
                elif what == "u":
                    read(pe, ("vt", h, 0, g))
                    for i, t in tiles:
                        last = nc.tensor.matmul(out[:, P * i:P * i + P], W[:, t], vt[:, t], start=True, stop=True)
                last.then_inc(worked, 1)

            def state(h, n):
                t, half, _, _ = chunk_at(n)
                m = STEPS * h + n
                if n == 0:
                    read(pe, ("wT", h, 0, GROUPS - 1))
                    pe.wait_ge(qdec, h + 1)
                if m >= 2:
                    pe.wait_ge(o_kept, m - 1)
                pe.wait_ge(s_kept, m + h + 1)
                nc.tensor.matmul(so[m % 2][:], wq[h % 2][:, t, 2 * half:2 * half + 2].rearrange("p a b -> p (a b)"),
                                 S[:, n % 2], start=True, stop=True, skip_group_check=True).then_inc(s_made, 1)

            def update(h, n):
                t, half, r, r2 = chunk_at(n)
                m = STEPS * h + n
                if n == 0:
                    pe.wait_ge(kscaled, 2 * h + 2)
                    read(pe, ("at", h, 0, GROUPS - 1))
                pe.wait_ge(v_new, m + 1)
                nc.tensor.matmul(skv[:], kd[h % 2][r, t], vnew[r, n % 2], start=True, stop=True).then_inc(kv_made, 1)
                nc.tensor.matmul(so[m % 2][r2], at[h % 2][r, t, r], vnew[r, n % 2],
                                 start=False, stop=True, skip_group_check=True).then_inc(o_made, 1)

            pe.wait_ge(chunk_in, 16)
            for item in plan:
                if item[0] == "fill":
                    fill(item[1])
                elif item[0] == "state":
                    state(*item[1:])
                elif item[0] == "update":
                    update(*item[1:])

        @block.vector
        def _(dve):
            def differences(h):
                read(dve, ("grow", h, 0, GROUPS - 1))
                if h >= 1:
                    dve.wait_ge(lbeta, h)
                for t in range(NT):
                    last = nc.vector.tensor_scalar(LA[:, P * t:P * t + P], grow[:, P * t:P * t + P],
                                                   gsum[:, t, h:h + 1], 0.0, ALU.subtract, ALU.min)
                last.then_inc(ldiff, 1)

            def normalise(h, i):
                j, r = ((PK, rk), (PQ, rq))[i]
                dve.wait_ge(rooted, 2 * h + i + 1)
                nc.vector.tensor_tensor(ys[:, j], ys[:, j], r[:], ALU.mult).then_inc(normed, 1)

            def decay_queries(h):
                dve.wait_ge(growexp, h + 1)
                dve.wait_ge(normed, 2 * h + 2)
                if h >= 2:
                    dve.wait_ge(s_made, STEPS * (h - 1))
                nc.vector.tensor_tensor(wq[h % 2][:, :, 1:3].rearrange("p t a b -> p t (a b)"), by_tile(ys[:, PQ]),
                                        by_tile(grow[:]), ALU.mult).then_inc(qdec, 1)

            def take(key):
                what, h, l, g = key
                src = by_tile(bank_of(key)[:, 0:GW])
                if what == "kk":
                    dve.wait_ge(lbeta, h + 1)
                    dst, by = group(U, g), by_tile(LB[:, GW * g:GW * g + GW])
                elif what == "at":
                    dve.wait_ge(lmasked, h + 1)
                    if h >= 2:
                        dve.wait_ge(o_made, STEPS * (h - 1))
                    dst, by = group(at[h % 2], g), by_tile(LA[:, GW * g:GW * g + GW])
                elif what == "Q":
                    dst, by = group(R, g), chunk[:, 4 + l:5 + l].to_broadcast([P, GT, P])
                    if h >= 1 and l == 0:
                        dve.wait_ge(worked, place["W", h - 1, LEVELS - 1, g] + 1)
                else:
                    if h >= 2:
                        dve.wait_ge(v_new, STEPS * (h - 1))
                    dst, by = group(u[h % 2], g), group(beta, g)[:, :, h:h + 1].to_broadcast([P, GT, P])
                dve.wait_ge(worked, place[key] + 1)
                nc.vector.tensor_tensor(dst, src, by, ALU.mult).then_inc(read_dve, 1)

            def turn(h, l, g):
                read(dve, ("W", h, l, g))
                flat = lambda x: group(x, g).rearrange("p t i -> p (t i)")
                nc.vector.transpose(flat(X), flat(W)).then_inc(x_turned, 1)

            def state(h, n):
                t, half, r, _ = chunk_at(n)
                m = STEPS * h + n
                dve.wait_ge(s_made, m + 1)
                if n == 0:
                    read(dve, ("u", h, 0, GROUPS - 1))
                nc.vector.scalar_tensor_tensor(vnew[r, n % 2], so[m % 2][r, :], nbeta[r, t, h:h + 1], u[h % 2][r, t],
                                               ALU.mult, ALU.add).then_inc(v_new, 1)

            def update(h, n):
                t, half, _, _ = chunk_at(n)
                m = STEPS * h + n
                dve.wait_ge(kv_made, m + 1)
                dve.wait_ge(s_kept, m + h + 1)
                nc.vector.scalar_tensor_tensor(S[:, (n + 1) % 2], S[:, n % 2], whole[:, half, t, h:h + 1], skv[:],
                                               ALU.mult, ALU.add).then_inc(s_kept, 1)
                if n == STEPS - 1 and h + 1 < H:
                    dve.wait_ge(s_kept, m + h + 2)
                    nc.vector.memset(S[:, 0], 0.0).then_inc(s_kept, 1)

            def out_squares(h):
                dve.wait_ge(o_squared, h + 1)
                nc.vector.tensor_reduce(ovar[:], osq[:], AX.X, ALU.add).then_inc(o_summed, 1)

            def out_gate(h):
                x = o[h % 2][:, 1:]
                dve.wait_ge(o_root, h + 1)
                nc.vector.tensor_tensor(x, x, orstd[:].unsqueeze(2).to_broadcast([P, NQT, P]),
                                        ALU.mult).then_inc(o_scaled, 1)
                dve.wait_ge(o_scaled, 2 * h + 1)
                dve.wait_ge(z_loaded, 32 * h + 32)
                nc.vector.tensor_tensor(x, x, zb[:], ALU.mult).then_inc(o_scaled, 1)

            dve.wait_ge(chunk_in, 16)
            nc.vector.memset(S[:, 0], 0.0).then_inc(s_kept, 1)
            for item in plan:
                if item[0] == "differences":
                    differences(item[1])
                elif item[0] == "normalise":
                    normalise(*item[1:])
                elif item[0] == "decay_queries":
                    decay_queries(item[1])
                elif item[0] == "out_squares":
                    out_squares(item[1])
                elif item[0] == "out_gate":
                    out_gate(item[1])
                elif item[0] == "state":
                    state(*item[1:])
                elif item[0] == "update":
                    update(*item[1:])
                elif item[0] == "fill":
                    what, h, l, g = key = item[1]
                    if what in by_dve:
                        take(key)
                    elif what == "W" and 0 < l < LEVELS - 1:
                        turn(h, l, g)

        @block.scalar
        def _(act):
            def squares(h, i):
                j = (PK, PQ)[i]
                act.wait_ge(y_loaded, 16 * h + 16)
                if h >= 1:
                    act.wait_ge(worked, place["sum_q", h - 1, 0, GROUPS - 1] + 1)
                nc.scalar.activation(sq[:, j], ys[:, j], ACT.Square).then_inc(squared, 1)

            def exponential(h, i):
                if i < 2:
                    r = (rk, rq)[i]
                    read(act, (("sum_k", "sum_q")[i], h, 0, GROUPS - 1))
                    nc.scalar.activation(r[:], r[:], ACT.Exp, scale=-0.5, bias=consts[:, 1 + i:2 + i]).then_inc(rooted, 1)
                    return
                act.wait_ge(ldiff, h + 1)
                if i == 2:
                    nc.scalar.activation(LA[:], LA[:], ACT.Exp).then_inc(lexp, 1)
                else:
                    nc.scalar.activation(grow[:], grow[:], ACT.Exp).then_inc(growexp, 1)

            def take(key):
                what, h, l, g = key
                bank = bank_of(key)[:, 0:GW]
                flat = slice(GW * g, GW * g + GW)
                func, more = ACT.Copy, {}
                if what == "grow":
                    dst = grow[:, flat]
                    if h >= 1:
                        act.wait_ge(qdec, h)
                elif what in ("sum_k", "sum_q"):
                    dst, func, more = (rk if what == "sum_k" else rq)[:, flat], ACT.Ln, {"bias": consts[:, 0:1]}
                    if h >= 1:
                        act.wait_ge(normed, 2 * h)
                elif what == "wT":
                    dst, bank = group(wq[h % 2], g)[:, :, 0:4:3], bank.rearrange("p (t a b) -> p t a b", t=GT, a=2)
                    if h >= 2:
                        act.wait_ge(s_made, STEPS * (h - 1))
                else:
                    dst, bank = group({"kt": kt, "vt": vt, "W": W}[what], g), by_tile(bank)
                    if what == "kt" and h >= 1:
                        act.wait_ge(kscaled, 2 * h)
                    if what == "vt" and h >= 1:
                        act.wait_ge(worked, place["u", h - 1, 0, g] + 1)
                    if what == "W" and l >= 2:
                        act.wait_ge(x_turned, x_no(h, l - 1, g))
                act.wait_ge(worked, place[key] + 1)
                nc.scalar.activation(dst, bank, func, **more).then_inc(read_act, 1)

            def take_post(key):
                _, h, _, g = key
                if h >= 1 and g == 0:
                    act.wait_ge(og_saved, 16 * h)
                act.wait_ge(worked, place[key] + 1)
                src = bank_of(key)[:].rearrange("p (t a b) -> p t a b", t=4, a=2)
                dst = og[:, 512 * g:512 * g + 512].rearrange("p (t a b) -> p t a b", t=4, a=2)
                nc.scalar.activation(dst[:, :, 0], src[:, :, 1], ACT.Copy, scale=gw[:, 0:1])
                nc.scalar.activation(dst[:, :, 1], src[:, :, 0], ACT.Copy, scale=gw[:, 0:1]).then_inc(read_act, 1)
                if g == 1:
                    read(act, key)
                    act.dma_start(og_dram[h], og[:]).then_inc(og_saved, 16)
                    if h + 1 < H:
                        load_z(h + 1)

            def load_z(h):
                for half in range(2):
                    src = zb_dram[:, CHUNK * (1 - half):CHUNK * (2 - half), P * h:P * h + P].rearrange("t p c -> p t c")
                    act.dma_start(zb[CHUNK * half:CHUNK * half + CHUNK], src).then_inc(z_loaded, 16)

            def out_squares(h):
                act.wait_ge(o_kept, STEPS * (h + 1))
                if h >= 1:
                    act.wait_ge(o_summed, h)
                nc.scalar.activation(osq[:], o[h % 2][:, 1:], ACT.Square).then_inc(o_squared, 1)

            def out_root(h):
                act.wait_ge(o_summed, h + 1)
                nc.scalar.activation(oln[:], ovar[:], ACT.Ln, scale=1.0 / DK, bias=consts[:, 0:1]).then_inc(o_ln, 1)
                act.wait_ge(o_ln, h + 1)
                nc.scalar.activation(orstd[:], oln[:], ACT.Exp, scale=-0.5).then_inc(o_root, 1)

            def keep_o(h, n):
                t, _, _, r2 = chunk_at(n)
                m = STEPS * h + n
                if n == 0 and h >= 2:
                    read(act, ("post", h - 2, 0, 1))
                act.wait_ge(o_made, m + 1)
                nc.scalar.activation(o[h % 2][r2, t], so[m % 2][r2, :], ACT.Copy).then_inc(o_kept, 1)

            act.wait_ge(const_made, 1)
            act.wait_ge(zeroed, 1)
            act.wait_ge(gw_loaded, 16)
            load_z(0)
            for item in plan:
                if item[0] == "squares":
                    squares(*item[1:])
                elif item[0] == "exponential":
                    exponential(*item[1:])
                elif item[0] == "out_squares":
                    out_squares(item[1])
                elif item[0] == "out_root":
                    out_root(item[1])
                elif item[0] == "update":
                    keep_o(*item[1:])
                elif item[0] == "fill" and item[1][0] == "post":
                    take_post(item[1])
                elif item[0] == "fill" and item[1][0] not in by_dve:
                    take(item[1])
            act.wait_ge(og_saved, 16 * H)


def first_merge_loads(g_dram, w_proj_a, w_proj_b, piece_raw, load_raw, piece_loaded, in_loaded):
    KA = WA // P
    wa_v, wb_v = (w.rearrange("l (k p) n -> p (l k) n", p=P) for w in (w_proj_a, w_proj_b))
    loads = [(piece_raw[:, 0, 0:KA], wa_v[:, :, 0:P], piece_loaded[0]),
             (piece_raw[:, 0, KA:], wb_v[:, :, 0:P], piece_loaded[0])]
    return loads + [(load_raw[:, k], g_dram[k], in_loaded[k]) for k in range(4)]


def merge(nc, x, g_dram, og_dram, gates_dram, w_proj_a, w_proj_b, w_out, out, piece_raw, load_raw, piece_loaded,
          in_loaded):
    KA = WA // P
    KS = KA + KD
    BLOCKS = [(0, k) for k in range(KA)] + [(1, k) for k in range(KD)]
    QUARTER = D // 4
    x_v, out_v = (a.rearrange("b (t p) d -> (b t) p d", p=P) for a in (x, out))
    wa_v, wb_v, wo_v = (w.rearrange("l (k p) n -> p (l k) n", p=P) for w in (w_proj_a, w_proj_b, w_out))
    with ExitStack() as ctx:
        sb = lambda name, shape, kind=F32: ctx.enter_context(nc.sbuf_tensor(name, shape, kind))
        sem = lambda n: ctx.enter_context(nc.semaphore(n))
        in_high, in_low = sb("in_high", [P, KS, SEQ], F32R), sb("in_low", [P, KS, SEQ], F32R)
        piece_high, piece_low = sb("piece_high", [P, 2, KS, P], F32R), sb("piece_low", [P, 2, KS, P], F32R)
        wo_raw = load_raw[:].rearrange("p (s a) t -> p s (a t)", s=2).rearrange("p s (k n) -> p s k n", n=QUARTER)
        merged = sb("merged", [P, KD, SEQ])
        gate, part = sb("mgate", [P, 2, 2, 512]), sb("part", [P, 2, 512])
        xin, res = sb("xin", [P, 2, 512]), sb("res", [P, 2, 512])
        NB = 8
        ps = [ctx.enter_context(nc.psum_tensor(f"mp{i}", [P, 512], F32)) for i in range(NB)]
        pairs = [(f, c) for f in range(KD) for c in range(2)]
        outs = [(t, c) for t in range(NQT) for c in range(2)]
        ring = lambda name, n: [sem(f"{name}{i}") for i in range(n)]
        wo_loaded = ring("wo_loaded", 2)
        gate_loaded, x_in, out_saved = ring("m_gate_loaded", 2), ring("x_in", 2), ring("out_saved", 2)
        in_high_ready, in_low_ready, piece_high_ready, piece_low_ready, wo_high_ready, wo_low_ready = (
            sem(n) for n in ("in_high_ready", "in_low_ready", "piece_high_ready", "piece_low_ready", "wo_high_ready",
                             "wo_low_ready"))
        made, taken, mixed, added = sem("m_made"), sem("m_taken"), sem("m_mixed"), sem("m_added")
        block = ctx.enter_context(nc.Block())

        def made_by(piece):
            return 4 * (piece + 1) if piece < KD else 2 * len(pairs) + 2 * (piece - KD + 1)

        @block.sync
        def _(sp):
            def load_piece(f):
                if f >= 2:
                    sp.wait_ge(piece_low_ready, f - 1)
                c = slice(P * f, P * f + P)
                sp.dma_start(piece_raw[:, f % 2, 0:KA], wa_v[:, :, c]).then_inc(piece_loaded[f % 2], 16)
                sp.dma_start(piece_raw[:, f % 2, KA:], wb_v[:, :, c]).then_inc(piece_loaded[f % 2], 16)

            def load_gates(n):
                f, c = pairs[n]
                if n >= 2:
                    sp.wait_ge(mixed, n - 1)
                for j in range(2):
                    sp.dma_start(gate[:, n % 2, j],
                                 gates_dram[KD * j + f, :, 512 * c:512 * c + 512]).then_inc(gate_loaded[n % 2], 16)

            def load_quarter(q):
                sp.dma_start(wo_raw[:, q % 2],
                             wo_v[:, :, QUARTER * q:QUARTER * q + QUARTER]).then_inc(wo_loaded[q % 2], 16)

            def load_x(n):
                t, c = outs[n]
                sp.dma_start(xin[:, n % 2], x_v[t][:, 512 * c:512 * c + 512]).then_inc(x_in[n % 2], 16)

            for b, (j, k) in enumerate(BLOCKS):
                if b < 4:
                    continue
                sp.wait_ge(in_low_ready, b - 3)
                sp.dma_start(load_raw[:, b % 4], (g_dram, og_dram)[j][k]).then_inc(in_loaded[b % 4], 16)
                if b == 4:
                    load_piece(1)
            load_gates(0)
            load_gates(1)
            sp.wait_ge(in_low_ready, KS)
            load_quarter(0)
            load_quarter(1)
            for f in range(1, KD):
                if f + 1 < KD:
                    load_piece(f + 1)
                load_gates(2 * f)
                load_gates(2 * f + 1)
            load_x(0)
            load_x(1)
            for q in (2, 3):
                sp.wait_ge(wo_low_ready, q - 1)
                load_quarter(q)
            for n in range(2, len(outs)):
                sp.wait_ge(added, n - 1)
                load_x(n)

        @block.scalar
        def _(act):
            def high_piece(s):
                if s >= 2:
                    act.wait_ge(made, made_by(s - 2))
                if s < KD:
                    act.wait_ge(piece_loaded[s % 2], 32 * (s // 2 + 1))
                    nc.scalar.activation(piece_high[:, s % 2], piece_raw[:, s % 2], ACT.Copy).then_inc(piece_high_ready, 1)
                else:
                    t = s - KD
                    act.wait_ge(mixed, len(pairs) - (1 if t < NQT // 2 else 0))
                    nc.scalar.activation(piece_high[:, s % 2, 0:KD], merged[:, :, P * t:P * t + P],
                                         ACT.Copy).then_inc(piece_high_ready, 1)

            def high_quarter(q):
                act.wait_ge(wo_loaded[q % 2], 16 * (q // 2 + 1))
                nc.scalar.activation(in_high[:, 0:KD, QUARTER * q:QUARTER * q + QUARTER], wo_raw[:, q % 2],
                                     ACT.Copy).then_inc(wo_high_ready, 1)

            def save(n):
                t, c = outs[n]
                act.wait_ge(added, n + 1)
                act.dma_start(out_v[t, :, 512 * c:512 * c + 512], res[:, n % 2]).then_inc(out_saved[n % 2], 16)

            high_piece(0)
            for b in range(KS):
                act.wait_ge(in_loaded[b % 4], 16 * (b // 4 + 1))
                nc.scalar.activation(in_high[:, b], load_raw[:, b % 4], ACT.Copy).then_inc(in_high_ready, 1)
            for s in range(1, KD + 1):
                high_piece(s)
            act.wait_ge(made, 2 * len(pairs))
            high_quarter(0)
            high_quarter(1)
            high_piece(KD + 1)
            high_quarter(2)
            high_quarter(3)
            for t in range(NQT):
                if t + 2 < NQT:
                    high_piece(KD + t + 2)
                save(2 * t)
                save(2 * t + 1)
            for s in range(2):
                act.wait_ge(out_saved[s], 16 * len(outs) // 2)

        @block.gpsimd
        def _(pool):
            for s in range(1, KD + NQT):
                t = s - KD
                ks, raw = (KS, piece_raw[:, s % 2]) if s < KD else (KD, merged[:, :, P * t:P * t + P])
                pool.wait_ge(piece_high_ready, s + 1)
                nc.gpsimd.tensor_tensor(piece_low[:, s % 2, 0:ks], raw, piece_high[:, s % 2, 0:ks],
                                        ALU.subtract).then_inc(piece_low_ready, 1)

        @block.tensor
        def _(pe):
            weight = lambda s, k: (piece_high[:, s % 2, k], piece_low[:, s % 2, k])
            moving = lambda k, a, b: (in_high[:, k, a:b], in_low[:, k, a:b])
            pe.wait_ge(piece_low_ready, 1)
            for b, (j, k) in enumerate(BLOCKS):
                pe.wait_ge(in_low_ready, b + 1)
                for c in range(2):
                    final = k == (KA, KD)[j] - 1
                    last = product(nc, ps[2 * c + j][:], [weight(0, b)], [moving(b, 512 * c, 512 * c + 512)],
                                   first=(k == 0), final=final)
                    if final:
                        last.then_inc(made, 1)
            for n, (f, c) in enumerate(pairs):
                if f == 0:
                    continue
                pe.wait_ge(piece_low_ready, f + 1)
                for j, blocks in enumerate((range(KA), range(KA, KS))):
                    m = 2 * n + j
                    if m >= NB:
                        pe.wait_ge(taken, m - NB + 1)
                    product(nc, ps[m % NB][:], [weight(f, b) for b in blocks],
                            [moving(b, 512 * c, 512 * c + 512) for b in blocks]).then_inc(made, 1)
            for n, (t, c) in enumerate(outs):
                m = 2 * len(pairs) + n
                if n < NB:
                    pe.wait_ge(taken, m - NB + 1)
                else:
                    pe.wait_ge(added, n - NB + 1)
                pe.wait_ge(piece_low_ready, KD + t + 1)
                for a in range(512 * c, 512 * c + 512, QUARTER if t == 0 else 512):
                    w = QUARTER if t == 0 else 512
                    if t == 0:
                        pe.wait_ge(wo_low_ready, a // QUARTER + 1)
                    last = product(nc, ps[m % NB][:, a - 512 * c:a - 512 * c + w], [weight(KD + t, k) for k in range(KD)],
                                   [moving(k, a, a + w) for k in range(KD)])
                last.then_inc(made, 1)

        @block.vector
        def _(dve):
            dve.wait_ge(piece_high_ready, 1)
            nc.vector.tensor_tensor(piece_low[:, 0], piece_raw[:, 0], piece_high[:, 0],
                                    ALU.subtract).then_inc(piece_low_ready, 1)
            for b in range(KS):
                dve.wait_ge(in_high_ready, b + 1)
                nc.vector.tensor_tensor(in_low[:, b], load_raw[:, b % 4], in_high[:, b],
                                        ALU.subtract).then_inc(in_low_ready, 1)
            for n, (f, c) in enumerate(pairs):
                s = slice(512 * c, 512 * c + 512)
                dve.wait_ge(gate_loaded[n % 2], 32 * (n // 2 + 1))
                dve.wait_ge(made, 4 if f == 0 else 2 * n + 1)
                if n >= 2:
                    dve.wait_ge(mixed, n - 1)
                nc.vector.tensor_tensor(part[:, n % 2], ps[2 * n % NB][:], gate[:, n % 2, 0], ALU.mult).then_inc(taken, 1)
                dve.wait_ge(made, 4 if f == 0 else 2 * n + 2)
                nc.vector.tensor_tensor(merged[:, f, s], ps[(2 * n + 1) % NB][:], gate[:, n % 2, 1],
                                        ALU.mult).then_inc(taken, 1)
                dve.wait_ge(taken, 2 * n + 2)
                nc.vector.tensor_tensor(merged[:, f, s], merged[:, f, s], part[:, n % 2], ALU.add).then_inc(mixed, 1)
            for q in range(4):
                dve.wait_ge(wo_high_ready, q + 1)
                at = (slice(None), slice(0, KD), slice(QUARTER * q, QUARTER * q + QUARTER))
                nc.vector.tensor_tensor(in_low[at], wo_raw[:, q % 2], in_high[at], ALU.subtract).then_inc(wo_low_ready, 1)
            for n, (t, c) in enumerate(outs):
                m = 2 * len(pairs) + n
                dve.wait_ge(x_in[n % 2], 16 * (n // 2 + 1))
                dve.wait_ge(made, m + 1)
                if n >= 2:
                    dve.wait_ge(out_saved[n % 2], 16 * (n // 2))
                nc.vector.tensor_tensor(res[:, n % 2], ps[m % NB][:], xin[:, n % 2], ALU.add).then_inc(added, 1)


def hybrid_layer(nc, x, meta_tokens, rel_bias, norm_w, w_in, q_norm_w, k_norm_w, conv_w, a_log, dt_bias, gdn_norm_w,
                 w_proj_a, w_proj_b, w_out, band_tab, chunk_tab, out):
    dram = lambda name, shape: nc.dram_tensor(name, shape, F32, kind="Internal").ap()
    za_dram, zb_dram = dram("za_dram", (NQT, P, WA)), dram("zb_dram", (NQT, P, D))
    gates_dram, band_dram = dram("gates_dram", (2 * KD, P, SEQ)), dram("band_dram", (H, band_tab.shape[1]))
    g_dram, og_dram = dram("g_dram", (WA // P, P, SEQ)), dram("og_dram", (H, P, SEQ))
    qkv_dram, conv_dram = dram("qkv_dram", (3, NT, P, WA)), dram("conv_dram", (3, H, P, T))
    sb = lambda stack, name, shape: stack.enter_context(nc.sbuf_tensor(name, shape, F32))
    with ExitStack() as whole_layer:
        ident, ones = sb(whole_layer, "ident", [P, P]), sb(whole_layer, "ones", [P, P])
        small = sb(whole_layer, "small", [P, NT, NSM])
        make_constants(nc, ident, ones)
        per_token = [sb(whole_layer, n, [P, NT, H]) for n in ("beta", "nbeta", "gates", "gsum", "to_here", "to_end")]
        whole = sb(whole_layer, "whole", [P, 2, NT, H])
        with ExitStack() as branch_a:
            score = [sb(branch_a, f"score{t}", [P, keys_of(t)]) for t in range(NQT)]
            with ExitStack() as normed:
                parts = lambda name, shape: normed.enter_context(nc.sbuf_tensor(name, shape, F32R))
                h_high, h_low = parts("h_high", [P, KD, TP]), parts("h_low", [P, KD, TP])
                w_raw = sb(normed, "w_raw", [P, 2, KD, LOAD])
                w_high, w_low = parts("w_high", [P, 2, KD, LOAD]), parts("w_low", [P, 2, KD, LOAD])
                w_low_ready = normed.enter_context(nc.semaphore("w_low_ready"))
                w_first = w_in.rearrange("l (k p) n -> p (l k) n", p=P)[:, :, OFF_QI:OFF_QI + LOAD]
                normed_tokens(nc, x, meta_tokens, norm_w, h_high, h_low, ident, w_first, w_raw, w_high, w_low,
                              w_low_ready)
                projections(nc, w_in, conv_w, h_high, h_low, w_raw, w_high, w_low, w_low_ready, ident, small, score,
                            qkv_dram, za_dram, zb_dram, gates_dram, conv_dram)
            qT, kT, band = sb(branch_a, "qT", [P, 4, SEQ]), sb(branch_a, "kT", [P, 4, T]), sb(branch_a, "band", [P, H, 2 * P])
            attention_operands(nc, small, chunk_tab, a_log, dt_bias, per_token, whole, ident, qkv_dram, qT, kT, band,
                               rel_bias, band_tab, band_dram, q_norm_w, k_norm_w)
            attention(nc, ident, score, qT, kT, band, qkv_dram, za_dram, g_dram)
        piece_raw, load_raw = sb(whole_layer, "piece_raw", [P, 2, WA // P + KD, P]), sb(whole_layer, "load_raw", [P, 4, SEQ])
        sems = lambda name, n: [whole_layer.enter_context(nc.semaphore(f"{name}{i}")) for i in range(n)]
        piece_loaded, in_loaded = sems("piece_loaded", 2), sems("in_loaded", 4)
        early_loads = first_merge_loads(g_dram, w_proj_a, w_proj_b, piece_raw, load_raw, piece_loaded, in_loaded)
        delta_heads(nc, conv_dram, gdn_norm_w, ident, ones, chunk_tab, *per_token, whole, zb_dram, og_dram, early_loads)
        merge(nc, x, g_dram, og_dram, gates_dram, w_proj_a, w_proj_b, w_out, out, piece_raw, load_raw, piece_loaded,
              in_loaded)


_INS = ["x", "meta_tokens", "rel_bias", "norm_w", "w_in", "q_norm_w", "k_norm_w", "conv_w", "a_log", "dt_bias",
        "gdn_norm_w", "w_proj_a", "w_proj_b", "w_out"]


def kernel(**inputs):
    import concourse.bacc as bacc
    import numpy as np
    from concourse.bass_utils import run_bass_kernel_spmd

    nc = bacc.Bacc("TRN2", target_bir_lowering=False, num_devices=1)
    arrays = {name: np.ascontiguousarray(inputs[name]) for name in _INS}
    arrays["band_tab"], arrays["chunk_tab"] = band_table(), chunk_table()
    args = {name: nc.dram_tensor(f"in_{name}", a.shape, mybir.dt.from_np(a.dtype), kind="ExternalInput").ap()
            for name, a in arrays.items()}
    out = nc.dram_tensor("layer_out", (1, SEQ, D), F32, kind="ExternalOutput").ap()
    hybrid_layer(nc, **args, out=out)
    r = run_bass_kernel_spmd(nc, [{f"in_{name}": a for name, a in arrays.items()}], core_ids=[0])
    return r.results[0]["layer_out"]
```
